# Optimizing a Trainium2 kernel written in Bass

```python
import jax, jax.numpy as jnp
from jax import lax
import numpy as np

D_MODEL = 1024
BATCH = 1
SEQ = 512
DEPTH = 1

D_MIX = D_MODEL
HEAD_DIM = 64
ATTN_WIDTH = D_MIX // 2
CONV_WIDTH = D_MIX - ATTN_WIDTH
N_HEADS = ATTN_WIDTH // HEAD_DIM
N_KV_HEADS = 2
GQA_GROUP = N_HEADS // N_KV_HEADS
KV_WIDTH = N_KV_HEADS * HEAD_DIM
N_CONV_GROUPS = CONV_WIDTH // HEAD_DIM
WINDOW = 128
CONV_K = 3
IN_WIDTH = ATTN_WIDTH + 2 * KV_WIDTH + 3 * CONV_WIDTH
N_KEYS = 128
N_EXPERTS = N_KEYS * N_KEYS
PEER_HEADS = 8
PEER_TOPK = 16
D_KEY = 256
D_HALF = D_KEY // 2
PEER_CHUNK = 128
EPS = 1e-6
NEG = -1e30


def rms_norm(x, g):
    x32 = x.astype(jnp.float32)
    y = x32 * lax.rsqrt(jnp.mean(x32 * x32, axis=-1, keepdims=True) + EPS)
    return (y * g.astype(jnp.float32)).astype(x.dtype)

def head_rms_norm(x, g, n_groups):
    shp = x.shape
    xh = x.reshape(shp[:-1] + (n_groups, HEAD_DIM))
    y = rms_norm(xh, g.reshape(n_groups, HEAD_DIM))
    return y.reshape(shp)

def modulate(h, shift, scale):
    return h * (1 + scale[:, None, :]) + shift[:, None, :]

def sliding_window_sink_attention(q, k, v, sinks):
    bsz, s_len = q.shape[0], q.shape[1]
    nb = s_len // WINDOW
    qb = q.reshape(bsz, nb, WINDOW, N_KV_HEADS, GQA_GROUP, HEAD_DIM)
    kb = k.reshape(bsz, nb, WINDOW, N_KV_HEADS, HEAD_DIM)
    vb = v.reshape(bsz, nb, WINDOW, N_KV_HEADS, HEAD_DIM)

    def with_prev(t):
        prev = jnp.pad(t[:, :-1], ((0, 0), (1, 0), (0, 0), (0, 0), (0, 0)))
        return jnp.concatenate([prev, t], axis=2)

    kk, vv = with_prev(kb), with_prev(vb)
    s = jnp.einsum('bnqkgd,bnjkd->bnkgqj', qb, kk).astype(jnp.float32) * (HEAD_DIM ** -0.5)
    qi = jnp.arange(WINDOW)[:, None]
    kj = jnp.arange(2 * WINDOW)[None, :]
    diff = qi + WINDOW - kj
    rel_ok = (diff >= 0) & (diff < WINDOW)
    blk = jnp.arange(nb)[:, None, None]
    valid = rel_ok[None] & ((blk > 0) | (kj[None] >= WINDOW))
    s = jnp.where(valid[None, :, None, None], s, NEG)
    sink = sinks.astype(jnp.float32).reshape(N_KV_HEADS, GQA_GROUP)[None, None, :, :, None, None]
    m = jnp.maximum(jnp.max(s, axis=-1, keepdims=True), sink)
    e = jnp.exp(s - m)
    p = e / (jnp.sum(e, axis=-1, keepdims=True) + jnp.exp(sink - m))
    o = jnp.einsum('bnkgqj,bnjkd->bnqkgd', p.astype(v.dtype), vv)
    return o.reshape(bsz, s_len, ATTN_WIDTH)

def short_gated_conv(b_gate, c_gate, u, conv_w):
    z = c_gate * u
    zp = jnp.pad(z, ((0, 0), (CONV_K - 1, 0), (0, 0)))
    s_len = z.shape[1]
    conv = zp[:, 0:s_len] * conv_w[0] + zp[:, 1:s_len + 1] * conv_w[1] + zp[:, 2:s_len + 2] * conv_w[2]
    return b_gate * conv

def peer_layer(h, w_query, peer_keys1, peer_keys2, peer_u, peer_v):
    bsz, s_len, d = h.shape
    t = bsz * s_len
    hf = h.reshape(t, d)
    q = (hf @ w_query).reshape(t, PEER_HEADS, D_KEY)
    s1 = jnp.einsum('thd,hnd->thn', q[..., :D_HALF], peer_keys1).astype(jnp.float32)
    s2 = jnp.einsum('thd,hnd->thn', q[..., D_HALF:], peer_keys2).astype(jnp.float32)
    v1, i1 = lax.top_k(s1, PEER_TOPK)
    v2, i2 = lax.top_k(s2, PEER_TOPK)
    cand = (v1[..., :, None] + v2[..., None, :]).reshape(t, PEER_HEADS, PEER_TOPK * PEER_TOPK)
    sc, ci = lax.top_k(cand, PEER_TOPK)
    e1 = jnp.take_along_axis(i1, ci // PEER_TOPK, axis=-1)
    e2 = jnp.take_along_axis(i2, ci % PEER_TOPK, axis=-1)
    idx = e1 * N_KEYS + e2
    gates = jax.nn.softmax(sc, axis=-1).astype(h.dtype)

    nchunk = t // PEER_CHUNK
    hc = hf.reshape(nchunk, PEER_CHUNK, d)
    ic = idx.reshape(nchunk, PEER_CHUNK, PEER_HEADS, PEER_TOPK)
    gc = gates.reshape(nchunk, PEER_CHUNK, PEER_HEADS, PEER_TOPK)

    def chunk_fn(args):
        hx, ix, gx = args
        u = peer_u[ix]
        a = jax.nn.gelu(jnp.einsum('td,thkd->thk', hx, u), approximate=False)
        vsel = peer_v[ix]
        return jnp.einsum('thk,thkd->td', gx * a, vsel)

    out = lax.map(chunk_fn, (hc, ic, gc))
    return out.reshape(bsz, s_len, d)

def first_inputs(seed: int = 0) -> dict:
    key = jax.random.key(seed)
    ks = jax.random.split(key, 20)
    D = D_MODEL
    f32 = jnp.float32
    return {
        "x": jax.random.normal(ks[0], (BATCH, SEQ, D), f32),
        "c": jax.random.normal(ks[1], (BATCH, D), f32),
        "w_ada": jax.random.normal(ks[2], (D, 6 * D), f32) * D ** -0.5,
        "b_ada": jax.random.normal(ks[3], (6 * D,), f32) * 0.02,
        "norm1_g": 1.0 + 0.02 * jax.random.normal(ks[4], (D,), f32),
        "w_in": jax.random.normal(ks[5], (D, IN_WIDTH), f32) * D ** -0.5,
        "b_in": jax.random.normal(ks[6], (IN_WIDTH,), f32) * 0.02,
        "attn_sinks": jax.random.normal(ks[7], (N_HEADS,), f32) * 0.5,
        "conv_w": jax.random.normal(ks[8], (CONV_K, CONV_WIDTH), f32) * CONV_K ** -0.5,
        "attn_out_g": 1.0 + 0.02 * jax.random.normal(ks[9], (ATTN_WIDTH,), f32),
        "conv_out_g": 1.0 + 0.02 * jax.random.normal(ks[10], (CONV_WIDTH,), f32),
        "w_out": jax.random.normal(ks[11], (D_MIX, D), f32) * D_MIX ** -0.5,
        "b_out": jax.random.normal(ks[12], (D,), f32) * 0.02,
        "norm2_g": 1.0 + 0.02 * jax.random.normal(ks[13], (D,), f32),
        "w_query": jax.random.normal(ks[14], (D, PEER_HEADS * D_KEY), f32) * D ** -0.5,
        "peer_keys1": jax.random.normal(ks[15], (PEER_HEADS, N_KEYS, D_HALF), f32) * D_HALF ** -0.5,
        "peer_keys2": jax.random.normal(ks[16], (PEER_HEADS, N_KEYS, D_HALF), f32) * D_HALF ** -0.5,
        "peer_u": jax.random.normal(ks[17], (N_EXPERTS, D), f32) * D ** -0.5,
        "peer_v": jax.random.normal(ks[18], (N_EXPERTS, D), f32) * PEER_HEADS ** -0.5,
        "final_g": 1.0 + 0.02 * jax.random.normal(ks[19], (D,), f32),
    }

def first_block(x, c, w_ada, b_ada, norm1_g, w_in, b_in, attn_sinks, conv_w, attn_out_g,
              conv_out_g, w_out, b_out, norm2_g, w_query, peer_keys1, peer_keys2,
              peer_u, peer_v, final_g):
    bsz, s_len, _ = x.shape
    for _layer in range(DEPTH):
        ada = jax.nn.silu(c) @ w_ada + b_ada
        shift1, scale1, gate1, shift2, scale2, gate2 = jnp.split(ada, 6, axis=-1)

        h = modulate(rms_norm(x, norm1_g), shift1, scale1)
        proj = h @ w_in + b_in
        o1 = ATTN_WIDTH
        o2 = o1 + KV_WIDTH
        o3 = o2 + KV_WIDTH
        o4 = o3 + CONV_WIDTH
        o5 = o4 + CONV_WIDTH
        q = proj[..., :o1].reshape(bsz, s_len, N_HEADS, HEAD_DIM)
        k = proj[..., o1:o2].reshape(bsz, s_len, N_KV_HEADS, HEAD_DIM)
        v = proj[..., o2:o3].reshape(bsz, s_len, N_KV_HEADS, HEAD_DIM)
        b_gate = proj[..., o3:o4]
        c_gate = proj[..., o4:o5]
        u_conv = proj[..., o5:]
        attn = head_rms_norm(sliding_window_sink_attention(q, k, v, attn_sinks), attn_out_g, N_HEADS)
        conv = head_rms_norm(short_gated_conv(b_gate, c_gate, u_conv, conv_w), conv_out_g, N_CONV_GROUPS)
        mix = jnp.concatenate([attn, conv], axis=-1) @ w_out + b_out
        x = x + gate1[:, None, :] * mix

        h2 = modulate(rms_norm(x, norm2_g), shift2, scale2)
        x = x + gate2[:, None, :] * peer_layer(h2, w_query, peer_keys1, peer_keys2, peer_u, peer_v)
    return rms_norm(x, final_g)


DEPTH_2 = 2

N_MIXERS = 2
MLA_HEADS = 8
MLA_Q_LORA = 256
MLA_KV_LORA = 256
MLA_NOPE = 128
MLA_ROPE = 64
MLA_V = 128
ROPE_THETA = 10000.0
Q_BLOCK = 128
HGRN_HEADS = 8
HGRN_DK = D_MODEL // HGRN_HEADS
HGRN_DV = D_MODEL // HGRN_HEADS
HGRN_CHUNK = 64
D_FF = ((8 * D_MODEL // 3 + 255) // 256) * 256
D_PLE = 256
LN_EPS = 1e-5
RMS_EPS = 1e-6
DEEPNORM_ALPHA = (2 * DEPTH_2) ** 0.25
DEEPNORM_BETA = (8 * DEPTH_2) ** -0.25
N_MLA_LAYERS = (DEPTH_2 + N_MIXERS - 1) // N_MIXERS
N_HGRN_LAYERS = DEPTH_2 // N_MIXERS


def layer_norm(x, g, b):
    xf = x.astype(jnp.float32)
    mu = jnp.mean(xf, axis=-1, keepdims=True)
    var = jnp.mean(jnp.square(xf - mu), axis=-1, keepdims=True)
    y = (xf - mu) * lax.rsqrt(var + LN_EPS) * g.astype(jnp.float32) + b.astype(jnp.float32)
    return y.astype(x.dtype)

def rms_norm_2(x, g):
    xf = x.astype(jnp.float32)
    y = xf * lax.rsqrt(jnp.mean(jnp.square(xf), axis=-1, keepdims=True) + RMS_EPS) * g.astype(jnp.float32)
    return y.astype(x.dtype)

def rope_tables(positions):
    inv_freq = ROPE_THETA ** (-jnp.arange(0, MLA_ROPE, 2, dtype=jnp.float32) / MLA_ROPE)
    ang = positions.astype(jnp.float32)[..., None] * inv_freq
    return jnp.cos(ang), jnp.sin(ang)

def apply_rope(t, cos, sin):
    half = t.shape[-1] // 2
    t1, t2 = t[..., :half], t[..., half:]
    out = jnp.concatenate([t1 * cos - t2 * sin, t2 * cos + t1 * sin], axis=-1)
    return out.astype(t.dtype)

def mla_mixer(x, cos, sin, w_dqkv, q_norm, kv_norm, w_uq, w_ukv, w_o):
    B, S, _ = x.shape
    H = MLA_HEADS
    down = x @ w_dqkv
    c_q = rms_norm_2(down[..., :MLA_Q_LORA], q_norm)
    c_kv = rms_norm_2(down[..., MLA_Q_LORA:MLA_Q_LORA + MLA_KV_LORA], kv_norm)
    k_rope = apply_rope(down[..., MLA_Q_LORA + MLA_KV_LORA:], cos, sin)
    q = (c_q @ w_uq).reshape(B, S, H, MLA_NOPE + MLA_ROPE)
    q_nope = q[..., :MLA_NOPE]
    q_rope = apply_rope(q[..., MLA_NOPE:], cos[:, :, None, :], sin[:, :, None, :])
    kv = (c_kv @ w_ukv).reshape(B, S, H, MLA_NOPE + MLA_V)
    k_nope, v = kv[..., :MLA_NOPE], kv[..., MLA_NOPE:]

    nblk = S // Q_BLOCK
    scale = (MLA_NOPE + MLA_ROPE) ** -0.5
    kpos = jnp.arange(S, dtype=jnp.int32)
    qpos = kpos.reshape(nblk, Q_BLOCK)

    def to_blocks(t):
        return jnp.moveaxis(t.reshape((B, nblk, Q_BLOCK) + t.shape[2:]), 1, 0)

    def attend(blk):
        qn, qr, qp = blk
        s = (jnp.einsum('bqhd,bkhd->bhqk', qn, k_nope)
             + jnp.einsum('bqhr,bkr->bhqk', qr, k_rope)).astype(jnp.float32) * scale
        s = jnp.where(kpos[None, None, None, :] <= qp[None, None, :, None], s, -jnp.inf)
        w = jax.nn.softmax(s, axis=-1).astype(v.dtype)
        return jnp.einsum('bhqk,bkhd->bqhd', w, v)

    o = lax.map(attend, (to_blocks(q_nope), to_blocks(q_rope), qpos))
    o = jnp.moveaxis(o, 0, 1).reshape(B, S, H * MLA_V)
    return o @ w_o

def hgrn2_mixer(x, lb, w_in, out_norm, w_o):
    B, S, _ = x.shape
    H, DK, DV, C = HGRN_HEADS, HGRN_DK, HGRN_DV, HGRN_CHUNK
    proj = x @ w_in
    q = jax.nn.silu(proj[..., :H * DK].astype(jnp.float32)).reshape(B, S, H, DK)
    f = proj[..., H * DK:2 * H * DK].astype(jnp.float32).reshape(B, S, H, DK)
    v = proj[..., 2 * H * DK:2 * H * DK + H * DV].astype(jnp.float32).reshape(B, S, H, DV)
    gate = proj[..., 2 * H * DK + H * DV:]
    lb = lb.reshape(H, DK)
    log_f = jnp.logaddexp(jnp.log(lb), jnp.log1p(-lb) + jax.nn.log_sigmoid(f))
    k = (1.0 - lb) * jax.nn.sigmoid(-f)

    n = S // C

    def to_chunks(t):
        return t.reshape(B, n, C, H, t.shape[-1]).transpose(1, 0, 3, 2, 4)

    causal = jnp.tril(jnp.ones((C, C), dtype=bool))

    def step(state, chunk):
        qc, kc, gc, vc = chunk
        G = jnp.cumsum(gc, axis=2)
        inter = jnp.einsum('bhtd,bhde->bhte', qc * jnp.exp(G), state)
        diff = G[:, :, :, None, :] - G[:, :, None, :, :]
        decay = jnp.exp(jnp.where(causal[:, :, None], diff, -jnp.inf))
        A = jnp.einsum('bhtd,bhsd,bhtsd->bhts', qc, kc, decay)
        intra = jnp.einsum('bhts,bhse->bhte', A, vc)
        G_last = G[:, :, -1:, :]
        new_state = (jnp.exp(G_last[:, :, 0, :])[..., None] * state
                     + jnp.einsum('bhsd,bhse->bhde', kc * jnp.exp(G_last - G), vc))
        return new_state, inter + intra

    s0 = jnp.zeros((B, H, DK, DV), jnp.float32)
    _, o = lax.scan(step, s0, (to_chunks(q), to_chunks(k), to_chunks(log_f), to_chunks(v)))
    o = o.transpose(1, 0, 3, 2, 4).reshape(B, S, H, DV)
    o = rms_norm_2(o, out_norm.reshape(H, DV))
    o = o * jax.nn.silu(gate.astype(jnp.float32)).reshape(B, S, H, DV)
    return o.reshape(B, S, H * DV).astype(x.dtype) @ w_o

def swiglu_ffn(x, w_in, w_down):
    h = x @ w_in
    g, u = h[..., :D_FF], h[..., D_FF:]
    return (jax.nn.silu(g) * u) @ w_down

def second_inputs(seed: int = 0) -> dict:
    key = jax.random.key(seed)
    ks = jax.random.split(key, 24)

    def w(k, shape, fan_in, scale=1.0):
        return jax.random.normal(k, shape, jnp.float32) * (fan_in ** -0.5) * scale

    def gain(k, shape):
        return 1.0 + 0.05 * jax.random.normal(k, shape, jnp.float32)

    def bias(k, shape):
        return 0.02 * jax.random.normal(k, shape, jnp.float32)

    NM, NH = N_MLA_LAYERS, N_HGRN_LAYERS
    return {
        'x': jax.random.normal(ks[0], (BATCH, SEQ, D_MODEL), jnp.float32),
        'p': jax.random.normal(ks[1], (DEPTH_2, BATCH, SEQ, D_PLE), jnp.float32),
        'positions': jnp.tile(jnp.arange(SEQ, dtype=jnp.int32)[None, :], (BATCH, 1)),
        'mla_w_dqkv': w(ks[2], (NM, D_MODEL, MLA_Q_LORA + MLA_KV_LORA + MLA_ROPE), D_MODEL),
        'mla_q_norm': gain(ks[3], (NM, MLA_Q_LORA)),
        'mla_kv_norm': gain(ks[4], (NM, MLA_KV_LORA)),
        'mla_w_uq': w(ks[5], (NM, MLA_Q_LORA, MLA_HEADS * (MLA_NOPE + MLA_ROPE)), MLA_Q_LORA),
        'mla_w_ukv': w(ks[6], (NM, MLA_KV_LORA, MLA_HEADS * (MLA_NOPE + MLA_V)), MLA_KV_LORA),
        'mla_w_o': w(ks[7], (NM, MLA_HEADS * MLA_V, D_MODEL), MLA_HEADS * MLA_V, DEEPNORM_BETA),
        'hgrn_w_in': w(ks[8], (NH, D_MODEL, 2 * HGRN_HEADS * HGRN_DK + 2 * HGRN_HEADS * HGRN_DV), D_MODEL),
        'hgrn_lb_logits': 0.1 * jax.random.normal(ks[9], (DEPTH_2, HGRN_HEADS * HGRN_DK), jnp.float32),
        'hgrn_out_norm': gain(ks[10], (NH, HGRN_HEADS * HGRN_DV)),
        'hgrn_w_o': w(ks[11], (NH, HGRN_HEADS * HGRN_DV, D_MODEL), HGRN_HEADS * HGRN_DV, DEEPNORM_BETA),
        'ffn_w_in': w(ks[12], (DEPTH_2, D_MODEL, 2 * D_FF), D_MODEL),
        'ffn_w_down': w(ks[13], (DEPTH_2, D_FF, D_MODEL), D_FF, DEEPNORM_BETA),
        'ln_mix_g': gain(ks[14], (DEPTH_2, D_MODEL)),
        'ln_mix_b': bias(ks[15], (DEPTH_2, D_MODEL)),
        'ln_ffn_g': gain(ks[16], (DEPTH_2, D_MODEL)),
        'ln_ffn_b': bias(ks[17], (DEPTH_2, D_MODEL)),
        'ple_w_proj': w(ks[18], (DEPTH_2, D_PLE, D_MODEL), D_PLE),
        'ple_w_gate': w(ks[19], (DEPTH_2, D_MODEL, D_MODEL), D_MODEL),
    }

def second_block(x, p, positions, mla_w_dqkv, mla_q_norm, mla_kv_norm, mla_w_uq, mla_w_ukv, mla_w_o,
              hgrn_w_in, hgrn_lb_logits, hgrn_out_norm, hgrn_w_o, ffn_w_in, ffn_w_down,
              ln_mix_g, ln_mix_b, ln_ffn_g, ln_ffn_b, ple_w_proj, ple_w_gate):
    cos, sin = rope_tables(positions)
    lb_soft = jax.nn.softmax(hgrn_lb_logits.astype(jnp.float32), axis=0)
    lower_bounds = jnp.cumsum(lb_soft, axis=0) - lb_soft[0:1]

    for i in range(DEPTH_2):
        j = i // N_MIXERS
        if i % N_MIXERS == 0:
            h = mla_mixer(x, cos, sin, mla_w_dqkv[j], mla_q_norm[j], mla_kv_norm[j],
                          mla_w_uq[j], mla_w_ukv[j], mla_w_o[j])
        else:
            h = hgrn2_mixer(x, lower_bounds[i], hgrn_w_in[j], hgrn_out_norm[j], hgrn_w_o[j])
        x = layer_norm(DEEPNORM_ALPHA * x + h, ln_mix_g[i], ln_mix_b[i])
        x = layer_norm(DEEPNORM_ALPHA * x + swiglu_ffn(x, ffn_w_in[i], ffn_w_down[i]), ln_ffn_g[i], ln_ffn_b[i])
        x = x + jax.nn.sigmoid(x @ ple_w_gate[i]) * (p[i] @ ple_w_proj[i])
    return x


def setup_inputs(seed=0):
    out = dict(first_inputs(seed))
    for name, value in second_inputs(seed + 1).items():
        if name != "x":
            out[name + "_2"] = value
    return out


def reference(
    x, c, w_ada, b_ada, norm1_g, w_in, b_in, attn_sinks, conv_w, attn_out_g, conv_out_g, w_out,
    b_out, norm2_g, w_query, peer_keys1, peer_keys2, peer_u, peer_v, final_g, p_2, positions_2,
    mla_w_dqkv_2, mla_q_norm_2, mla_kv_norm_2, mla_w_uq_2, mla_w_ukv_2, mla_w_o_2, hgrn_w_in_2,
    hgrn_lb_logits_2, hgrn_out_norm_2, hgrn_w_o_2, ffn_w_in_2, ffn_w_down_2, ln_mix_g_2,
    ln_mix_b_2, ln_ffn_g_2, ln_ffn_b_2, ple_w_proj_2, ple_w_gate_2,
):
    x = first_block(
        x, c, w_ada, b_ada, norm1_g, w_in, b_in, attn_sinks, conv_w, attn_out_g, conv_out_g,
        w_out, b_out, norm2_g, w_query, peer_keys1, peer_keys2, peer_u, peer_v, final_g,
    )
    return second_block(
        x, p_2, positions_2, mla_w_dqkv_2, mla_q_norm_2, mla_kv_norm_2, mla_w_uq_2, mla_w_ukv_2,
        mla_w_o_2, hgrn_w_in_2, hgrn_lb_logits_2, hgrn_out_norm_2, hgrn_w_o_2, ffn_w_in_2,
        ffn_w_down_2, ln_mix_g_2, ln_mix_b_2, ln_ffn_g_2, ln_ffn_b_2, ple_w_proj_2,
        ple_w_gate_2,
    )


_drawn_inputs = setup_inputs


def setup_inputs(seed=0):
    import zlib

    import numpy as np

    out = dict(_drawn_inputs(seed))
    spreads = {}
    factors = {'norm1_g': 3.454,
     'b_in': 3.007,
     'attn_sinks': 8.0,
     'attn_out_g': 5.021,
     'conv_out_g': 5.349,
     'b_out': 4.044,
     'norm2_g': 4.016,
     'final_g': 3.237,
     'mla_q_norm_2': 8.0,
     'mla_kv_norm_2': 8.0,
     'hgrn_lb_logits_2': 8.0,
     'hgrn_out_norm_2': 5.839}
    for name, (base, spread) in spreads.items():
        noise = np.random.default_rng([zlib.crc32(name.encode()), seed]).standard_normal(out[name].shape)
        drawn = base * np.exp(spread * noise) if base else spread * noise
        out[name] = __import__('jax').numpy.asarray(drawn.astype(out[name].dtype))
    for name, factor in factors.items():
        out[name] = (out[name] * factor).astype(out[name].dtype)
    return out
```

```python
import numpy as np
import concourse.bass as bass
from concourse import mybir
from contextlib import ExitStack

F32 = mybir.dt.float32
U32 = mybir.dt.uint32
I32 = mybir.dt.int32
ALU = mybir.AluOpType
ACT = mybir.ActivationFunctionType
AX = mybir.AxisListType.X

P = 128
T = 512
D = 1024
KC = D // P
TB = T // P
RING = 4
BLOCKS = 8

HEADS = 8
HD = 64
NKEY = 128
TOPK = 16
GROUP = 16
GROUPS = NKEY // GROUP
FF = 22
ALPHA = (2 * 2) ** 0.25
NEG = -1e30
LOWEST = -3e38
CH = 64
NCH = T // CH
LEVELS = 6

PARTS = [("shift1", 8), ("scale1", 8), ("w_in", 18), ("w_v", 1), ("ada_rest", 24), ("w_out", 8), ("gate2", 8), ("w_query", 16),
         ("keys", 2), ("u_first", GROUP)]
for _g in range(GROUPS):
    _u = GROUP // 2 if _g < GROUPS - 1 else 0
    PARTS += [(f"v{_g}a", 8), (f"u{_g + 1}a", _u), (f"v{_g}b", 8), (f"u{_g + 1}b", _u)]
PARTS += [("dqkv", 6), ("uq", 4), ("uk", 2), ("uv", 2), ("w_o", 8)]
for _i in range(2):
    if _i:
        PARTS += [("hgrn_in", 16), ("hgrn_v", 8), ("hgrn_gate", 8), ("hgrn_o", 8)]
    PARTS += [(f"ffn_in{_i}", 2 * FF), (f"ffn_down{_i}", 24), (f"ple_gate{_i}", 8), (f"ple_proj{_i}", 2)]
FIRST = {}
NTILES = 0
for _name, _n in PARTS:
    FIRST[_name] = NTILES
    NTILES += _n

PRODUCTS = [("w_in", 19), ("w_out", 8), ("w_query", 16), ("keys", 16), ("u_first", GROUP)]
PRODUCTS += [(f"u{g}", GROUP) for g in range(1, GROUPS)]
PRODUCTS += [("dqkv", 6), ("uq", 16), ("uk", 8), ("uv", 8), ("w_o", 8), ("ffn_in0", 2 * FF), ("ffn_down0", 8),
             ("ple_gate0", 8), ("ple_proj0", 8), ("hgrn_in", 32), ("hgrn_o", 8), ("ffn_in1", 2 * FF),
             ("ffn_down1", 8), ("ple_gate1", 8), ("ple_proj1", 8)]
PROD = {}
_p = 0
for _name, _n in PRODUCTS:
    PROD[_name] = _p
    _p += _n

NORMS = [("norm1", 1, KC), ("attn", 4, 1), ("conv", 4, 1), ("norm2", 1, KC), ("final", 1, KC), ("cq", 1, 2),
         ("ckv", 1, 2), ("mix0", 1, KC), ("ffn0", 1, KC), ("hgrn", 8, 1), ("mix1", 1, KC), ("ffn1", 1, KC)]
NGROUP, NSQ = {}, {}
_g0 = _s0 = 0
for _name, _n, _k in NORMS:
    NGROUP[_name], NSQ[_name] = _g0, _s0
    _g0 += _n
    _s0 += _n * _k
NORM_SHAPE = {name: (n, k) for name, n, k in NORMS}

COLS = [("c", 8), ("b_ada", 48), ("norm1_g", 8), ("b_in", 18), ("b_v", 128), ("sinks", 8), ("conv_w", 12),
        ("attn_out_g", 4), ("conv_out_g", 4), ("b_out", 8), ("norm2_g", 8), ("final_g", 8), ("q_norm", 2),
        ("kv_norm", 2), ("lb", 16), ("out_norm", 8), ("ln_mix_g", 16), ("ln_mix_b", 16), ("ln_ffn_g", 16),
        ("ln_ffn_b", 16), ("inv_freq", 1), ("sin_sign", 1)]
COL = {}
_c = 0
for _name, _n in COLS:
    COL[_name] = _c
    _c += _n
NCOLS = _c
ROUND = 1.5 * 2.0 ** 23
TWO_PI = (6.28125, 0.0019350051879882812, 2.0 * np.pi - 6.28125 - 0.0019350051879882812)


def build(nc, stream, x_in, params, positions, ple_in, out, gate_map):
    with ExitStack() as ctx:
        def sb(name, shape, dt=F32):
            return ctx.enter_context(nc.sbuf_tensor(name, shape, dt))

        def sem(name):
            return ctx.enter_context(nc.semaphore(name))

        ps = ctx.enter_context(nc.psum_tensor("ps", [P, 8, T], F32))

        ring = [sb(f"ring{i}", [P, BLOCKS, P]) for i in range(RING)]
        X = sb("X", [P, KC, T])
        H = sb("H", [P, KC, T])
        ACC = sb("ACC", [P, KC, T])
        A = sb("A", [P, 64, T])
        par = sb("par", [P, NCOLS])
        pos = sb("pos", [P, T], I32)
        ada = sb("ada", [P, 48])
        cs = sb("cs", [P, 8])
        ones = sb("ones", [P, P])
        halves = sb("halves", [P, P])
        ident = sb("ident", [P, P])
        iota = sb("iota", [P, P])
        win_mask = sb("win_mask", [P, 2 * P])
        diag_mask = sb("diag_mask", [P, P])
        level_mask = sb("level_mask", [P, LEVELS, P])
        scan_keep = sb("scan_keep", [P, T])
        small = sb("small", [P, 96])
        eps = sb("eps", [P, 2])
        dec = sb("dec", [P, HEADS, NCH])

        weights_loaded = [sem(f"weights_loaded{i}") for i in range(RING)]
        inputs_loaded = sem("inputs_loaded")
        pos_loaded = sem("pos_loaded")
        tiles_started = sem("tiles_started")
        product_ready = sem("product_ready")
        bank_free = sem("bank_free")
        consts_ready = sem("consts_ready")
        pool_step = sem("pool_step")
        dve_step = sem("dve_step")
        c_ready = sem("c_ready")
        lb_in = sem("lb_in")
        lb_exp = sem("lb_exp")
        ada_sums = sem("ada_sums")
        ada_ready = sem("ada_ready")
        sq_ready = sem("sq_ready")
        sq_used = sem("sq_used")
        root_ready = sem("root_ready")
        rstd_ready = sem("rstd_ready")
        scaled_ready = sem("scaled_ready")
        h_ready = sem("h_ready")
        residual_ready = sem("residual_ready")
        mean_ready = sem("mean_ready")
        centered_ready = sem("centered_ready")
        bias_ready = sem("bias_ready")
        scores_ready = sem("scores_ready")
        shift_ready = sem("shift_ready")
        exp_ready = sem("exp_ready")
        sink_ready = sem("sink_ready")
        probs_ready = sem("probs_ready")
        pt_ready = sem("pt_ready")
        pt_taken = sem("pt_taken")
        o_ready = sem("o_ready")
        o_taken = sem("o_taken")
        conv_ready = sem("conv_ready")
        gate_in = sem("gate_in")
        gate_exp = sem("gate_exp")
        route_ready = sem("route_ready")
        route_turned = sem("route_turned")
        route_taken = sem("route_taken")
        onehot_ready = sem("onehot_ready")
        onehot_free = sem("onehot_free")
        gate_bank_free = sem("gate_bank_free")
        gate_stored = sem("gate_stored")
        gates_loaded = [sem(f"gates_loaded{i}") for i in range(8)]
        mixed_ready = sem("mixed_ready")
        sums_ready = sem("sums_ready")
        sum_bank_free = sem("sum_bank_free")
        rope_in = sem("rope_in")
        rope_out = sem("rope_out")
        rope_ready = sem("rope_ready")
        ff_ready = sem("ff_ready")
        p_loaded = sem("p_loaded")
        forget_in = sem("forget_in")
        log_ready = sem("log_ready")
        cum_ready = sem("cum_ready")
        decay_in = sem("decay_in")
        decay_ready = sem("decay_ready")
        khat_ready = sem("khat_ready")
        kt_ready = sem("kt_ready")
        kt_taken = sem("kt_taken")
        gap_ready = sem("gap_ready")
        gap_exp = sem("gap_exp")
        level_ready = sem("level_ready")
        pair_ready = sem("pair_ready")
        masked_ready = sem("masked_ready")
        intra_ready = sem("intra_ready")
        intra_taken = sem("intra_taken")
        inter_ready = sem("inter_ready")
        delta_ready = sem("delta_ready")
        inter_added = sem("inter_added")
        state_ready = sem("state_ready")
        gated_ready = sem("gated_ready")
        stored = sem("stored")
        block = ctx.enter_context(nc.Block())

        def col(name, j=0, n=1):
            return par[:, COL[name] + j:COL[name] + j + n]

        def plane(i):
            return A[:, i, :]

        class Steps:
            def __init__(self, eng, s):
                self.eng, self.sem, self.n = eng, s, 0

            def do(self, ins):
                ins.then_inc(self.sem, 1)
                self.n += 1
                return self.n

            def wait(self, n=None):
                self.eng.wait_ge(self.sem, self.n if n is None else n)

        SHIFT1, SCALE1, GATE1, SHIFT2, SCALE2, GATE2 = range(0, 48, 8)

        def ada_col(part, j=0, n=1):
            return ada[:, part + j:part + j + n]

        GS1, LB, OMLB, GSTMP = 0, 8, 16, 24
        PQ, PKD, PB_, PCG, PU, PV = 0, 4, 6, 10, 14, 18
        ATT, Z, MIX = 19, 23, 28
        PROBS, PT = (36, 38), (40, 42)
        zv = A[:, Z:Z + 5, :].rearrange("p a t -> p (a t)")[:, 0:4 * (T + 2)].rearrange("p (c t) -> p c t", c=4)
        STAGE = 16
        SCORES = 48
        GRING = 32
        accf = ACC[:].rearrange("p a t -> p (a t)")
        staging = A[:, STAGE:STAGE + 32, :].rearrange("p a t -> p (a t)").rearrange("p (i t) -> p i t", i=NKEY)
        turned = accf[:, 2048:2048 + 3 * P].rearrange("p (a t) -> p a t", a=3)
        hot1 = accf[:, 2560:3072].rearrange("p (s i) -> p s i", s=4)
        hot2 = accf[:, 3072:3584].rearrange("p (s i) -> p s i", s=4)
        routed = accf[:, 1664:2048].rearrange("p (a t) -> p a t", a=3)
        CQN, CKN, COS, SIN, QN, QR, QS, KN, VM, OM = 6, 8, 10, 11, 14, 22, 26, 30, 38, 46
        MPROBS, MPT = (54, 56), (58, 60)
        HF, SG, UU, TMP = 0, 22, 24, 30
        HQ, HLF, HK, HG, HGT, HV, HO, HM, HE = 0, 8, 16, 24, 32, 40, 48, 56, 58
        STATE = A[:, 62:64, :].rearrange("p a t -> p (a t)").rearrange("p (h e) -> p h e", h=HEADS)

        NORM = {}
        NORM.update(norm1=(60, 52), attn=(60, 52), conv=(60, 56), norm2=(60, 52), final=(60, 52),
                    cq=(54, 58), ckv=(54, 59), mix0=(54, 58), ffn0=(54, 58), hgrn=(8, 0), mix1=(54, 58),
                    ffn1=(54, 58))
        AFTER = {"mix0": "mla", "ffn0": "ffn0", "mix1": "hgrn", "ffn1": "ffn1"}
        eps_col = {1e-6: eps[:, 0:1], 1e-5: eps[:, 1:2]}

        def sm(unit, c, n=1):
            return small[:, 64 + 16 * (unit % 2) + c:64 + 16 * (unit % 2) + c + n]

        LN = {"mix0": 0, "ffn0": 1, "mix1": 2, "ffn1": 3}
        SCALED = NSQ
        HB = {"norm1": 0, "norm2": 8, "mix0": 16, "ffn0": 24, "mix1": 32, "ffn1": 40}
        RES = {"w_out": 0, "peer": 8, "mla": 16, "ffn0": 24, "ple0": 32, "hgrn": 40, "ffn1": 48, "ple1": 56}
        WIN_ORDER = (0, 2, 1, 3)
        UNITS = 8

        @block.tensor
        def _(pe):
            mm = nc.tensor.matmul

            def tile_in(tile, s, turn=0):
                slot = (tile + s) % RING
                pe.wait_ge(weights_loaded[slot], turn * 16 + ((tile + s) // RING + 1) * 16)
                return ring[slot]

            def linear(name, rhs, kb=8, by_token=False, tiles=None, first=0, count=None):
                t0 = FIRST[tiles or name]
                p0 = PROD[name] + first
                pad = 8 * -(-kb // 8) if kb > 8 else kb
                n = dict(PRODUCTS)[name] if count is None else count
                body = max(RING, RING * pad // 8)
                per = body * 8 // pad

                def some(i, np_):
                    for q in range(np_):
                        p = p0 + q
                        pe.wait_ge(bank_free, i * per + p + 1)
                        for tb in range(TB if by_token else 1):
                            for b in range(kb):
                                s, w = divmod(q * pad + b, 8)
                                new = w == 0 and tb == 0
                                w_ap = tile_in(t0, s, i * (body // RING)) if new else ring[(t0 + s) % RING]
                                if by_token:
                                    last = mm(ps[:, p % 2, tb * P:(tb + 1) * P], rhs(b)[:, tb * P:(tb + 1) * P],
                                              w_ap[:, w, :], start=b == 0, stop=b == kb - 1)
                                else:
                                    last = mm(ps[:, p % 2, :], w_ap[:, w, :], rhs(b), start=b == 0, stop=b == kb - 1)
                                if new:
                                    last.then_inc(tiles_started, 1)
                        last.then_inc(product_ready, 1)
                loops = n // per
                if loops > 1:
                    with pe.Fori(0, loops) as i:
                        some(i, per)
                    rest = n - loops * per
                    if rest:
                        t0, p0 = t0 + loops * body, p0 + loops * per
                        some(0, rest)
                else:
                    some(0, n)

            def sums(name, matrix):
                n, k = NORM_SHAPE[name]
                for j in range(n * k):
                    c, g = NSQ[name] + j, NGROUP[name] + j // k
                    if j % k == 0 and g >= 2:
                        pe.wait_ge(root_ready, g - 1)
                    pe.wait_ge(sq_ready, c + 1)
                    mm(ps[:, 2 + g % 2, :], matrix[:], plane(NORM[name][0] + c % 4), start=j % k == 0,
                       stop=j % k == k - 1).then_inc(sq_used, 1)

            def mean(res):
                for j in range(KC):
                    pe.wait_ge(residual_ready, RES[res] + j + 1)
                    last = mm(ps[:, 4, :], ones[:], X[:, j, :], start=j == 0, stop=j == KC - 1)
                last.then_inc(mean_ready, 1)

            def ada_columns(tile, column, n):
                for s in range(n):
                    w = tile_in(tile, s)
                    for k in range(KC):
                        last = mm(ps[:, 7, column + s:column + s + 1], w[:, k, :], cs[:, k:k + 1], start=k == 0,
                                  stop=k == KC - 1)
                        if k == 0:
                            last.then_inc(tiles_started, 1)
                    last.then_inc(ada_sums, 1)

            pe.sem_inc(onehot_free, 4)
            pe.wait_ge(c_ready, 1)
            ada_columns(FIRST["shift1"], SHIFT1, 8)
            ada_columns(FIRST["scale1"], SCALE1, 8)
            pe.wait_ge(consts_ready, 1)
            sums("norm1", ones)
            pe.wait_ge(h_ready, HB["norm1"] + KC)
            linear("w_in", lambda b: H[:, b, :], first=0, count=18)
            linear("w_in", lambda b: H[:, b, :], by_token=True, tiles="w_v", first=18, count=1)


            def win_scores(u):
                n, kv = divmod(u, 2)
                if u:
                    pe.wait_ge(exp_ready, u)
                lo = P if n == 0 else 0
                for g in range(4):
                    h = kv * 4 + WIN_ORDER[g]
                    r = slice(64 * (h % 2), 64 * (h % 2) + 64)
                    last = mm(ps[:, 2 + g // 2, (g % 2) * 256 + lo:(g % 2) * 256 + 256],
                              A[r, PQ + h // 2, n * P:(n + 1) * P], A[r, PKD + kv, (n - 1) * P + lo:(n + 1) * P],
                              start=True, stop=True)
                last.then_inc(scores_ready, 1)

            pe.wait_ge(bank_free, 2 + PROD["w_in"] + 6)
            win_scores(0)
            pe.wait_ge(bias_ready, 1)
            for u in range(UNITS):
                n, kv = divmod(u, 2)
                if u + 1 < UNITS:
                    win_scores(u + 1)
                ada_columns(FIRST["ada_rest"] + 3 * u, GATE1 + 3 * u, 3)
                pe.wait_ge(probs_ready, u + 1)
                kbs = [1] if n == 0 else [0, 1]
                pv = A[:, PROBS[u % 2]:PROBS[u % 2] + 2, :].rearrange("p a (h k) -> p (a h) k", h=2)
                if u:
                    pe.wait_ge(pt_taken, u)
                for g in range(4):
                    for kb in kbs:
                        i = g * 2 + kb
                        last = nc.tensor.transpose(ps[:, 4 + i // 4, (i % 4) * P:(i % 4) * P + P],
                                                   pv[:, g, kb * P:(kb + 1) * P], ident[:])
                last.then_inc(pt_ready, 1)
                pe.wait_ge(pt_taken, u + 1)
                if u:
                    pe.wait_ge(o_taken, u)
                ptv = A[:, PT[u % 2]:PT[u % 2] + 2, :].rearrange("p a (h k) -> p (a h) k", h=4)
                for g in range(4):
                    h = WIN_ORDER[g]
                    for kb in kbs:
                        t0 = (n - 1 + kb) * P
                        last = mm(ps[64 * (h % 2):64 * (h % 2) + 64, 6, (h // 2) * P:(h // 2) * P + P],
                                  A[:, PV, t0 + kv * 64:t0 + kv * 64 + 64], ptv[:, g * 2 + kb, :],
                                  start=kb == kbs[0], stop=kb == 1)
                last.then_inc(o_ready, 1)
            sums("attn", halves)
            sums("conv", halves)
            pe.wait_ge(scaled_ready, SCALED["conv"] + 4)
            linear("w_out", lambda b: A[:, MIX + b, :])
            pe.wait_ge(ada_ready, 2)
            ada_columns(FIRST["gate2"], GATE2, 8)
            sums("norm2", ones)
            pe.wait_ge(h_ready, HB["norm2"] + KC)
            linear("w_query", lambda b: H[:, b, :])

            for t in range(2):
                w = tile_in(FIRST["keys"], t)
                for tb in range(TB):
                    for f in range(2):
                        p = PROD["keys"] + t * 8 + tb * 2 + f
                        pe.wait_ge(bank_free, p + 1)
                        if t == 0 and tb == 0:
                            pe.wait_ge(bank_free, 2 + PROD["w_query"] + 16)
                        for j in range(4):
                            hh = t * 8 + f * 4 + j
                            last = mm(ps[:, p % 2, j * P:(j + 1) * P], A[:, STAGE + hh, tb * P:(tb + 1) * P],
                                      w[:, f * 4 + j, :], start=True, stop=True)
                            if tb == 0 and f == 0 and j == 0:
                                last.then_inc(tiles_started, 1)
                        last.then_inc(product_ready, 1)

            ps_gates = ps[:, 6:8, :].rearrange("p b (t i) -> p b t i", t=4)
            for tb in range(TB):
                for s in range(4):
                    t = tb * 4 + s
                    w = tile_in(FIRST["u_first"] + t, 0)
                    pe.wait_ge(bank_free, PROD["u_first"] + t + 1)
                    for k in range(KC):
                        last = mm(ps[:, (PROD["u_first"] + t) % 2, :], w[:, k, :], H[:, k, :], start=k == 0,
                                  stop=k == KC - 1)
                        if k == 0:
                            last.then_inc(tiles_started, 1)
                    last.then_inc(product_ready, 1)
                pe.wait_ge(route_ready, tb + 1)
                for a in range(3):
                    last = nc.tensor.transpose(ps[:, 2, a * P:(a + 1) * P], routed[:, a, :], ident[:])
                last.then_inc(route_turned, 1)
                with pe.Fori(0, P // 8) as i:
                    for s in range(8):
                        tok = tb * P + s
                        pe.wait_ge(onehot_ready, i * 8 + tok + 1)
                        if s % 4 == 0:
                            pe.wait_ge(gate_bank_free, i * 2 + tok // 4 + 1)
                        mm(ps_gates[:, s // 4, s % 4, :], hot2[:, s % 4, :], hot1[:, s % 4, :], start=True,
                           stop=True).then_inc(onehot_free, 1)

            def expert_up(g, half, gi):
                t0, p0 = FIRST[f"u{g}" + "ab"[half]], PROD[f"u{g}"] + 8 * half
                for s in range(8):
                    w = tile_in(t0, s, gi * (64 // RING))
                    pe.wait_ge(bank_free, gi * 32 + p0 + s + 1)
                    for k in range(KC):
                        last = mm(ps[:, (p0 + s) % 2, :], w[:, k, :], H[:, k, :], start=k == 0, stop=k == KC - 1)
                        if k == 0:
                            last.then_inc(tiles_started, 1)
                    last.then_inc(product_ready, 1)

            def expert_down(g, half, gi):
                t0 = FIRST[f"v{g}" + "ab"[half]]
                for s in range(8):
                    w = tile_in(t0, s, gi * (64 // RING))
                    for e in range(2):
                        i = 2 * s + e
                        if half == 0:
                            pe.wait_ge(mixed_ready, gi * 32 + g * GROUP + i + 1)
                        for d in range(4):
                            if i == 0:
                                pe.wait_ge(sum_bank_free, gi * 16 + 4 * (2 * g + half) + d + 1)
                            last = mm(ps[:, 2 + d, :], w[:, 4 * e + d, :], A[:, (g % 2) * GROUP + i, :], start=i == 0,
                                      stop=i == GROUP - 1)
                            if e == 0 and d == 0:
                                last.then_inc(tiles_started, 1)
                            if i == GROUP - 1:
                                last.then_inc(sums_ready, 1)

            with pe.Fori(0, GROUPS // 2 - 1) as gi:
                for g in range(2):
                    for half in range(2):
                        expert_down(g, half, gi)
                        expert_up(g + 1, half, gi)
            for g in (GROUPS - 2, GROUPS - 1):
                for half in range(2):
                    expert_down(g, half, 0)
                    if g < GROUPS - 1:
                        expert_up(g + 1, half, 0)
            sums("final", ones)

            pe.wait_ge(scaled_ready, SCALED["final"] + KC)
            linear("dqkv", lambda b: X[:, b, :])
            sums("cq", ones)
            sums("ckv", ones)
            pe.wait_ge(scaled_ready, SCALED["ckv"] + 2)
            linear("uq", lambda b: plane(CQN + b), kb=2)
            linear("uk", lambda b: plane(CKN + b), kb=2)
            linear("uv", lambda b: plane(CKN + b), kb=2, by_token=True)

            def mla_scores(m):
                n, pair = divmod(m, 4)
                pe.wait_ge(exp_ready, UNITS + m)
                for g in range(2):
                    h = 2 * pair + g
                    out_ = ps[:, 2 + g, 0:(n + 1) * P]
                    mm(out_, A[:, QN + h, n * P:(n + 1) * P], A[:, KN + h, 0:(n + 1) * P], start=True, stop=False)
                    r = slice(64 * g, 64 * g + 64)
                    last = mm(out_, A[r, QR + pair, n * P:(n + 1) * P], A[r, 4, 0:(n + 1) * P], start=False,
                              stop=True)
                last.then_inc(scores_ready, 1)

            pe.wait_ge(rope_ready, 2)
            mla_scores(0)
            for m in range(16):
                n, pair = divmod(m, 4)
                if m + 1 < 16:
                    mla_scores(m + 1)
                pe.wait_ge(probs_ready, UNITS + m + 1)
                pe.wait_ge(pt_taken, UNITS + m)
                pv = A[:, MPROBS[m % 2]:MPROBS[m % 2] + 2, :]
                for g in range(2):
                    for kb in range(n + 1):
                        last = nc.tensor.transpose(ps[:, 4 + g, kb * P:(kb + 1) * P], pv[:, g, kb * P:(kb + 1) * P],
                                                   ident[:])
                last.then_inc(pt_ready, 1)
                pe.wait_ge(pt_taken, UNITS + m + 1)
                pe.wait_ge(o_taken, UNITS + m)
                for g in range(2):
                    for kb in range(n + 1):
                        last = mm(ps[:, 6, g * P:(g + 1) * P], A[:, VM + 2 * pair + g, kb * P:(kb + 1) * P],
                                  A[:, MPT[m % 2] + g, kb * P:(kb + 1) * P], start=kb == 0, stop=kb == n)
                last.then_inc(o_ready, 1)
            pe.wait_ge(o_taken, UNITS + 16)
            linear("w_o", lambda b: plane(OM + b))
            mean("mla")
            sums("mix0", ones)

            def ffn_and_ple(i):
                pe.wait_ge(h_ready, HB[f"mix{i}"] + KC)
                linear(f"ffn_in{i}", lambda b: X[:, b, :])
                pe.wait_ge(ff_ready, 2 + FF * (i + 1))
                linear(f"ffn_down{i}", lambda b: plane(HF + b), kb=FF)
                mean(f"ffn{i}")
                sums(f"ffn{i}", ones)
                pe.wait_ge(h_ready, HB[f"ffn{i}"] + KC)
                linear(f"ple_gate{i}", lambda b: X[:, b, :])
                pe.wait_ge(p_loaded, 16 * (i + 1))
                linear(f"ple_proj{i}", lambda b: ACC[:, b, :], kb=2)

            ffn_and_ple(0)

            pe.wait_ge(residual_ready, RES["ple0"] + KC)
            linear("hgrn_in", lambda b: X[:, b, :], count=16)
            linear("hgrn_in", lambda b: X[:, b, :], by_token=True, tiles="hgrn_v", first=16, count=8)
            linear("hgrn_in", lambda b: X[:, b, :], tiles="hgrn_gate", first=24, count=8)
            for h in range(HEADS):
                pe.wait_ge(khat_ready, h + 1)
                if h >= 2:
                    pe.wait_ge(kt_taken, h - 1)
                for tb in range(TB):
                    last = nc.tensor.transpose(ps[:, 2 + h % 2, tb * P:(tb + 1) * P], H[:, h, tb * P:(tb + 1) * P],
                                               ident[:])
                last.then_inc(kt_ready, 1)

            def pairs(u):
                h, lv = divmod(u, LEVELS + 1)
                if lv < LEVELS:
                    pe.wait_ge(level_ready, h * LEVELS + lv + 1)
                    k_ap = q_ap = plane(HM + (h * LEVELS + lv) % 2)
                else:
                    k_ap, q_ap = plane(HK + h), plane(HQ + h)
                if u >= 2:
                    pe.wait_ge(masked_ready, u - 1)
                for tb in range(TB):
                    r = slice(tb * P, (tb + 1) * P)
                    last = mm(ps[:, 6 + u % 2, r], k_ap[:, r], q_ap[:, r], start=True, stop=True)
                last.then_inc(pair_ready, 1)

            n_units = HEADS * (LEVELS + 1)
            pe.wait_ge(kt_taken, HEADS)
            pairs(0)
            for u in range(n_units):
                h, lv = divmod(u, LEVELS + 1)
                if u + 1 < n_units:
                    pairs(u + 1)
                pe.wait_ge(masked_ready, u + 1)
                if lv == 0 and h >= 2:
                    pe.wait_ge(intra_taken, h - 1)
                for tb in range(TB):
                    r = slice(tb * P, (tb + 1) * P)
                    last = mm(ps[:, 4 + h % 2, r], A[:, HV + h, r], H[:, u % 2, r], start=lv == 0 and tb == 0,
                              stop=lv == LEVELS, skip_group_check=True)
                last.then_inc(intra_ready, 1)
            for c in range(NCH):
                r = slice(64 * (c % 2), 64 * (c % 2) + 64)
                w = slice((c // 2) * P, (c // 2) * P + P)
                if c < NCH - 1:
                    if c:
                        pe.wait_ge(state_ready, HEADS * c)
                    for h in range(HEADS):
                        last = mm(ps[:, 2 + h // 4, (h % 4) * P:(h % 4) * P + P], ACC[r, h, w], A[r, HV + h, w],
                                  start=True, stop=True)
                    last.then_inc(delta_ready, 1)
                if c:
                    if c >= 2:
                        pe.wait_ge(inter_added, c - 1)
                    pe.wait_ge(state_ready, HEADS * c)
                    for h in range(HEADS):
                        last = mm(ps[:, 6, h * CH:(h + 1) * CH], STATE[:, h, :], A[:, HLF + h, c * CH:(c + 1) * CH],
                                  start=True, stop=True)
                    last.then_inc(inter_ready, 1)
            sums("hgrn", ones)
            pe.wait_ge(gated_ready, HEADS)
            linear("hgrn_o", lambda b: plane(HO + b))
            mean("hgrn")
            sums("mix1", ones)
            ffn_and_ple(1)

        @block.scalar
        def _(act):
            fn = nc.scalar.activation

            def take(name, j, out_, func=ACT.Copy, **kw):
                p = PROD[name] + j
                act.wait_ge(product_ready, p + 1)
                fn(out_, ps[:, p % 2, :], func, **kw).then_inc(bank_free, 1)

            def norm(name, src, ready, width, eps):
                n, k = NORM_SHAPE[name]

                def root(g):
                    act.wait_ge(sq_used, NSQ[name] + (g + 1) * k)
                    fn(plane(NORM[name][1] + g), ps[:, 2 + (NGROUP[name] + g) % 2, :], ACT.Sqrt, scale=1.0 / width,
                       bias=eps_col[eps]).then_inc(root_ready, 1)

                for j in range(n * k):
                    c = NSQ[name] + j
                    if c >= 4:
                        act.wait_ge(sq_used, c - 3)
                    ready(j)
                    fn(plane(NORM[name][0] + c % 4), src(j), ACT.Square).then_inc(sq_ready, 1)
                    if k == 1 and j:
                        root(j - 1)
                root(n - 1)

            def add_bias(name, dst, bias):
                for j in range(KC):
                    act.wait_ge(scaled_ready, SCALED[name] + j + 1)
                    fn(dst(j), dst(j), ACT.Identity, bias=bias(j)).then_inc(h_ready, 1)

            act.sem_inc(bank_free, 2)
            act.sem_inc(gate_bank_free, 2)
            act.wait_ge(inputs_loaded, 16 * 2)
            fn(cs[:], col("c", 0, 8), ACT.Silu).then_inc(c_ready, 1)
            act.wait_ge(lb_in, 1)
            fn(small[:, 40:56], small[:, 40:56], ACT.Exp).then_inc(lb_exp, 1)
            act.wait_ge(consts_ready, 1)
            norm("norm1", lambda j: X[:, j, :], lambda j: None, D, 1e-6)
            act.wait_ge(ada_ready, 1)
            add_bias("norm1", lambda j: H[:, j, :], lambda j: ada_col(SHIFT1, j))
            order = list(range(4)) + [4, 5] + list(range(6, 18))
            for j in order:
                take("w_in", j, plane(j), ACT.Identity, bias=col("b_in", j))
            take("w_in", 18, plane(PV))

            def attention(base, n_units, exps, turned_out, o_out):
                for u in range(n_units):
                    if u == 0:
                        exps(0)
                    b = base + u
                    act.wait_ge(pt_ready, b + 1)
                    if b - base >= 2:
                        act.wait_ge(o_ready, b - 1)
                    turned_out(u)
                    if u + 1 < n_units:
                        exps(u + 1)
                    act.wait_ge(o_ready, b + 1)
                    o_out(u)

            def win_exps(u):
                n, kv = divmod(u, 2)
                lo = P if n == 0 else 0
                act.wait_ge(shift_ready, u + 1)
                if u >= 2:
                    act.wait_ge(pt_ready, u - 1)
                pv = A[:, PROBS[u % 2]:PROBS[u % 2] + 2, :].rearrange("p a (h k) -> p (a h) k", h=2)
                fn(sm(u, 8, 4), sm(u, 4, 4), ACT.Exp).then_inc(sink_ready, 1)
                for g in range(4):
                    last = fn(pv[:, g, lo:2 * P], ps[:, 2 + g // 2, (g % 2) * 256 + lo:(g % 2) * 256 + 256], ACT.Exp,
                              bias=sm(u, g), accum_out=sm(u, 12 + g))
                last.then_inc(exp_ready, 1)

            def win_turned(u):
                kbs = [1] if u < 2 else [0, 1]
                src = ps[:, 4:6, :].rearrange("p b (h k) -> p (b h) k", h=4)
                dst = A[:, PT[u % 2]:PT[u % 2] + 2, :].rearrange("p a (h k) -> p (a h) k", h=4)
                if u < 2:
                    src = src.rearrange("p (g k) t -> p g k t", k=2)[:, :, 1, :]
                    dst = dst.rearrange("p (g k) t -> p g k t", k=2)[:, :, 1, :]
                fn(dst, src, ACT.Copy).then_inc(pt_taken, 1)

            def win_out(u):
                n, kv = divmod(u, 2)
                fn(A[:, ATT + 2 * kv:ATT + 2 * kv + 2, n * P:(n + 1) * P],
                   ps[:, 6, 0:2 * P].rearrange("p (c t) -> p c t", c=2), ACT.Copy).then_inc(o_taken, 1)

            attention(0, UNITS, win_exps, win_turned, win_out)
            norm("attn", lambda j: plane(ATT + j), lambda j: act.wait_ge(o_taken, UNITS), HD, 1e-6)
            norm("conv", lambda j: zv[:, j, 2:T + 2], lambda j: act.wait_ge(conv_ready, j + 1), HD, 1e-6)
            for j in range(KC):
                take("w_out", j, plane(j), ACT.Identity, bias=col("b_out", j))
            norm("norm2", lambda j: X[:, j, :], lambda j: act.wait_ge(residual_ready, RES["w_out"] + j + 1), D, 1e-6)
            act.wait_ge(ada_ready, 3)
            add_bias("norm2", lambda j: H[:, j, :], lambda j: ada_col(SHIFT2, j))
            for j in range(16):
                take("w_query", j, plane(STAGE + j))

            for t in range(2):
                for tb in range(TB):
                    for f in range(2):
                        take("keys", t * 8 + tb * 2 + f, plane(SCORES + 4 * tb + 2 * t + f))
            ps_gates = ps[:, 6:8, :].rearrange("p b (t i) -> p b i t", t=4)
            for tb in range(TB):
                for s in range(4):
                    take("u_first", tb * 4 + s, plane(tb * 4 + s), ACT.Gelu)
                act.wait_ge(gate_in, tb + 1)
                g_ap = routed[:, 2, :]
                fn(g_ap, g_ap, ACT.Exp).then_inc(gate_exp, 1)
                act.wait_ge(route_turned, tb + 1)
                fn(turned[:], ps[:, 2, 0:3 * P].rearrange("p (a t) -> p a t", a=3), ACT.Copy).then_inc(route_taken, 1)
                if tb == 0:
                    act.wait_ge(bank_free, 2 + PROD["keys"] + 16)
                else:
                    act.wait_ge(gate_stored, 16 * tb)
                with act.Fori(0, P // 8) as i:
                    for b in range(2):
                        act.wait_ge(onehot_free, i * 8 + 4 + tb * P + 4 * b + 4)
                        fn(staging[:, :, bass.ds(i * 8 + 4 * b, 4)], ps_gates[:, b, :, :], ACT.Copy)\
                            .then_inc(gate_bank_free, 1)
                act.wait_ge(gate_bank_free, 2 + 32 * (tb + 1))
                act.dma_start(gate_map.rearrange("i j t -> j i t")[:, :, tb * P:(tb + 1) * P], staging)\
                    .then_inc(gate_stored, 16)

            act.wait_ge(gate_stored, 16 * TB)

            def gelus(g, gi):
                for s in range(GROUP):
                    p = PROD[f"u{g}"] + s
                    act.wait_ge(product_ready, gi * 32 + p + 1)
                    fn(A[:, (g % 2) * GROUP + s, :], ps[:, p % 2, :], ACT.Gelu).then_inc(bank_free, 1)

            with act.Fori(0, GROUPS // 2 - 1) as gi:
                gelus(1, gi)
                gelus(2, gi)
            gelus(GROUPS - 1, 0)
            norm("final", lambda j: X[:, j, :], lambda j: act.wait_ge(residual_ready, RES["peer"] + j + 1), D, 1e-6)

            act.wait_ge(rope_in, 1)
            fn(plane(SIN), plane(SIN), ACT.Sin)
            fn(plane(COS), plane(COS), ACT.Sin).then_inc(rope_out, 1)
            for j in range(6):
                take("dqkv", j, plane(j))
            norm("cq", lambda j: plane(j), lambda j: act.wait_ge(bank_free, 2 + PROD["dqkv"] + j + 1), 256, 1e-6)
            norm("ckv", lambda j: plane(2 + j), lambda j: act.wait_ge(bank_free, 2 + PROD["dqkv"] + 2 + j + 1), 256,
                 1e-6)
            for j in range(16):
                take("uq", j, plane(QN + j))
            for j in range(8):
                take("uk", j, plane(KN + j))
            for j in range(8):
                take("uv", j, plane(VM + j))

            scale = 192 ** -0.5

            def mla_exps(m):
                n, pair = divmod(m, 4)
                act.wait_ge(shift_ready, UNITS + m + 1)
                if m >= 2:
                    act.wait_ge(pt_ready, UNITS + m - 1)
                for g in range(2):
                    last = fn(A[:, MPROBS[m % 2] + g, 0:(n + 1) * P], ps[:, 2 + g, 0:(n + 1) * P], ACT.Exp,
                              bias=sm(m, g), scale=scale, accum_out=sm(m, 12 + g))
                last.then_inc(exp_ready, 1)

            def mla_turned(m):
                w = (m // 4 + 1) * P
                fn(A[:, MPT[m % 2]:MPT[m % 2] + 2, 0:w], ps[:, 4:6, 0:w], ACT.Copy).then_inc(pt_taken, 1)

            def mla_out(m):
                n, pair = divmod(m, 4)
                fn(A[:, OM + 2 * pair:OM + 2 * pair + 2, n * P:(n + 1) * P],
                   ps[:, 6, 0:2 * P].rearrange("p (c t) -> p c t", c=2), ACT.Copy).then_inc(o_taken, 1)

            attention(UNITS, 16, mla_exps, mla_turned, mla_out)
            for j in range(KC):
                take("w_o", j, plane(TMP + j))

            def layer_norm(name, g, b):
                i = LN[name]
                norm(name, lambda j: H[:, j, :], lambda j: act.wait_ge(centered_ready, KC * i + j + 1), D, 1e-5)
                add_bias(name, lambda j: X[:, j, :], lambda j: col(b, KC * int(name[-1]) + j))

            def ffn_and_ple(f):
                layer_norm(f"mix{f}", "ln_mix_g", "ln_mix_b")
                with act.Fori(0, FF // 2) as i:
                    for j in range(2):
                        p = PROD[f"ffn_in{f}"] + 2 * j
                        act.wait_ge(ff_ready, i * 2 + FF * f + j + 1)
                        act.wait_ge(product_ready, i * 4 + p + 1)
                        fn(plane(SG + j), ps[:, p % 2, :], ACT.Silu).then_inc(bank_free, 1)
                        act.wait_ge(product_ready, i * 4 + p + 2)
                        fn(plane(UU + j), ps[:, (p + 1) % 2, :], ACT.Copy).then_inc(bank_free, 1)
                for j in range(KC):
                    take(f"ffn_down{f}", j, plane(TMP + j))
                layer_norm(f"ffn{f}", "ln_ffn_g", "ln_ffn_b")
                for j in range(KC):
                    take(f"ple_gate{f}", j, plane(j), ACT.Sigmoid)
                for j in range(KC):
                    take(f"ple_proj{f}", j, plane(8 + j))

            ffn_and_ple(0)

            for j in range(8):
                take("hgrn_in", j, plane(HQ + j), ACT.Silu)
            for j in range(8):
                p = PROD["hgrn_in"] + 8 + j
                act.wait_ge(product_ready, p + 1)
                fn(plane(HLF + j), ps[:, p % 2, :], ACT.Sigmoid)
                fn(plane(HK + j), ps[:, p % 2, :], ACT.Sigmoid, scale=-1.0).then_inc(bank_free, 1)
            for j in range(8):
                take("hgrn_in", 16 + j, plane(HV + j))
            for j in range(8):
                take("hgrn_in", 24 + j, plane(HGT + j), ACT.Silu)
            for h in range(HEADS):
                act.wait_ge(forget_in, h + 1)
                fn(plane(HLF + h), plane(HLF + h), ACT.Ln).then_inc(log_ready, 1)
            for h in range(HEADS):
                act.wait_ge(cum_ready, h + 1)
                fn(plane(HLF + h), plane(HG + h), ACT.Exp).then_inc(decay_ready, 1)
                act.wait_ge(decay_in, h + 1)
                fn(H[:, h, :], H[:, h, :], ACT.Exp).then_inc(decay_ready, 1)
            ends = A[:, HG:HG + 8, :].rearrange("p h (c t) -> p h c t", c=NCH)[:, :, :, CH - 1]
            fn(dec[:], ends, ACT.Exp).then_inc(decay_ready, 1)
            for h in range(HEADS):
                act.wait_ge(kt_ready, h + 1)
                if h == 0:
                    act.wait_ge(residual_ready, RES["ple0"] + KC)
                fn(ACC[:, h, :], ps[:, 2 + h % 2, :], ACT.Copy).then_inc(kt_taken, 1)
            for h in range(HEADS):
                for lv in range(LEVELS):
                    e = h * LEVELS + lv
                    act.wait_ge(gap_ready, e + 1)
                    fn(plane(HE + e % 4), plane(HE + e % 4), ACT.Exp).then_inc(gap_exp, 1)
                if h:
                    act.wait_ge(intra_ready, (LEVELS + 1) * h)
                    fn(plane(HO + h - 1), ps[:, 4 + (h - 1) % 2, :], ACT.Copy).then_inc(intra_taken, 1)
            act.wait_ge(intra_ready, (LEVELS + 1) * HEADS)
            fn(plane(HO + HEADS - 1), ps[:, 4 + (HEADS - 1) % 2, :], ACT.Copy).then_inc(intra_taken, 1)
            norm("hgrn", lambda j: plane(HO + j), lambda j: act.wait_ge(inter_added, NCH - 1), P, 1e-6)
            for j in range(KC):
                take("hgrn_o", j, plane(TMP + j))
            ffn_and_ple(1)

        @block.vector
        def _(dve):
            v = nc.vector
            own = Steps(dve, dve_step)

            def taken(name, j):
                dve.wait_ge(bank_free, 2 + PROD[name] + j + 1)

            def inverse(name):
                for g in range(NORM_SHAPE[name][0]):
                    dve.wait_ge(root_ready, NGROUP[name] + g + 1)
                    r = plane(NORM[name][1] + g)
                    v.reciprocal(r, r).then_inc(rstd_ready, 1)

            def scaled(name, src, gain, dst):
                n, k = NORM_SHAPE[name]
                for j in range(n * k):
                    dve.wait_ge(rstd_ready, NGROUP[name] + j // k + 1)
                    v.scalar_tensor_tensor(out=dst(j), in0=src(j), scalar=gain(j), in1=plane(NORM[name][1] + j // k),
                                           op0=ALU.mult, op1=ALU.mult).then_inc(scaled_ready, 1)

            dve.sem_inc(sum_bank_free, 4)
            dve.sem_inc(ff_ready, 2)
            dve.wait_ge(inputs_loaded, 16 * 2)

            lb0, lb1 = col("lb", 0, 8), col("lb", 8, 8)
            t0, t1, t2 = small[:, 32:40], small[:, 40:48], small[:, 48:56]
            own.do(v.tensor_tensor(t0, lb0, lb1, ALU.max))
            own.wait()
            own.do(v.tensor_tensor(t1, lb0, t0, ALU.subtract))
            v.tensor_tensor(t2, lb1, t0, ALU.subtract).then_inc(lb_in, 1)
            own.wait()
            dve.wait_ge(lb_exp, 1)
            own.do(v.tensor_tensor(t0, t1, t2, ALU.add))
            own.wait()
            own.do(v.reciprocal(t0, t0))
            own.wait()
            own.do(v.tensor_tensor(t1, t1, t0, ALU.mult))
            own.do(v.tensor_tensor(t2, t2, t0, ALU.mult))
            own.wait()
            own.do(v.tensor_tensor(t2, t1, t2, ALU.add))
            own.wait()
            own.do(v.tensor_tensor(small[:, LB:LB + 8], t2, t1, ALU.subtract))
            own.wait()
            own.do(v.tensor_scalar(small[:, OMLB:OMLB + 8], small[:, LB:LB + 8], -1.0, 1.0, ALU.mult, ALU.add))

            def ada_part(part, n, at):
                dve.wait_ge(ada_sums, part + n)
                v.tensor_tensor(ada_col(part, 0, n), ps[:, 7, part:part + n], col("b_ada", part, n), ALU.add)\
                    .then_inc(ada_ready, 1)

            def modulation(part, at, gain):
                dve.wait_ge(ada_ready, at)
                own.do(v.scalar_tensor_tensor(out=small[:, GS1:GS1 + 8], in0=ada_col(part, 0, 8), scalar=1.0,
                                              in1=col(gain, 0, 8), op0=ALU.add, op1=ALU.mult))
                own.wait()

            ada_part(0, 16, 1)
            modulation(SCALE1, 1, "norm1_g")
            inverse("norm1")
            scaled("norm1", lambda j: X[:, j, :], lambda j: small[:, GS1 + j:GS1 + j + 1], lambda j: H[:, j, :])

            taken("w_in", 18)
            pv3 = plane(PV).rearrange("p (b c) -> p b c", b=TB)
            v.tensor_tensor(pv3, pv3, col("b_v", 0, P).unsqueeze(1).broadcast_to([P, TB, P]), ALU.add)\
                .then_inc(bias_ready, 1)
            dve.wait_ge(consts_ready, 1)

            def win_shift(u):
                n, kv = divmod(u, 2)
                lo = P if n == 0 else 0
                dve.wait_ge(scores_ready, u + 1)
                s = ps[:, 2:4, :].rearrange("p b (h k) -> p (b h) k", h=2)[:, :, lo:2 * P]
                own.do(v.scalar_tensor_tensor(out=s, in0=s, scalar=HD ** -0.5,
                                              in1=win_mask[:, lo:2 * P].unsqueeze(1).broadcast_to([P, 4, 2 * P - lo]),
                                              op0=ALU.mult, op1=ALU.add))
                own.wait()
                own.do(v.tensor_reduce(sm(u, 0, 4), s, AX, ALU.max))
                own.wait()
                own.do(v.tensor_tensor(sm(u, 0, 4), sm(u, 0, 4), col("sinks", 4 * kv, 4), ALU.max))
                own.wait()
                own.do(v.tensor_tensor(sm(u, 4, 4), col("sinks", 4 * kv, 4), sm(u, 0, 4), ALU.subtract))
                v.tensor_scalar(sm(u, 0, 4), sm(u, 0, 4), -1.0, None, ALU.mult).then_inc(shift_ready, 1)

            def win_probs(u):
                n, kv = divmod(u, 2)
                lo = P if n == 0 else 0
                dve.wait_ge(exp_ready, u + 1)
                own.do(v.tensor_tensor(sm(u, 12, 4), sm(u, 12, 4), sm(u, 8, 4), ALU.add))
                own.wait()
                own.do(v.reciprocal(sm(u, 12, 4), sm(u, 12, 4)))
                own.wait()
                pv = A[:, PROBS[u % 2]:PROBS[u % 2] + 2, :].rearrange("p a (h k) -> p (a h) k", h=2)[:, :, lo:2 * P]
                v.tensor_tensor(pv, pv, sm(u, 12, 4).unsqueeze(2).broadcast_to([P, 4, 2 * P - lo]), ALU.mult)\
                    .then_inc(probs_ready, 1)

            win_shift(0)
            for u in range(UNITS):
                win_probs(u)
                if u + 1 < UNITS:
                    win_shift(u + 1)
                if u == 0:
                    own.do(v.memset(zv[:, :, 0:2], 0.0))
                    own.do(v.tensor_tensor(zv[:, :, 2:T + 2], A[:, PCG:PCG + 4, :], A[:, PU:PU + 4, :], ALU.mult))
                    gated = own.n
                if 1 <= u <= 4:
                    j = u - 1
                    own.wait(gated)
                    cp = plane(PU + j)
                    own.do(v.tensor_scalar(cp, zv[:, j, 2:T + 2], col("conv_w", 8 + j), None, ALU.mult))
                    own.wait()
                    own.do(v.scalar_tensor_tensor(out=cp, in0=zv[:, j, 1:T + 1], scalar=col("conv_w", 4 + j), in1=cp,
                                                  op0=ALU.mult, op1=ALU.add))
                    own.wait()
                    own.do(v.scalar_tensor_tensor(out=cp, in0=zv[:, j, 0:T], scalar=col("conv_w", j), in1=cp,
                                                  op0=ALU.mult, op1=ALU.add))
                    own.wait()
                    v.tensor_tensor(zv[:, j, 2:T + 2], cp, plane(PB_ + j), ALU.mult).then_inc(conv_ready, 1)
            inverse("attn")
            scaled("attn", lambda j: plane(ATT + j), lambda j: col("attn_out_g", j), lambda j: plane(MIX + j))
            inverse("conv")
            scaled("conv", lambda j: zv[:, j, 2:T + 2], lambda j: col("conv_out_g", j), lambda j: plane(MIX + 4 + j))
            ada_part(16, 24, 2)
            dve.wait_ge(ada_ready, 2)

            for j in range(KC):
                taken("w_out", j)
                v.scalar_tensor_tensor(out=X[:, j, :], in0=plane(j), scalar=ada_col(GATE1, j), in1=X[:, j, :],
                                       op0=ALU.mult, op1=ALU.add).then_inc(residual_ready, 1)
            ada_part(40, 8, 3)
            modulation(SCALE2, 3, "norm2_g")
            inverse("norm2")
            dve.wait_ge(residual_ready, RES["w_out"] + KC)
            scaled("norm2", lambda j: X[:, j, :], lambda j: small[:, GS1 + j:GS1 + j + 1], lambda j: H[:, j, :])

            best = accf[:, 0:256].rearrange("p (h k) -> p h k", h=16)
            best_at = accf[:, 256:512].rearrange("p (h k) -> p h k", h=16)
            best_i = best_at.bitcast(U32)
            best_f = accf[:, 512:768].rearrange("p (h k) -> p h k", h=16)
            top = accf[:, 768:896].rearrange("p (h k) -> p h k", h=8)
            top_i = accf[:, 896:1024].bitcast(U32)
            hi_i = accf[:, 1024:1152].bitcast(U32)
            lo_i = accf[:, 1152:1280].bitcast(U32)
            hi = accf[:, 1280:1408]
            lo = accf[:, 1408:1536]
            total = accf[:, 1536:1544]

            def route(tb):
                four = A[:, SCORES + 4 * tb:SCORES + 4 * tb + 4, :].rearrange("p a t -> p (a t)")
                s = four.rearrange("p (h n) -> p h n", h=16)
                taken("keys", 8 + tb * 2 + 1)
                for h in range(16):
                    own.do(v.max(best[:, h, 0:8], s[:, h, :]))
                own.wait()
                for h in range(16):
                    own.do(v.max_index(best_i[:, h, 0:8], best[:, h, 0:8], s[:, h, :]))
                own.wait()
                for h in range(16):
                    own.do(v.match_replace(out=s[:, h, :], in_to_replace=best[:, h, 0:8], in_values=s[:, h, :],
                                           imm_value=LOWEST))
                own.wait()
                for h in range(16):
                    own.do(v.max(best[:, h, 8:16], s[:, h, :]))
                own.wait()
                for h in range(16):
                    own.do(v.max_index(best_i[:, h, 8:16], best[:, h, 8:16], s[:, h, :]))
                own.wait()
                own.do(v.tensor_copy(best_f, best_i))
                pair = best.rearrange("p (h f) k -> p h f k", f=2)
                cand4 = four.rearrange("p (h a b) -> p h a b", h=8, a=TOPK)
                cand = four.rearrange("p (h n) -> p h n", h=8)
                for h in range(8):
                    own.do(v.tensor_tensor(cand4[:, h], pair[:, h, 0, :].unsqueeze(2).broadcast_to([P, TOPK, TOPK]),
                                           pair[:, h, 1, :].unsqueeze(1).broadcast_to([P, TOPK, TOPK]), ALU.add))
                own.wait()
                top_iv = top_i.rearrange("p (h k) -> p h k", h=8)
                for h in range(8):
                    own.do(v.max(top[:, h, 0:8], cand[:, h, :]))
                own.wait()
                for h in range(8):
                    own.do(v.max_index(top_iv[:, h, 0:8], top[:, h, 0:8], cand[:, h, :]))
                own.wait()
                for h in range(8):
                    own.do(v.match_replace(out=cand[:, h, :], in_to_replace=top[:, h, 0:8], in_values=cand[:, h, :],
                                           imm_value=LOWEST))
                own.wait()
                for h in range(8):
                    own.do(v.max(top[:, h, 8:16], cand[:, h, :]))
                own.wait()
                for h in range(8):
                    own.do(v.max_index(top_iv[:, h, 8:16], top[:, h, 8:16], cand[:, h, :]))
                g_ap = routed[:, 2, :].rearrange("p (h k) -> p h k", h=8)
                if tb:
                    dve.wait_ge(route_turned, tb)
                v.tensor_tensor(g_ap, top, top[:, :, 0:1].broadcast_to([P, 8, TOPK]), ALU.subtract)\
                    .then_inc(gate_in, 1)
                own.wait()
                own.do(v.tensor_scalar(hi_i, top_i, 4, None, ALU.logical_shift_right))
                own.do(v.tensor_scalar(lo_i, top_i, 15, None, ALU.bitwise_and))
                own.wait()
                own.do(v.tensor_copy(hi, hi_i))
                own.do(v.tensor_copy(lo, lo_i))
                own.wait()
                pick = four.rearrange("p (h k a) -> p h k a", h=8, k=TOPK)
                pick3 = four.rearrange("p (q a) -> p q a", a=TOPK)
                bf = best_f.rearrange("p (h f) k -> p h f k", f=2)
                for f, place in enumerate((hi, lo)):
                    own.do(v.tensor_tensor(pick3, place.unsqueeze(2).broadcast_to([P, P, TOPK]),
                                           iota[:, 0:TOPK].unsqueeze(1).broadcast_to([P, P, TOPK]), ALU.is_equal))
                    own.wait()
                    own.do(v.tensor_tensor(pick, pick, bf[:, :, f, :].unsqueeze(2).broadcast_to([P, 8, TOPK, TOPK]),
                                           ALU.mult))
                    own.wait()
                    own.do(v.tensor_reduce(routed[:, f, :], pick3, AX, ALU.add))
                    own.wait()
                dve.wait_ge(gate_exp, tb + 1)
                own.do(v.tensor_reduce(total, g_ap, AX, ALU.add))
                own.wait()
                own.do(v.reciprocal(total, total))
                own.wait()
                v.tensor_tensor(g_ap, g_ap, total.unsqueeze(2).broadcast_to([P, 8, TOPK]), ALU.mult)\
                    .then_inc(route_ready, 1)

            for tb in range(TB):
                route(tb)
                dve.wait_ge(route_taken, tb + 1)
                with dve.Fori(0, P // 8) as i:
                    for s in range(8):
                        tok = tb * P + s
                        dve.wait_ge(onehot_free, i * 8 + tok + 1)
                        t = bass.ds(i * 8 + s, 1)
                        v.tensor_scalar(hot2[:, s % 4, :], iota[:], turned[:, 1, t], None, ALU.is_equal)
                        v.tensor_scalar(hot1[:, s % 4, :], iota[:], turned[:, 0, t], turned[:, 2, t], ALU.is_equal,
                                        ALU.mult).then_inc(onehot_ready, 1)

            def mix(g, i0, gi, n=8):
                for s in range(i0, i0 + n):
                    p = PROD["u_first"] + g * GROUP + s
                    dve.wait_ge(bank_free, gi * 32 + 2 + p + 1)
                    slot = (g * GROUP + s) % 8
                    dve.wait_ge(gates_loaded[slot], gi * 64 + 16 * ((g * GROUP + s) // 8 + 1))
                    a = A[:, (g % 2) * GROUP + s, :]
                    v.tensor_tensor(a, a, plane(GRING + slot), ALU.mult).then_inc(mixed_ready, 1)

            def add_sums(g, half, gi):
                for d in range(4):
                    n = 4 * (2 * g + half) + d
                    dve.wait_ge(sums_ready, gi * 16 + n + 1)
                    if g:
                        dve.wait_ge(sum_bank_free, gi * 16 + n - 3)
                    a = ACC[:, 4 * half + d, :]
                    v.tensor_tensor(a, a, ps[:, 2 + d, :], ALU.add).then_inc(sum_bank_free, 1)

            dve.wait_ge(onehot_free, 4 + T)
            own.do(v.memset(ACC[:], 0.0))
            own.wait()
            mix(0, 0, 0, GROUP)
            for half in range(2):
                add_sums(0, half, 0)
                mix(1, 8 * half, 0)
            with dve.Fori(0, GROUPS // 2 - 1) as gi:
                for g in (1, 2):
                    for half in range(2):
                        add_sums(g, half, gi)
                        mix(g + 1, 8 * half, gi)
            for half in range(2):
                add_sums(GROUPS - 1, half, 0)

            for j in range(KC):
                dve.wait_ge(sum_bank_free, 4 + 8 * (GROUPS - 1) + j + 1)
                v.scalar_tensor_tensor(out=X[:, j, :], in0=ACC[:, j, :], scalar=ada_col(GATE2, j), in1=X[:, j, :],
                                       op0=ALU.mult, op1=ALU.add).then_inc(residual_ready, 1)

            ang, k, r = plane(12), plane(13), plane(SIN)
            dve.wait_ge(pos_loaded, 16)
            own.do(v.tensor_copy(ang, pos[:]))
            own.wait()
            own.do(v.tensor_scalar(ang, ang, col("inv_freq"), None, ALU.mult))
            own.wait()
            own.do(v.tensor_scalar(k, ang, 1.0 / (2.0 * np.pi), None, ALU.mult))
            own.wait()
            own.do(v.tensor_scalar(k, k, ROUND, None, ALU.add))
            own.wait()
            own.do(v.tensor_scalar(k, k, -ROUND, None, ALU.add))
            own.wait()
            for c in TWO_PI:
                own.do(v.scalar_tensor_tensor(out=ang, in0=k, scalar=-c, in1=ang, op0=ALU.mult, op1=ALU.add))
                own.wait()
            own.do(v.tensor_scalar(ang, ang, float(np.float32(3.1415925)), float(np.float32(-3.1415925)), ALU.min,
                                   ALU.max))
            own.wait()
            own.do(v.tensor_scalar(r, ang, 1.0, None, ALU.mult))
            own.do(v.scalar_tensor_tensor(out=k, in0=ang, scalar=-1.0, in1=ang, op0=ALU.mult, op1=ALU.max))
            own.wait()
            v.tensor_scalar(plane(COS), k, -1.0, float(np.pi / 2), ALU.mult, ALU.add).then_inc(rope_in, 1)
            inverse("final")
            dve.wait_ge(residual_ready, RES["peer"] + KC)
            scaled("final", lambda j: X[:, j, :], lambda j: col("final_g", j), lambda j: X[:, j, :])
            dve.wait_ge(rope_out, 1)
            own.do(v.tensor_scalar(plane(SIN), plane(SIN), col("sin_sign"), None, ALU.mult))

            inverse("cq")
            scaled("cq", lambda j: plane(j), lambda j: col("q_norm", j), lambda j: plane(CQN + j))
            inverse("ckv")
            scaled("ckv", lambda j: plane(2 + j), lambda j: col("kv_norm", j), lambda j: plane(CKN + j))

            def rope(main, swapped, n):
                a, b = A[:, main:main + n, :], A[:, swapped:swapped + n, :]
                own.wait()
                own.do(v.tensor_tensor(a, a, plane(COS).unsqueeze(1).broadcast_to([P, n, T]), ALU.mult))
                own.do(v.tensor_tensor(b, b, plane(SIN).unsqueeze(1).broadcast_to([P, n, T]), ALU.mult))
                own.wait()
                v.tensor_tensor(a, a, b, ALU.add).then_inc(rope_ready, 1)

            taken("dqkv", 5)
            rope(4, 5, 1)
            taken("uq", 15)
            rope(QR, QS, 4)

            scale = 192 ** -0.5

            def mla_shift(m):
                n, pair = divmod(m, 4)
                dve.wait_ge(scores_ready, UNITS + m + 1)
                d = ps[:, 2:4, n * P:(n + 1) * P]
                own.do(v.tensor_tensor(d, d, diag_mask[:].unsqueeze(1).broadcast_to([P, 2, P]), ALU.add))
                own.wait()
                own.do(v.tensor_reduce(sm(m, 0, 2), ps[:, 2:4, 0:(n + 1) * P], AX, ALU.max))
                own.wait()
                v.tensor_scalar(sm(m, 0, 2), sm(m, 0, 2), -scale, None, ALU.mult).then_inc(shift_ready, 1)

            def mla_probs(m):
                n, pair = divmod(m, 4)
                dve.wait_ge(exp_ready, UNITS + m + 1)
                own.do(v.reciprocal(sm(m, 12, 2), sm(m, 12, 2)))
                own.wait()
                for g in range(2):
                    a = A[:, MPROBS[m % 2] + g, 0:(n + 1) * P]
                    last = v.tensor_scalar(a, a, sm(m, 12 + g), None, ALU.mult)
                last.then_inc(probs_ready, 1)

            mla_shift(0)
            for m in range(16):
                mla_probs(m)
                if m + 1 < 16:
                    mla_shift(m + 1)

            def residual(name, stage, alpha):
                for j in range(KC):
                    taken(stage, j)
                    v.scalar_tensor_tensor(out=X[:, j, :], in0=X[:, j, :], scalar=alpha, in1=plane(TMP + j),
                                           op0=ALU.mult, op1=ALU.add).then_inc(residual_ready, 1)

            def layer_norm(name, gain):
                i = LN[name]
                dve.wait_ge(mean_ready, i + 1)
                dve.wait_ge(residual_ready, RES[AFTER[name]] + KC)
                for j in range(KC):
                    v.scalar_tensor_tensor(out=H[:, j, :], in0=ps[:, 4, :], scalar=-1.0 / D, in1=X[:, j, :],
                                           op0=ALU.mult, op1=ALU.add).then_inc(centered_ready, 1)
                inverse(name)
                dve.wait_ge(centered_ready, KC * (i + 1))
                scaled(name, lambda j: H[:, j, :], lambda j: col(gain, KC * int(name[-1]) + j), lambda j: X[:, j, :])

            def ffn_and_ple(f):
                layer_norm(f"mix{f}", "ln_mix_g")
                with dve.Fori(0, FF // 2) as i:
                    for j in range(2):
                        dve.wait_ge(bank_free, i * 4 + 2 + PROD[f"ffn_in{f}"] + 2 * j + 2)
                        v.tensor_tensor(A[:, bass.ds(i * 2 + (HF + j), 1), :], A[:, SG + j:SG + j + 1, :],
                                        A[:, UU + j:UU + j + 1, :], ALU.mult).then_inc(ff_ready, 1)
                dve.wait_ge(h_ready, HB[f"mix{f}"] + KC)
                residual(f"ffn{f}", f"ffn_down{f}", ALPHA)
                layer_norm(f"ffn{f}", "ln_ffn_g")
                for j in range(KC):
                    taken(f"ple_proj{f}", j)
                    own.do(v.tensor_tensor(plane(8 + j), plane(8 + j), plane(j), ALU.mult))
                own.wait()
                dve.wait_ge(h_ready, HB[f"ffn{f}"] + KC)
                for j in range(KC):
                    v.tensor_tensor(X[:, j, :], X[:, j, :], plane(8 + j), ALU.add).then_inc(residual_ready, 1)

            residual("mla", "w_o", ALPHA)
            ffn_and_ple(0)

            for h in range(HEADS):
                taken("hgrn_in", 8 + h)
                lf = plane(HLF + h)
                own.do(v.tensor_scalar(lf, lf, small[:, OMLB + h:OMLB + h + 1], small[:, LB + h:LB + h + 1], ALU.mult,
                                       ALU.add))
                own.do(v.tensor_scalar(plane(HK + h), plane(HK + h), small[:, OMLB + h:OMLB + h + 1], None, ALU.mult))
                own.wait()
                v.tensor_scalar(lf, lf, 2.0 ** -63, None, ALU.max).then_inc(forget_in, 1)
            for h in range(HEADS):
                dve.wait_ge(log_ready, h + 1)
                v.tensor_tensor_scan(plane(HG + h), scan_keep[:], plane(HLF + h), 0.0, ALU.mult, ALU.add)\
                    .then_inc(cum_ready, 1)
                dve.wait_ge(cum_ready, h + 1)
                g4 = plane(HG + h).rearrange("p (c t) -> p c t", c=NCH)
                if h == 0:
                    dve.wait_ge(scaled_ready, SCALED["ffn0"] + KC)
                v.tensor_tensor(H[:, h, :].rearrange("p (c t) -> p c t", c=NCH),
                                g4[:, :, CH - 1:CH].broadcast_to([P, NCH, CH]), g4, ALU.subtract)\
                    .then_inc(decay_in, 1)
            for h in range(HEADS):
                dve.wait_ge(decay_ready, 2 * h + 2)
                own.do(v.tensor_tensor(plane(HLF + h), plane(HLF + h), plane(HQ + h), ALU.mult))
                v.tensor_tensor(H[:, h, :], H[:, h, :], plane(HK + h), ALU.mult).then_inc(khat_ready, 1)

            def by_level(ap, lv):
                return ap.rearrange("p (b two m) -> p b two m", two=2, m=2 ** lv)

            def make_level(e):
                h, lv = divmod(e, LEVELS)
                dve.wait_ge(gap_exp, e + 1)
                if e >= 2:
                    last_unit = ((e - 2) // LEVELS) * (LEVELS + 1) + (e - 2) % LEVELS
                    dve.wait_ge(pair_ready, last_unit + 1)
                m, x = by_level(plane(HM + e % 2), lv), by_level(plane(HE + e % 4), lv)
                v.tensor_tensor(m[:, :, 1, :], x[:, :, 1, :], by_level(plane(HQ + h), lv)[:, :, 1, :], ALU.mult)
                v.tensor_tensor(m[:, :, 0, :], x[:, :, 0, :], by_level(plane(HK + h), lv)[:, :, 0, :], ALU.mult)\
                    .then_inc(level_ready, 1)

            def mask_pairs(u):
                h, lv = divmod(u, LEVELS + 1)
                mask = level_mask[:, lv, :] if lv < LEVELS else ident[:]
                dve.wait_ge(pair_ready, u + 1)
                if u >= 2:
                    dve.wait_ge(intra_ready, u - 1)
                v.tensor_tensor(H[:, u % 2, :].rearrange("p (b t) -> p b t", b=TB),
                                ps[:, 6 + u % 2, :].rearrange("p (b t) -> p b t", b=TB),
                                mask.unsqueeze(1).broadcast_to([P, TB, P]), ALU.mult).then_inc(masked_ready, 1)

            make_level(0)
            for u in range(HEADS * (LEVELS + 1)):
                h, lv = divmod(u, LEVELS + 1)
                if lv != LEVELS - 1 and h * LEVELS + lv + (lv < LEVELS) < HEADS * LEVELS:
                    make_level(h * LEVELS + lv + (lv < LEVELS))
                mask_pairs(u)

            ov = A[:, HO:HO + 8, :]
            for c in range(NCH):
                if c:
                    dve.wait_ge(inter_ready, c)
                    dve.wait_ge(intra_taken, HEADS)
                    o_c = ov[:, :, c * CH:(c + 1) * CH]
                    v.tensor_tensor(o_c, o_c, ps[:, 6, :].rearrange("p (h t) -> p h t", h=HEADS), ALU.add)\
                        .then_inc(inter_added, 1)
                if c < NCH - 1:
                    dve.wait_ge(delta_ready, c + 1)
                    if c:
                        dve.wait_ge(state_ready, HEADS * c)
                    for h in range(HEADS):
                        d = ps[:, 2 + h // 4, (h % 4) * P:(h % 4) * P + P]
                        if c == 0:
                            v.tensor_copy(STATE[:, h, :], d).then_inc(state_ready, 1)
                        else:
                            v.scalar_tensor_tensor(out=STATE[:, h, :], in0=STATE[:, h, :],
                                                   scalar=dec[:, h, c:c + 1], in1=d, op0=ALU.mult,
                                                   op1=ALU.add).then_inc(state_ready, 1)
            inverse("hgrn")
            dve.wait_ge(inter_added, NCH - 1)
            scaled("hgrn", lambda j: plane(HO + j), lambda j: col("out_norm", j), lambda j: plane(HO + j))
            for h in range(HEADS):
                dve.wait_ge(scaled_ready, SCALED["hgrn"] + h + 1)
                v.tensor_tensor(plane(HO + h), plane(HO + h), plane(HGT + h), ALU.mult).then_inc(gated_ready, 1)
            residual("hgrn", "hgrn_o", ALPHA)
            ffn_and_ple(1)

        @block.gpsimd
        def _(pool):
            g = nc.gpsimd
            own = Steps(pool, pool_step)

            def select(ap, op, fill, base, pattern, mult):
                own.wait()
                own.do(g.affine_select(out=ap, in_=ap, compare_op=op, fill=fill, base=base, pattern=pattern,
                                       channel_multiplier=mult))

            own.do(g.memset(eps[:, 0:1], 1e-6))
            own.do(g.memset(eps[:, 1:2], 1e-5))
            own.do(g.memset(ones[:], 1.0))
            own.do(g.memset(halves[:], 1.0))
            own.do(g.memset(ident[:], 0.0))
            own.do(g.memset(win_mask[:], 0.0))
            own.do(g.memset(diag_mask[:], 0.0))
            own.do(g.memset(level_mask[:], 0.0))
            own.do(g.memset(scan_keep[:], 1.0))
            own.wait()
            own.do(g.memset(scan_keep[:].rearrange("p (c t) -> p c t", c=NCH)[:, :, 0:1], 0.0))
            own.do(g.iota(iota[:], [[1, P]], base=0, channel_multiplier=0, allow_small_or_imprecise_dtypes=True))
            hv = halves[:].rearrange("p (c t) -> p c t", c=2)
            select(hv, ALU.is_ge, 0.0, 0, [[-64, 2], [0, 64]], 1)
            select(hv, ALU.is_ge, 0.0, 63, [[64, 2], [0, 64]], -1)
            select(ident[:], ALU.not_equal, 1.0, 0, [[-1, P]], 1)
            select(win_mask[:], ALU.is_ge, NEG, P, [[-1, 2 * P]], 1)
            select(win_mask[:], ALU.is_gt, NEG, 0, [[1, 2 * P]], -1)
            select(diag_mask[:], ALU.is_ge, NEG, 0, [[-1, P]], 1)
            for lv in range(LEVELS):
                m = 2 ** lv
                nb = P // (2 * m)
                second = level_mask[:, lv, :].rearrange("p (b two m) -> p b two m", two=2, m=m)[:, :, 1, :]
                own.wait()
                own.do(g.memset(second, 1.0))
                select(second, ALU.is_ge, 0.0, 0, [[-2 * m, nb], [0, m]], 1)
                select(second, ALU.is_ge, 0.0, m - 1, [[2 * m, nb], [0, m]], -1)
            own.wait()
            g.memset(small[:, 24:32], 0.0).then_inc(consts_ready, 1)

            pool.wait_ge(gate_stored, 16 * TB)
            for s in range(8):
                pool.dma_start(plane(GRING + s), gate_map[s]).then_inc(gates_loaded[s], 16)
            with pool.Fori(1, NKEY // 8) as i:
                for s in range(8):
                    pool.wait_ge(mixed_ready, i * 8 + s - 7)
                    pool.dma_start(A[:, GRING + s:GRING + s + 1, :], gate_map[bass.ds(i * 8 + s, 1)]
                                   .rearrange("i j t -> j i t")).then_inc(gates_loaded[s], 16)

            pool.wait_ge(residual_ready, RES["peer"] + KC)
            pool.dma_start(ACC[:, 0:2, :], ple_in[0]).then_inc(p_loaded, 16)

            pool.wait_ge(decay_ready, 2 * HEADS)
            for h in range(HEADS):
                for lv in range(LEVELS):
                    e = h * LEVELS + lv
                    if e >= 4:
                        pool.wait_ge(level_ready, e - 3)
                    m = 2 ** lv
                    gv = plane(HG + h).rearrange("p (b two m) -> p b two m", two=2, m=m)
                    xv = plane(HE + e % 4).rearrange("p (b two m) -> p b two m", two=2, m=m)
                    mid = gv[:, :, 0, m - 1:m].broadcast_to([P, T // (2 * m), m])
                    g.tensor_tensor(xv[:, :, 1, :], gv[:, :, 1, :], mid, ALU.subtract)
                    g.tensor_tensor(xv[:, :, 0, :], mid, gv[:, :, 0, :], ALU.subtract).then_inc(gap_ready, 1)
            pool.wait_ge(residual_ready, RES["hgrn"] + KC)
            pool.dma_start(ACC[:, 0:2, :], ple_in[1]).then_inc(p_loaded, 16)

        @block.sync
        def _(sp):
            sp.dma_start(par[:], params).then_inc(inputs_loaded, 16)
            sp.dma_start(X[:], x_in).then_inc(inputs_loaded, 16)
            for s in range(RING):
                sp.dma_start(ring[s][:], stream[s]).then_inc(weights_loaded[s], 16)
            sp.dma_start(pos[:], positions).then_inc(pos_loaded, 16)

            def refill(i, s):
                sp.wait_ge(tiles_started, i * RING + s - RING + 2)
                sp.dma_start(ring[s][:], stream[bass.ds(i * RING + s, 1)].rearrange("a p b n -> (a p) b n"))\
                    .then_inc(weights_loaded[s], 16)

            with sp.Fori(1, NTILES // RING) as i:
                for s in range(RING):
                    refill(i, s)
            for s in range(NTILES % RING):
                refill(NTILES // RING, s)
            for j in range(KC):
                sp.wait_ge(residual_ready, RES["ple1"] + j + 1)
                sp.dma_start(out[:, j, :], X[:, j, :]).then_inc(stored, 16)
            sp.wait_ge(stored, 16 * KC)


def blocks(w):
    w = np.asarray(w)
    k, n = w.shape
    return w.reshape(k // P, P, n // P, P).transpose(0, 2, 1, 3)


def by_output(w, pad=0):
    b = blocks(w).transpose(1, 0, 2, 3)
    if pad:
        b = np.concatenate([b, np.zeros((b.shape[0], pad, P, P), b.dtype)], axis=1)
    return b.reshape(-1, P, P)


def columns(v, n=None):
    return np.asarray(v).reshape(-1, P).T


def kernel(**inputs):
    import concourse.bacc as _bacc
    from concourse.bass_utils import run_bass_kernel_spmd as _run

    a = {k: np.asarray(v) for k, v in inputs.items()}
    parts = {}
    w_ada = by_output(a["w_ada"])
    for name, lo, n in (("shift1", 0, 8), ("scale1", 8, 8), ("ada_rest", 16, 24), ("gate2", 40, 8)):
        parts[name] = w_ada[lo * 8:(lo + n) * 8]
    w, b = a["w_in"], a["b_in"]
    pick = np.r_[0:512, 512:576, 512:576, 576:640, 576:640, 768:2304]
    parts["w_in"] = by_output(w[:, pick])
    parts["w_v"] = by_output(w[:, 640:768])
    parts["w_out"] = by_output(a["w_out"])
    parts["w_query"] = by_output(a["w_query"])
    keys = np.stack([a["peer_keys1"], a["peer_keys2"]], axis=1)
    parts["keys"] = keys.reshape(16, P, P).transpose(0, 2, 1)
    u = a["peer_u"].reshape(NKEY, P, KC, P).transpose(0, 2, 3, 1)
    v = a["peer_v"].reshape(NKEY, P, 2, 4, P).transpose(2, 0, 3, 1, 4)
    for g in range(GROUPS):
        if g == 0:
            parts["u_first"] = u[0:GROUP].reshape(-1, P, P)
        else:
            parts[f"u{g}a"] = u[g * GROUP:g * GROUP + 8].reshape(-1, P, P)
            parts[f"u{g}b"] = u[g * GROUP + 8:(g + 1) * GROUP].reshape(-1, P, P)
        for half in range(2):
            parts[f"v{g}" + "ab"[half]] = v[half, g * GROUP:(g + 1) * GROUP].reshape(-1, P, P)
    w = a["mla_w_dqkv_2"][0]
    turn = np.r_[544:576, 512:544]
    parts["dqkv"] = by_output(w[:, np.r_[0:576, 512:576, turn, turn]])
    w = a["mla_w_uq_2"][0].reshape(256, HEADS, 192)
    parts["uq"] = by_output(np.concatenate([w[:, :, 0:128].reshape(256, -1), w[:, :, 128:192].reshape(256, -1),
                                            w[:, :, np.r_[160:192, 128:160]].reshape(256, -1)], axis=1))
    w = a["mla_w_ukv_2"][0].reshape(256, HEADS, 256)
    parts["uk"] = by_output(w[:, :, 0:128].reshape(256, -1))
    parts["uv"] = by_output(w[:, :, 128:256].reshape(256, -1))
    parts["w_o"] = by_output(a["mla_w_o_2"][0])
    for i in range(2):
        w = a["ffn_w_in_2"][i].reshape(D, 2, FF, P).transpose(0, 2, 1, 3).reshape(D, -1)
        parts[f"ffn_in{i}"] = by_output(w)
        parts[f"ffn_down{i}"] = by_output(a["ffn_w_down_2"][i], pad=24 - FF)
        parts[f"ple_gate{i}"] = by_output(a["ple_w_gate_2"][i])
        parts[f"ple_proj{i}"] = by_output(a["ple_w_proj_2"][i])
    w = a["hgrn_w_in_2"][0]
    parts["hgrn_in"] = by_output(w[:, 0:2048])
    parts["hgrn_v"] = by_output(w[:, 2048:3072])
    parts["hgrn_gate"] = by_output(w[:, 3072:4096])
    parts["hgrn_o"] = by_output(a["hgrn_w_o_2"][0])
    flat = np.concatenate([parts[name] for name, n in PARTS if n])
    stream = np.ascontiguousarray(flat.reshape(NTILES, BLOCKS, P, P).transpose(0, 2, 1, 3))

    freq = (10000.0 ** (-np.arange(0, 64, 2, dtype=np.float32) / np.float32(64))).astype(np.float32)
    sign = np.repeat([-1.0, 1.0], 32)
    cols = dict(
        c=columns(a["c"]), b_ada=columns(a["b_ada"]), norm1_g=columns(a["norm1_g"]), b_in=columns(b[pick]),
        b_v=np.broadcast_to(b[640:768], (P, P)), sinks=np.broadcast_to(a["attn_sinks"][[0, 2, 1, 3, 4, 6, 5, 7]], (P, 8)),
        conv_w=columns(a["conv_w"]), attn_out_g=columns(a["attn_out_g"]), conv_out_g=columns(a["conv_out_g"]),
        b_out=columns(a["b_out"]), norm2_g=columns(a["norm2_g"]), final_g=columns(a["final_g"]),
        q_norm=columns(a["mla_q_norm_2"]), kv_norm=columns(a["mla_kv_norm_2"]), lb=columns(a["hgrn_lb_logits_2"]),
        out_norm=columns(a["hgrn_out_norm_2"]), ln_mix_g=columns(a["ln_mix_g_2"]), ln_mix_b=columns(a["ln_mix_b_2"]),
        ln_ffn_g=columns(a["ln_ffn_g_2"]), ln_ffn_b=columns(a["ln_ffn_b_2"]),
        inv_freq=np.tile(freq, 4)[:, None], sin_sign=np.tile(sign, 2)[:, None])
    arrays = {
        "stream": stream,
        "x_in": np.ascontiguousarray(a["x"][0].T.reshape(KC, P, T).transpose(1, 0, 2)),
        "params": np.ascontiguousarray(np.concatenate([cols[name] for name, _ in COLS], axis=1).astype(np.float32)),
        "positions": np.ascontiguousarray(np.broadcast_to(a["positions_2"].reshape(1, T), (P, T))),
        "ple_in": np.ascontiguousarray(a["p_2"][:, 0].transpose(0, 2, 1).reshape(2, 2, P, T).transpose(0, 2, 1, 3)),
    }
    nc = _bacc.Bacc("TRN2", target_bir_lowering=False, num_devices=1)
    args = [nc.dram_tensor(n, list(v.shape), mybir.dt.from_np(v.dtype), kind="ExternalInput").ap()
            for n, v in arrays.items()]
    out = nc.dram_tensor("out", [P, KC, T], F32, kind="ExternalOutput").ap()
    gate_map = nc.dram_tensor("gate_map", [NKEY, P, T], F32, kind="Internal").ap()
    build(nc, *args, out, gate_map)
    r = _run(nc, [arrays], core_ids=[0])
    got = np.asarray(r.results[0]["out"])
    return got.transpose(2, 1, 0).reshape(1, T, D)
```

```python
import numpy as np
import concourse.bass as bass
from concourse import mybir
from contextlib import ExitStack

F32 = mybir.dt.float32
F32R = mybir.dt.float32r
U32 = mybir.dt.uint32
I32 = mybir.dt.int32
ALU = mybir.AluOpType
ACT = mybir.ActivationFunctionType
AX = mybir.AxisListType.X

PLANES = 74
P = 128
T = 512
D = 1024
KC = D // P
TB = T // P
RING = 4
SPLIT = 2
DVE_TILES = 16
BLOCKS = 8

HEADS = 8
HD = 64
NKEY = 128
TOPK = 16
EARLY = 18
FF = 22
ALPHA = (2 * 2) ** 0.25
NEG = -1e30
LOWEST = -3e38
CH = 64
NCH = T // CH
LEVELS = 6

PARTS = [("shift1", 8), ("scale1", 8), ("w_in", 18), ("w_v", 1), ("ada_rest", 24), ("w_out", 8), ("gate2", 8), ("w_query", 16),
         ("keys", 2), ("up", NKEY), ("down", NKEY)]
PARTS += [("dqkv", 6), ("uq", 4), ("uk", 2), ("uv", 2), ("w_o", 8)]
for _i in range(2):
    if _i:
        PARTS += [("hgrn_in", 16), ("hgrn_v", 8), ("hgrn_gate", 8), ("hgrn_o", 8)]
    PARTS += [(f"ffn_in{_i}", 2 * FF), (f"ffn_down{_i}", 24), (f"ple_gate{_i}", 8), (f"ple_proj{_i}", 2)]
FIRST = {}
NTILES = 0
for _name, _n in PARTS:
    FIRST[_name] = NTILES
    NTILES += _n

PRODUCTS = [("w_in", 19), ("w_out", 8), ("w_query", 16), ("keys", 16), ("up", NKEY)]
PRODUCTS += [("dqkv", 6), ("uq", 16), ("uk", 8), ("uv", 8), ("w_o", 8), ("ffn_in0", 2 * FF), ("ffn_down0", 8),
             ("ple_gate0", 8), ("ple_proj0", 8), ("hgrn_in", 32), ("hgrn_o", 8), ("ffn_in1", 2 * FF),
             ("ffn_down1", 8), ("ple_gate1", 8), ("ple_proj1", 8)]
PROD = {}
_p = 0
for _name, _n in PRODUCTS:
    PROD[_name] = _p
    _p += _n

NORMS = [("norm1", 1, KC), ("attn", 4, 1), ("conv", 4, 1), ("norm2", 1, KC), ("final", 1, KC), ("cq", 1, 2),
         ("ckv", 1, 2), ("mix0", 1, KC), ("ffn0", 1, KC), ("hgrn", 8, 1), ("mix1", 1, KC), ("ffn1", 1, KC)]
NGROUP, NSQ = {}, {}
_g0 = _s0 = 0
for _name, _n, _k in NORMS:
    NGROUP[_name], NSQ[_name] = _g0, _s0
    _g0 += _n
    _s0 += _n * _k
NORM_SHAPE = {name: (n, k) for name, n, k in NORMS}

SPLITS = [("norm1", 8), ("mix", 8), ("norm2", 8), ("x_mla", 8), ("cq", 2), ("ckv", 2), ("o_mla", 8), ("mix0", 8),
          ("ff0", FF), ("ffn0", 8), ("p0", 2), ("x_hgrn", 8), ("o_hgrn", 8), ("mix1", 8), ("ff1", FF), ("ffn1", 8),
          ("p1", 2)]
SPL = {}
_n0 = 0
for _name, _n in SPLITS:
    SPL[_name] = _n0
    _n0 += _n

PARTS_AT = dict(mixed=(32, 36), norm1=(0, 8), mix=(0, 8), norm2=(0, 8), x_mla=(0, 8),
                cq=(32, 36), ckv=(34, 38),
                o_mla=(24, 32), mix0=(0, 8), ff0=(22, 44), ffn0=(22, 30), p0=(58, 60), x_hgrn=(0, 8),
                o_hgrn=(24, 32), mix1=(0, 8), ff1=(22, 44), ffn1=(22, 30), p1=(58, 60))
HFF = 20

COLS = [("c", 8), ("b_ada", 48), ("norm1_g", 8), ("b_in", 18), ("b_v", 128), ("sinks", 8), ("conv_w", 12),
        ("attn_out_g", 4), ("conv_out_g", 4), ("b_out", 8), ("norm2_g", 8), ("final_g", 8), ("q_norm", 2),
        ("kv_norm", 2), ("lb", 16), ("out_norm", 8), ("ln_mix_g", 16), ("ln_mix_b", 16), ("ln_ffn_g", 16),
        ("ln_ffn_b", 16), ("inv_freq", 1), ("sin_sign", 1)]
COL = {}
_c = 0
for _name, _n in COLS:
    COL[_name] = _c
    _c += _n
NCOLS = _c
ROUND = 1.5 * 2.0 ** 23
TWO_PI = (6.28125, 0.0019350051879882812, 2.0 * np.pi - 6.28125 - 0.0019350051879882812)


def build(nc, stream, x_in, params, positions, ple_in, out, gate_map, gelu_map):
    with ExitStack() as ctx:
        def sb(name, shape, dt=F32):
            return ctx.enter_context(nc.sbuf_tensor(name, shape, dt))

        def sem(name):
            return ctx.enter_context(nc.semaphore(name))

        ps = ctx.enter_context(nc.psum_tensor("ps", [P, 8, T], F32))

        ring = [sb(f"ring{i}", [P, BLOCKS, P]) for i in range(RING)]
        whi = [sb(f"whi{i}", [P, BLOCKS, P], F32R) for i in range(SPLIT)]
        wlo = [sb(f"wlo{i}", [P, BLOCKS, P], F32R) for i in range(SPLIT)]
        X = sb("X", [P, KC, T])

        def overlay(name, first, n, dt):
            with nc.sbuf_tensor(f"{name}_before", [P, first, T], dt) if first else ExitStack():
                with nc.sbuf_tensor(name, [P, n, T], dt) as t:
                    return t

        parts = {name: [overlay(f"{name}_{side}", first, n, F32R) for side, first in zip(("hi", "lo"), PARTS_AT[name])]
                 for name, n in SPLITS + [("mixed", 4)]}
        gated = overlay("gated", HFF, 2, F32)
        A = sb("A", [P, PLANES, T])
        par = sb("par", [P, NCOLS])
        ada = sb("ada", [P, 48])
        cs = sb("cs", [P, 8])
        cparts = sb("cparts", [P, 8, 2], F32R)
        ones = sb("ones", [P, P])
        halves = sb("halves", [P, P])
        ident = sb("ident", [P, P])
        iota = sb("iota", [P, P])
        win_mask = sb("win_mask", [P, 2 * P])
        diag_mask = sb("diag_mask", [P, P])
        level_mask = sb("level_mask", [P, LEVELS, P])
        scan_keep = sb("scan_keep", [P, T])
        small = sb("small", [P, 96])
        eps = sb("eps", [P, 2])
        dec = sb("dec", [P, HEADS, NCH])

        weights_loaded = [sem(f"weights_loaded{i}") for i in range(RING)]
        inputs_loaded = sem("inputs_loaded")
        pos_loaded = sem("pos_loaded")
        split_ready = sem("split_ready")
        whi_ready = sem("whi_ready")
        split_begun = sem("split_begun")
        hi_ready = sem("hi_ready")
        lo_ready = sem("lo_ready")
        tiles_started = sem("tiles_started")
        product_ready = sem("product_ready")
        bank_free = sem("bank_free")
        consts_ready = sem("consts_ready")
        pool_step = sem("pool_step")
        dve_step = sem("dve_step")
        silu_ready = sem("silu_ready")
        c_ready = sem("c_ready")
        lb_in = sem("lb_in")
        lb_exp = sem("lb_exp")
        ada_sums = sem("ada_sums")
        ada_ready = sem("ada_ready")
        sq_ready = sem("sq_ready")
        sq_used = sem("sq_used")
        root_ready = sem("root_ready")
        rstd_ready = sem("rstd_ready")
        scaled_ready = sem("scaled_ready")
        h_ready = sem("h_ready")
        residual_ready = sem("residual_ready")
        mean_ready = sem("mean_ready")
        centered_ready = sem("centered_ready")
        bias_ready = sem("bias_ready")
        scores_ready = sem("scores_ready")
        shift_ready = sem("shift_ready")
        exp_ready = sem("exp_ready")
        sink_ready = sem("sink_ready")
        probs_ready = sem("probs_ready")
        pt_ready = sem("pt_ready")
        pt_taken = sem("pt_taken")
        o_ready = sem("o_ready")
        o_taken = sem("o_taken")
        conv_ready = sem("conv_ready")
        gate_in = sem("gate_in")
        gate_exp = sem("gate_exp")
        route_ready = sem("route_ready")
        route_turned = sem("route_turned")
        route_taken = sem("route_taken")
        onehot_ready = sem("onehot_ready")
        onehot_free = sem("onehot_free")
        gate_bank_free = sem("gate_bank_free")
        gate_stored = sem("gate_stored")
        gelu_stored = [sem(f"gelu_stored{i}") for i in range(2)]
        ring_loaded = [sem(f"ring_loaded{i}") for i in range(8)]
        mixed_ready = sem("mixed_ready")
        mixed_hi = sem("mixed_hi")
        mixed_lo = sem("mixed_lo")
        sums_ready = sem("sums_ready")
        ones_ready = sem("ones_ready")
        rope_in = sem("rope_in")
        rope_out = sem("rope_out")
        rope_ready = sem("rope_ready")
        ff_ready = sem("ff_ready")
        p_loaded = sem("p_loaded")
        forget_in = sem("forget_in")
        log_ready = sem("log_ready")
        cum_ready = sem("cum_ready")
        decay_in = sem("decay_in")
        decay_ready = sem("decay_ready")
        khat_ready = sem("khat_ready")
        kt_ready = sem("kt_ready")
        kt_taken = sem("kt_taken")
        gap_ready = sem("gap_ready")
        gap_exp = sem("gap_exp")
        level_ready = sem("level_ready")
        pair_ready = sem("pair_ready")
        masked_ready = sem("masked_ready")
        intra_ready = sem("intra_ready")
        intra_taken = sem("intra_taken")
        inter_ready = sem("inter_ready")
        delta_ready = sem("delta_ready")
        inter_added = sem("inter_added")
        state_ready = sem("state_ready")
        gated_ready = sem("gated_ready")
        stored = sem("stored")
        block = ctx.enter_context(nc.Block())

        def col(name, j=0, n=1):
            return par[:, COL[name] + j:COL[name] + j + n]

        def plane(i):
            return A[:, i, :]

        class Steps:
            def __init__(self, eng, s):
                self.eng, self.sem, self.n = eng, s, 0

            def do(self, ins):
                ins.then_inc(self.sem, 1)
                self.n += 1
                return self.n

            def wait(self, n=None):
                self.eng.wait_ge(self.sem, self.n if n is None else n)

        SHIFT1, SCALE1, GATE1, SHIFT2, SCALE2, GATE2 = range(0, 48, 8)

        def ada_col(part, j=0, n=1):
            return ada[:, part + j:part + j + n]

        GS1, LB, OMLB = 0, 8, 16
        TMPH = 16
        PQ, PKD, PB_, PCG, PU, PV = 24, 28, 30, 34, 38, 42
        ATT, Z, MIX = 43, 47, 52
        PROBS, PT = (60, 62), (64, 66)
        zv = A[:, Z:Z + 5, :].rearrange("p a t -> p (a t)")[:, 0:4 * (T + 2)].rearrange("p (c t) -> p c t", c=4)
        STAGE = 16
        SCORES = 48
        GELU = 72
        UR, GR = 16, 24
        accf = A[:, 64:72, :].rearrange("p a t -> p (a t)")
        staging = A[:, STAGE:STAGE + 32, :].rearrange("p a t -> p (a t)").rearrange("p (i t) -> p i t", i=NKEY)
        turned = accf[:, 2048:2048 + 3 * P].rearrange("p (a t) -> p a t", a=3)
        hot1 = accf[:, 2560:3072].rearrange("p (s i) -> p s i", s=4)
        hot2 = accf[:, 3072:3584].rearrange("p (s i) -> p s i", s=4)
        routed = accf[:, 1664:2048].rearrange("p (a t) -> p a t", a=3)
        DOWN, COS, SIN, ANG, POS, CQN, CKN, QN, QR, QS, KN, VM, OM = 16, 64, 65, 66, 71, 27, 29, 40, 48, 52, 56, 0, 8
        MPROBS, MPT = (64, 66), (68, 70)
        TMPO, CENTER, SG, UU, TMPD, TMPG, TMPP, PRAW = 40, 56, 16, 18, 0, 40, 48, 66
        HQ, HLF, HK, HV, HGT, HG, HKH, HKT, HO, HM, HE, HMASK = 16, 24, 32, 40, 48, 56, 0, 8, 64, 72, 0, 4
        STATE = A[:, 6:8, :].rearrange("p a t -> p (a t)").rearrange("p (h e) -> p h e", h=HEADS)

        def hi(name, j):
            return parts[name][0][:, j, :]

        def lo(name, j):
            return parts[name][1][:, j, :]

        NORM = {}
        NORM.update(norm1=(68, 72), attn=(68, 16), conv=(68, 20), norm2=(68, 72), final=(68, 72),
                    cq=(68, 72), ckv=(68, 73), mix0=(68, 72), ffn0=(68, 72), hgrn=(0, 16), mix1=(68, 72),
                    ffn1=(68, 72))
        AFTER = {"mix0": "mla", "ffn0": "ffn0", "mix1": "hgrn", "ffn1": "ffn1"}
        eps_col = {1e-6: eps[:, 0:1], 1e-5: eps[:, 1:2]}

        def sm(unit, c, n=1):
            return small[:, 64 + 16 * (unit % 2) + c:64 + 16 * (unit % 2) + c + n]

        LN = {"mix0": 0, "ffn0": 1, "mix1": 2, "ffn1": 3}
        SCALED = NSQ
        RES = {"w_out": 0, "peer": 8, "mla": 16, "ffn0": 24, "ple0": 32, "hgrn": 40, "ffn1": 48, "ple1": 56}
        WIN_ORDER = (0, 2, 1, 3)
        UNITS = 8

        @block.tensor
        def _(pe):
            mm = nc.tensor.matmul

            def tile_in(tile, i=0):
                pe.wait_ge(split_ready, i + tile + 1)
                return whi[tile % SPLIT], wlo[tile % SPLIT]

            def three(out_, left, right, start, stop):
                (lh, ll), (rh, rl) = left, right
                first = mm(out_, lh, rh, start=start, stop=False)
                mm(out_, lh, rl, start=False, stop=False)
                return first, mm(out_, ll, rh, start=False, stop=stop)

            def linear(name, operand, kb=8, by_token=False, tiles=None, first=0, count=None):
                t0 = FIRST[tiles or name]
                p0 = PROD[name] + first
                pad = 8 * -(-kb // 8) if kb > 8 else kb
                n = dict(PRODUCTS)[name] if count is None else count
                body = max(SPLIT, 2 * pad // 8)
                per = body * 8 // pad

                def some(t0, p0, i, np_):
                    for q in range(np_):
                        p = p0 + q
                        pe.wait_ge(bank_free, i * per + p + 1)
                        for tb in range(TB if by_token else 1):
                            for b in range(kb):
                                s, w = divmod(q * pad + b, 8)
                                new = w == 0 and tb == 0
                                if new:
                                    tile_in(t0 + s, i * body)
                                wh, wl = (x[(t0 + s) % SPLIT][:, w, :] for x in (whi, wlo))
                                xh, xl = hi(operand, b), lo(operand, b)
                                out_ = ps[:, p % 2, :]
                                left, right = (wh, wl), (xh, xl)
                                if by_token:
                                    r = slice(tb * P, (tb + 1) * P)
                                    out_ = ps[:, p % 2, r]
                                    left, right = (xh[:, r], xl[:, r]), (wh, wl)
                                begun, last = three(out_, left, right, b == 0, b == kb - 1)
                                if new:
                                    begun.then_inc(tiles_started, 1)
                        last.then_inc(product_ready, 1)
                loops = n // per
                if loops > 1:
                    with pe.Fori(0, loops) as i:
                        some(t0, p0, i, per)
                    if n > loops * per:
                        some(t0 + loops * body, p0 + loops * per, 0, n - loops * per)
                else:
                    some(t0, p0, 0, n)

            def parts_of(name):
                pe.wait_ge(lo_ready, SPL[name] + dict(SPLITS)[name])

            def sums(name, matrix):
                n, k = NORM_SHAPE[name]
                for j in range(n * k):
                    c, g = NSQ[name] + j, NGROUP[name] + j // k
                    if j % k == 0 and g >= 2:
                        pe.wait_ge(root_ready, g - 1)
                    pe.wait_ge(sq_ready, c + 1)
                    mm(ps[:, 2 + g % 2, :], matrix[:], plane(NORM[name][0] + c % 4), start=j % k == 0,
                       stop=j % k == k - 1).then_inc(sq_used, 1)

            def mean(res):
                for j in range(KC):
                    pe.wait_ge(residual_ready, RES[res] + j + 1)
                    last = mm(ps[:, 4, :], ones[:], X[:, j, :], start=j == 0, stop=j == KC - 1)
                last.then_inc(mean_ready, 1)

            def ada_columns(tile, column, n):
                for s in range(n):
                    wh, wl = tile_in(tile + s)
                    for k in range(KC):
                        pair = ps[:, 7, 2 * (column + s):2 * (column + s) + 2]
                        begun = mm(pair, wh[:, k, :], cparts[:, k, :], start=k == 0, stop=False)
                        last = mm(pair, wl[:, k, :], cparts[:, k, :], start=False, stop=k == KC - 1)
                        if k == 0:
                            begun.then_inc(tiles_started, 1)
                    last.then_inc(ada_sums, 1)

            pe.sem_inc(onehot_free, 4)
            pe.wait_ge(c_ready, 1)
            ada_columns(FIRST["shift1"], SHIFT1, 8)
            ada_columns(FIRST["scale1"], SCALE1, 8)
            pe.wait_ge(ones_ready, 1)
            sums("norm1", ones)
            parts_of("norm1")
            linear("w_in", "norm1", count=18)
            linear("w_in", "norm1", by_token=True, tiles="w_v", first=18, count=1)
            pe.wait_ge(consts_ready, 1)


            def win_scores(u):
                n, kv = divmod(u, 2)
                if u:
                    pe.wait_ge(exp_ready, u)
                lo = P if n == 0 else 0
                for g in range(4):
                    h = kv * 4 + WIN_ORDER[g]
                    r = slice(64 * (h % 2), 64 * (h % 2) + 64)
                    last = mm(ps[:, 2 + g // 2, (g % 2) * 256 + lo:(g % 2) * 256 + 256],
                              A[r, PQ + h // 2, n * P:(n + 1) * P], A[r, PKD + kv, (n - 1) * P + lo:(n + 1) * P],
                              start=True, stop=True)
                last.then_inc(scores_ready, 1)

            pe.wait_ge(bank_free, 2 + PROD["w_in"] + 6)
            win_scores(0)
            pe.wait_ge(bias_ready, 1)
            for u in range(UNITS):
                n, kv = divmod(u, 2)
                if u + 1 < UNITS:
                    win_scores(u + 1)
                ada_columns(FIRST["ada_rest"] + 3 * u, GATE1 + 3 * u, 3)
                pe.wait_ge(probs_ready, u + 1)
                kbs = [1] if n == 0 else [0, 1]
                pv = A[:, PROBS[u % 2]:PROBS[u % 2] + 2, :].rearrange("p a (h k) -> p (a h) k", h=2)
                if u:
                    pe.wait_ge(pt_taken, u)
                for g in range(4):
                    for kb in kbs:
                        i = g * 2 + kb
                        last = nc.tensor.transpose(ps[:, 4 + i // 4, (i % 4) * P:(i % 4) * P + P],
                                                   pv[:, g, kb * P:(kb + 1) * P], ident[:])
                last.then_inc(pt_ready, 1)
                pe.wait_ge(pt_taken, u + 1)
                if u:
                    pe.wait_ge(o_taken, u)
                ptv = A[:, PT[u % 2]:PT[u % 2] + 2, :].rearrange("p a (h k) -> p (a h) k", h=4)
                for g in range(4):
                    h = WIN_ORDER[g]
                    for kb in kbs:
                        t0 = (n - 1 + kb) * P
                        last = mm(ps[64 * (h % 2):64 * (h % 2) + 64, 6, (h // 2) * P:(h // 2) * P + P],
                                  A[:, PV, t0 + kv * 64:t0 + kv * 64 + 64], ptv[:, g * 2 + kb, :],
                                  start=kb == kbs[0], stop=kb == 1)
                last.then_inc(o_ready, 1)
            sums("attn", halves)
            sums("conv", halves)
            parts_of("mix")
            linear("w_out", "mix")
            pe.wait_ge(ada_ready, 2)
            ada_columns(FIRST["gate2"], GATE2, 8)
            sums("norm2", ones)
            parts_of("norm2")
            linear("w_query", "norm2")

            for t in range(2):
                wh, wl = (x[:].bitcast(F32) for x in tile_in(FIRST["keys"] + t))
                for tb in range(TB):
                    for f in range(2):
                        p = PROD["keys"] + t * 8 + tb * 2 + f
                        pe.wait_ge(bank_free, p + 1)
                        if t == 0 and tb == 0:
                            pe.wait_ge(bank_free, 2 + PROD["w_query"] + 16)
                        for j in range(4):
                            hh = t * 8 + f * 4 + j
                            q = A[:, STAGE + hh, tb * P:(tb + 1) * P]
                            begun = mm(ps[:, p % 2, j * P:(j + 1) * P], q, wh[:, f * 4 + j, :], start=True, stop=False)
                            last = mm(ps[:, p % 2, j * P:(j + 1) * P], q, wl[:, f * 4 + j, :], start=False, stop=True)
                            if tb == 0 and f == 0 and j == 0:
                                begun.then_inc(tiles_started, 1)
                        last.then_inc(product_ready, 1)

            ps_gates = ps[:, 6:8, :].rearrange("p b (t i) -> p b t i", t=4)

            def expert_up(first, n):
                with pe.Fori(0, n // 2) as i:
                    for s in range(2):
                        t, p = FIRST["up"] + first + s, PROD["up"] + first + s
                        wh, wl = tile_in(t, i * 2)
                        pe.wait_ge(bank_free, i * 2 + p + 1)
                        for k in range(KC):
                            begun, last = three(ps[:, p % 2, :], (wh[:, k, :], wl[:, k, :]),
                                                (hi("norm2", k), lo("norm2", k)), k == 0, k == KC - 1)
                            if k == 0:
                                begun.then_inc(tiles_started, 1)
                        last.then_inc(product_ready, 1)

            for tb in range(TB):
                expert_up(tb * EARLY, EARLY)
                pe.wait_ge(route_ready, tb + 1)
                for a in range(3):
                    last = nc.tensor.transpose(ps[:, 2, a * P:(a + 1) * P], routed[:, a, :], ident[:])
                last.then_inc(route_turned, 1)
                with pe.Fori(0, P // 8) as i:
                    for s in range(8):
                        tok = tb * P + s
                        pe.wait_ge(onehot_ready, i * 8 + tok + 1)
                        if s % 4 == 0:
                            pe.wait_ge(gate_bank_free, i * 2 + tok // 4 + 1)
                        mm(ps_gates[:, s // 4, s % 4, :], hot2[:, s % 4, :], hot1[:, s % 4, :], start=True,
                           stop=True).then_inc(onehot_free, 1)

            expert_up(TB * EARLY, NKEY - TB * EARLY)

            pe.wait_ge(bank_free, 2 + PROD["up"] + NKEY)
            pe.wait_ge(gate_bank_free, 2 + P)
            pe.wait_ge(route_taken, TB)

            def expert_down(n0, i=0):
                for s in range(4):
                    n = n0 + s
                    t = FIRST["down"] + n
                    wh, wl = tile_in(t, i * 4)
                    pe.wait_ge(mixed_lo, i * 4 + n + 1)
                    for d in range(8):
                        begun, last = three(ps[:, d, :], (wh[:, d, :], wl[:, d, :]), (hi("mixed", s), lo("mixed", s)),
                                            n == 0, n == NKEY - 1)
                        if d == 0:
                            begun.then_inc(tiles_started, 1)
                        if n == NKEY - 1:
                            last.then_inc(sums_ready, 1)

            expert_down(0)
            with pe.Fori(0, NKEY // 4 - 2) as i:
                expert_down(4, i)
            expert_down(NKEY - 4)
            pe.wait_ge(residual_ready, RES["peer"] + 4)
            sums("final", ones)

            parts_of("x_mla")
            linear("dqkv", "x_mla")
            sums("cq", ones)
            sums("ckv", ones)
            parts_of("cq")
            linear("uq", "cq", kb=2)
            parts_of("ckv")
            linear("uk", "ckv", kb=2)
            linear("uv", "ckv", kb=2, by_token=True)

            def mla_scores(m):
                n, pair = divmod(m, 4)
                pe.wait_ge(exp_ready, UNITS + m)
                for g in range(2):
                    h = 2 * pair + g
                    out_ = ps[:, 2 + g, 0:(n + 1) * P]
                    mm(out_, A[:, QN + h, n * P:(n + 1) * P], A[:, KN + h, 0:(n + 1) * P], start=True, stop=False)
                    r = slice(64 * g, 64 * g + 64)
                    last = mm(out_, A[r, QR + pair, n * P:(n + 1) * P], A[r, DOWN + 4, 0:(n + 1) * P], start=False,
                              stop=True)
                last.then_inc(scores_ready, 1)

            pe.wait_ge(rope_ready, 2)
            mla_scores(0)
            for m in range(16):
                n, pair = divmod(m, 4)
                if m + 1 < 16:
                    mla_scores(m + 1)
                pe.wait_ge(probs_ready, UNITS + m + 1)
                pe.wait_ge(pt_taken, UNITS + m)
                pv = A[:, MPROBS[m % 2]:MPROBS[m % 2] + 2, :]
                for g in range(2):
                    for kb in range(n + 1):
                        last = nc.tensor.transpose(ps[:, 4 + g, kb * P:(kb + 1) * P], pv[:, g, kb * P:(kb + 1) * P],
                                                   ident[:])
                last.then_inc(pt_ready, 1)
                pe.wait_ge(pt_taken, UNITS + m + 1)
                pe.wait_ge(o_taken, UNITS + m)
                for g in range(2):
                    for kb in range(n + 1):
                        last = mm(ps[:, 6, g * P:(g + 1) * P], A[:, VM + 2 * pair + g, kb * P:(kb + 1) * P],
                                  A[:, MPT[m % 2] + g, kb * P:(kb + 1) * P], start=kb == 0, stop=kb == n)
                last.then_inc(o_ready, 1)
            parts_of("o_mla")
            linear("w_o", "o_mla")
            mean("mla")
            sums("mix0", ones)

            def ffn_and_ple(i):
                parts_of(f"mix{i}")
                linear(f"ffn_in{i}", f"mix{i}")
                parts_of(f"ff{i}")
                linear(f"ffn_down{i}", f"ff{i}", kb=FF)
                mean(f"ffn{i}")
                sums(f"ffn{i}", ones)
                parts_of(f"ffn{i}")
                linear(f"ple_gate{i}", f"ffn{i}")
                parts_of(f"p{i}")
                linear(f"ple_proj{i}", f"p{i}", kb=2)

            ffn_and_ple(0)

            parts_of("x_hgrn")
            linear("hgrn_in", "x_hgrn", count=16)
            linear("hgrn_in", "x_hgrn", by_token=True, tiles="hgrn_v", first=16, count=8)
            linear("hgrn_in", "x_hgrn", tiles="hgrn_gate", first=24, count=8)
            for h in range(HEADS):
                pe.wait_ge(khat_ready, h + 1)
                if h >= 2:
                    pe.wait_ge(kt_taken, h - 1)
                for tb in range(TB):
                    last = nc.tensor.transpose(ps[:, 2 + h % 2, tb * P:(tb + 1) * P], A[:, HKH + h, tb * P:(tb + 1) * P],
                                               ident[:])
                last.then_inc(kt_ready, 1)

            def pairs(u):
                h, lv = divmod(u, LEVELS + 1)
                if lv < LEVELS:
                    pe.wait_ge(level_ready, h * LEVELS + lv + 1)
                    k_ap = q_ap = plane(HM + (h * LEVELS + lv) % 2)
                else:
                    k_ap, q_ap = plane(HK + h), plane(HQ + h)
                if u >= 2:
                    pe.wait_ge(masked_ready, u - 1)
                for tb in range(TB):
                    r = slice(tb * P, (tb + 1) * P)
                    last = mm(ps[:, 6 + u % 2, r], k_ap[:, r], q_ap[:, r], start=True, stop=True)
                last.then_inc(pair_ready, 1)

            n_units = HEADS * (LEVELS + 1)
            pe.wait_ge(kt_taken, HEADS)
            pairs(0)
            for u in range(n_units):
                h, lv = divmod(u, LEVELS + 1)
                if u + 1 < n_units:
                    pairs(u + 1)
                pe.wait_ge(masked_ready, u + 1)
                if lv == 0 and h >= 2:
                    pe.wait_ge(intra_taken, h - 1)
                for tb in range(TB):
                    r = slice(tb * P, (tb + 1) * P)
                    last = mm(ps[:, 4 + h % 2, r], A[:, HV + h, r], A[:, HMASK + u % 2, r], start=lv == 0 and tb == 0,
                              stop=lv == LEVELS, skip_group_check=True)
                last.then_inc(intra_ready, 1)
            for c in range(NCH):
                r = slice(64 * (c % 2), 64 * (c % 2) + 64)
                w = slice((c // 2) * P, (c // 2) * P + P)
                if c < NCH - 1:
                    if c:
                        pe.wait_ge(state_ready, HEADS * c)
                    for h in range(HEADS):
                        last = mm(ps[:, 2 + h // 4, (h % 4) * P:(h % 4) * P + P], A[r, HKT + h, w], A[r, HV + h, w],
                                  start=True, stop=True)
                    last.then_inc(delta_ready, 1)
                if c:
                    if c >= 2:
                        pe.wait_ge(inter_added, c - 1)
                    pe.wait_ge(state_ready, HEADS * c)
                    for h in range(HEADS):
                        last = mm(ps[:, 6, h * CH:(h + 1) * CH], STATE[:, h, :], A[:, HLF + h, c * CH:(c + 1) * CH],
                                  start=True, stop=True)
                    last.then_inc(inter_ready, 1)
            sums("hgrn", ones)
            parts_of("o_hgrn")
            linear("hgrn_o", "o_hgrn")
            mean("hgrn")
            sums("mix1", ones)
            ffn_and_ple(1)

        @block.scalar
        def _(act):
            fn = nc.scalar.activation

            def take(name, j, out_, func=ACT.Copy, **kw):
                p = PROD[name] + j
                act.wait_ge(product_ready, p + 1)
                fn(out_, ps[:, p % 2, :], func, **kw).then_inc(bank_free, 1)

            def norm(name, src, ready, width, eps):
                n, k = NORM_SHAPE[name]

                def root(g):
                    act.wait_ge(sq_used, NSQ[name] + (g + 1) * k)
                    fn(plane(NORM[name][1] + g), ps[:, 2 + (NGROUP[name] + g) % 2, :], ACT.Sqrt, scale=1.0 / width,
                       bias=eps_col[eps]).then_inc(root_ready, 1)

                for j in range(n * k):
                    c = NSQ[name] + j
                    if c >= 4:
                        act.wait_ge(sq_used, c - 3)
                    ready(j)
                    fn(plane(NORM[name][0] + c % 4), src(j), ACT.Square).then_inc(sq_ready, 1)
                    if k == 1 and j:
                        root(j - 1)
                root(n - 1)

            def high(name, src, ready, func=ACT.Copy, **kw):
                for j in range(dict(SPLITS)[name]):
                    ready(j)
                    fn(hi(name, j), src(j), func, **{k: x(j) for k, x in kw.items()}).then_inc(hi_ready, 1)

            act.sem_inc(bank_free, 2)
            act.sem_inc(gate_bank_free, 2)
            act.wait_ge(inputs_loaded, 16 * 2)
            fn(cs[:], col("c", 0, 8), ACT.Silu).then_inc(silu_ready, 1)
            act.wait_ge(lb_in, 1)
            fn(small[:, 40:56], small[:, 40:56], ACT.Exp).then_inc(lb_exp, 1)
            act.wait_ge(ones_ready, 1)
            norm("norm1", lambda j: X[:, j, :], lambda j: None, D, 1e-6)
            act.wait_ge(ada_ready, 1)
            high("norm1", lambda j: plane(TMPH + j), lambda j: act.wait_ge(scaled_ready, SCALED["norm1"] + j + 1),
                 ACT.Identity, bias=lambda j: ada_col(SHIFT1, j))
            for j in range(18):
                take("w_in", j, plane(PQ + j), ACT.Identity, bias=col("b_in", j))
            take("w_in", 18, plane(PV))

            def attention(base, n_units, exps, turned_out, o_out):
                for u in range(n_units):
                    if u == 0:
                        exps(0)
                    b = base + u
                    act.wait_ge(pt_ready, b + 1)
                    if b - base >= 2:
                        act.wait_ge(o_ready, b - 1)
                    turned_out(u)
                    if u + 1 < n_units:
                        exps(u + 1)
                    act.wait_ge(o_ready, b + 1)
                    o_out(u)

            def win_exps(u):
                n, kv = divmod(u, 2)
                lo = P if n == 0 else 0
                act.wait_ge(shift_ready, u + 1)
                if u >= 2:
                    act.wait_ge(pt_ready, u - 1)
                pv = A[:, PROBS[u % 2]:PROBS[u % 2] + 2, :].rearrange("p a (h k) -> p (a h) k", h=2)
                fn(sm(u, 8, 4), sm(u, 4, 4), ACT.Exp).then_inc(sink_ready, 1)
                for g in range(4):
                    last = fn(pv[:, g, lo:2 * P], ps[:, 2 + g // 2, (g % 2) * 256 + lo:(g % 2) * 256 + 256], ACT.Exp,
                              bias=sm(u, g), accum_out=sm(u, 12 + g))
                last.then_inc(exp_ready, 1)

            def win_turned(u):
                kbs = [1] if u < 2 else [0, 1]
                src = ps[:, 4:6, :].rearrange("p b (h k) -> p (b h) k", h=4)
                dst = A[:, PT[u % 2]:PT[u % 2] + 2, :].rearrange("p a (h k) -> p (a h) k", h=4)
                if u < 2:
                    src = src.rearrange("p (g k) t -> p g k t", k=2)[:, :, 1, :]
                    dst = dst.rearrange("p (g k) t -> p g k t", k=2)[:, :, 1, :]
                fn(dst, src, ACT.Copy).then_inc(pt_taken, 1)

            def win_out(u):
                n, kv = divmod(u, 2)
                fn(A[:, ATT + 2 * kv:ATT + 2 * kv + 2, n * P:(n + 1) * P],
                   ps[:, 6, 0:2 * P].rearrange("p (c t) -> p c t", c=2), ACT.Copy).then_inc(o_taken, 1)

            attention(0, UNITS, win_exps, win_turned, win_out)
            norm("attn", lambda j: plane(ATT + j), lambda j: act.wait_ge(o_taken, UNITS), HD, 1e-6)
            norm("conv", lambda j: zv[:, j, 2:T + 2], lambda j: act.wait_ge(conv_ready, j + 1), HD, 1e-6)
            high("mix", lambda j: plane(MIX + j),
                 lambda j: act.wait_ge(scaled_ready, SCALED["attn" if j < 4 else "conv"] + j % 4 + 1))
            for j in range(KC):
                take("w_out", j, plane(PQ + j), ACT.Identity, bias=col("b_out", j))
            norm("norm2", lambda j: X[:, j, :], lambda j: act.wait_ge(residual_ready, RES["w_out"] + j + 1), D, 1e-6)
            act.wait_ge(ada_ready, 3)
            high("norm2", lambda j: plane(TMPH + j), lambda j: act.wait_ge(scaled_ready, SCALED["norm2"] + j + 1),
                 ACT.Identity, bias=lambda j: ada_col(SHIFT2, j))
            act.dma_start(plane(POS).bitcast(I32), positions).then_inc(pos_loaded, 16)
            for j in range(16):
                take("w_query", j, plane(STAGE + j))

            for t in range(2):
                for tb in range(TB):
                    for f in range(2):
                        take("keys", t * 8 + tb * 2 + f, plane(SCORES + 4 * tb + 2 * t + f))
            def gelu_out(n0, i=0, waits=True):
                for s in range(2):
                    n, p = n0 + s, PROD["up"] + n0 + s
                    if waits:
                        act.wait_ge(gelu_stored[s], i * 16 + 16 * (n // 2))
                    act.wait_ge(product_ready, i * 2 + p + 1)
                    fn(plane(GELU + s), ps[:, p % 2, :], ACT.Gelu).then_inc(bank_free, 1)
                    act.wait_ge(bank_free, i * 2 + 2 + p + 1)
                    act.dma_start(gelu_map[bass.ds(i * 2 + n, 1)].rearrange("i j t -> j i t"),
                                  A[:, GELU + s:GELU + s + 1, :]).then_inc(gelu_stored[s], 16)

            ps_gates = ps[:, 6:8, :].rearrange("p b (t i) -> p b i t", t=4)
            for tb in range(TB):
                if tb == 0:
                    gelu_out(0, waits=False)
                with act.Fori(tb == 0, EARLY // 2) as i:
                    gelu_out(tb * EARLY, i)
                act.wait_ge(gate_in, tb + 1)
                g_ap = routed[:, 2, :]
                fn(g_ap, g_ap, ACT.Exp).then_inc(gate_exp, 1)
                act.wait_ge(route_turned, tb + 1)
                fn(turned[:], ps[:, 2, 0:3 * P].rearrange("p (a t) -> p a t", a=3), ACT.Copy).then_inc(route_taken, 1)
                if tb == 0:
                    act.wait_ge(bank_free, 2 + PROD["keys"] + 16)
                else:
                    act.wait_ge(gate_stored, 16 * tb)
                with act.Fori(0, P // 8) as i:
                    for b in range(2):
                        act.wait_ge(onehot_free, i * 8 + 4 + tb * P + 4 * b + 4)
                        fn(staging[:, :, bass.ds(i * 8 + 4 * b, 4)], ps_gates[:, b, :, :], ACT.Copy)\
                            .then_inc(gate_bank_free, 1)
                act.wait_ge(gate_bank_free, 2 + 32 * (tb + 1))
                act.dma_start(gate_map.rearrange("i j t -> j i t")[:, :, tb * P:(tb + 1) * P], staging)\
                    .then_inc(gate_stored, 16)

            act.wait_ge(rope_in, 1)
            fn(plane(SIN), plane(SIN), ACT.Sin)
            fn(plane(COS), plane(COS), ACT.Sin).then_inc(rope_out, 1)

            def load_mixed(s, m, i=0):
                for planes, source in ((UR, gelu_map), (GR, gate_map)):
                    act.dma_start(A[:, planes + s:planes + s + 1, :], source[bass.ds(i * 8 + m, 1)]
                                  .rearrange("i j t -> j i t")).then_inc(ring_loaded[s], 16)

            def high_mixed(n, i=0, load=True):
                act.wait_ge(mixed_ready, i * 8 + n + 1)
                if n >= 4:
                    act.wait_ge(tiles_started, i * 8 + FIRST["down"] + n - 2)
                fn(hi("mixed", n % 4), plane(UR + n % 8), ACT.Copy).then_inc(mixed_hi, 1)
                if load and n >= 4:
                    act.wait_ge(mixed_lo, i * 8 + n - 3)
                    load_mixed((n + 4) % 8, n + 4, i)

            last = NKEY - 8
            with act.Fori(0, (last - TB * EARLY) // 2) as i:
                gelu_out(TB * EARLY, i)
            act.wait_ge(gate_stored, 16 * TB)
            for s in range(8):
                load_mixed(s, s)
            gelu_out(last)
            gelu_out(last + 2)
            for n in range(4):
                high_mixed(n)
            gelu_out(last + 4)
            gelu_out(last + 6)
            for s in range(2):
                act.wait_ge(gelu_stored[s], 16 * NKEY // 2)
            for n in range(4, 8):
                high_mixed(n)
            with act.Fori(0, NKEY // 8 - 2) as i:
                for n in range(8, 16):
                    high_mixed(n, i)
            for n in range(last, NKEY):
                high_mixed(n, load=n + 4 < NKEY)
            norm("final", lambda j: X[:, j, :], lambda j: act.wait_ge(residual_ready, RES["peer"] + j + 1), D, 1e-6)

            high("x_mla", lambda j: X[:, j, :], lambda j: act.wait_ge(scaled_ready, SCALED["final"] + j + 1))
            for j in range(6):
                take("dqkv", j, plane(DOWN + j))
            norm("cq", lambda j: plane(DOWN + j), lambda j: act.wait_ge(bank_free, 2 + PROD["dqkv"] + j + 1), 256, 1e-6)
            norm("ckv", lambda j: plane(DOWN + 2 + j), lambda j: act.wait_ge(bank_free, 2 + PROD["dqkv"] + 2 + j + 1), 256,
                 1e-6)
            high("cq", lambda j: plane(CQN + j), lambda j: act.wait_ge(scaled_ready, SCALED["cq"] + j + 1))
            high("ckv", lambda j: plane(CKN + j), lambda j: act.wait_ge(scaled_ready, SCALED["ckv"] + j + 1))
            for j in range(16):
                take("uq", j, plane(QN + j))
            for j in range(8):
                take("uk", j, plane(KN + j))
            for j in range(8):
                take("uv", j, plane(VM + j))

            scale = 192 ** -0.5

            def mla_exps(m):
                n, pair = divmod(m, 4)
                act.wait_ge(shift_ready, UNITS + m + 1)
                if m >= 2:
                    act.wait_ge(pt_ready, UNITS + m - 1)
                for g in range(2):
                    last = fn(A[:, MPROBS[m % 2] + g, 0:(n + 1) * P], ps[:, 2 + g, 0:(n + 1) * P], ACT.Exp,
                              bias=sm(m, g), scale=scale, accum_out=sm(m, 12 + g))
                last.then_inc(exp_ready, 1)

            def mla_turned(m):
                w = (m // 4 + 1) * P
                fn(A[:, MPT[m % 2]:MPT[m % 2] + 2, 0:w], ps[:, 4:6, 0:w], ACT.Copy).then_inc(pt_taken, 1)

            def mla_out(m):
                n, pair = divmod(m, 4)
                fn(A[:, OM + 2 * pair:OM + 2 * pair + 2, n * P:(n + 1) * P],
                   ps[:, 6, 0:2 * P].rearrange("p (c t) -> p c t", c=2), ACT.Copy).then_inc(o_taken, 1)

            attention(UNITS, 16, mla_exps, mla_turned, mla_out)
            high("o_mla", lambda j: plane(OM + j), lambda j: act.wait_ge(o_taken, UNITS + 16))
            for j in range(KC):
                take("w_o", j, plane(TMPO + j))

            def layer_norm(name, g, b):
                i = LN[name]
                norm(name, lambda j: plane(CENTER + j), lambda j: act.wait_ge(centered_ready, KC * i + j + 1), D, 1e-5)
                for j in range(KC):
                    act.wait_ge(scaled_ready, SCALED[name] + j + 1)
                    fn(X[:, j, :], X[:, j, :], ACT.Identity, bias=col(b, KC * int(name[-1]) + j)).then_inc(h_ready, 1)
                high(name, lambda j: X[:, j, :], lambda j: act.wait_ge(h_ready, KC * i + j + 1))

            def ffn_and_ple(f):
                act.wait_ge(residual_ready, RES[AFTER[f"mix{f}"]] + KC)
                act.dma_start(A[:, PRAW:PRAW + 2, :], ple_in[f]).then_inc(p_loaded, 16)
                layer_norm(f"mix{f}", "ln_mix_g", "ln_mix_b")
                with act.Fori(0, FF // 2) as i:
                    for j in range(2):
                        p = PROD[f"ffn_in{f}"] + 2 * j
                        act.wait_ge(product_ready, i * 4 + p + 1)
                        fn(plane(SG + j), ps[:, p % 2, :], ACT.Silu).then_inc(bank_free, 1)
                        act.wait_ge(product_ready, i * 4 + p + 2)
                        fn(plane(UU + j), ps[:, (p + 1) % 2, :], ACT.Copy).then_inc(bank_free, 1)
                        act.wait_ge(ff_ready, i * 2 + FF * f + j + 1)
                        fn(parts[f"ff{f}"][0][:, bass.ds(i * 2 + j, 1), :], gated[:, j:j + 1, :], ACT.Copy)\
                            .then_inc(hi_ready, 1)
                for j in range(KC):
                    take(f"ffn_down{f}", j, plane(TMPD + j))
                layer_norm(f"ffn{f}", "ln_ffn_g", "ln_ffn_b")
                high(f"p{f}", lambda j: plane(PRAW + j), lambda j: act.wait_ge(p_loaded, 16 * (f + 1)))
                for j in range(KC):
                    take(f"ple_gate{f}", j, plane(TMPG + j), ACT.Sigmoid)
                for j in range(KC):
                    take(f"ple_proj{f}", j, plane(TMPP + j))

            ffn_and_ple(0)

            high("x_hgrn", lambda j: X[:, j, :], lambda j: act.wait_ge(residual_ready, RES["ple0"] + j + 1))
            for j in range(8):
                take("hgrn_in", j, plane(HQ + j), ACT.Silu)
            for j in range(8):
                p = PROD["hgrn_in"] + 8 + j
                act.wait_ge(product_ready, p + 1)
                fn(plane(HLF + j), ps[:, p % 2, :], ACT.Sigmoid)
                fn(plane(HK + j), ps[:, p % 2, :], ACT.Sigmoid, scale=-1.0).then_inc(bank_free, 1)
            for j in range(8):
                take("hgrn_in", 16 + j, plane(HV + j))
            for j in range(8):
                take("hgrn_in", 24 + j, plane(HGT + j), ACT.Silu)
            for h in range(HEADS):
                act.wait_ge(forget_in, h + 1)
                fn(plane(HLF + h), plane(HLF + h), ACT.Ln).then_inc(log_ready, 1)
            for h in range(HEADS):
                act.wait_ge(cum_ready, h + 1)
                fn(plane(HLF + h), plane(HG + h), ACT.Exp).then_inc(decay_ready, 1)
                act.wait_ge(decay_in, h + 1)
                fn(plane(HKH + h), plane(HKH + h), ACT.Exp).then_inc(decay_ready, 1)
            ends = A[:, HG:HG + 8, :].rearrange("p h (c t) -> p h c t", c=NCH)[:, :, :, CH - 1]
            fn(dec[:], ends, ACT.Exp).then_inc(decay_ready, 1)
            for h in range(HEADS):
                act.wait_ge(kt_ready, h + 1)
                fn(plane(HKT + h), ps[:, 2 + h % 2, :], ACT.Copy).then_inc(kt_taken, 1)
            for h in range(HEADS):
                for lv in range(LEVELS):
                    e = h * LEVELS + lv
                    act.wait_ge(gap_ready, e + 1)
                    fn(plane(HE + e % 4), plane(HE + e % 4), ACT.Exp).then_inc(gap_exp, 1)
                if h:
                    act.wait_ge(intra_ready, (LEVELS + 1) * h)
                    fn(plane(HO + h - 1), ps[:, 4 + (h - 1) % 2, :], ACT.Copy).then_inc(intra_taken, 1)
            act.wait_ge(intra_ready, (LEVELS + 1) * HEADS)
            fn(plane(HO + HEADS - 1), ps[:, 4 + (HEADS - 1) % 2, :], ACT.Copy).then_inc(intra_taken, 1)
            norm("hgrn", lambda j: plane(HO + j), lambda j: act.wait_ge(inter_added, NCH - 1), P, 1e-6)
            high("o_hgrn", lambda j: plane(HO + j), lambda j: act.wait_ge(gated_ready, j + 1))
            for j in range(KC):
                take("hgrn_o", j, plane(TMPO + j))
            ffn_and_ple(1)

        @block.vector
        def _(dve):
            v = nc.vector
            own = Steps(dve, dve_step)

            def taken(name, j):
                dve.wait_ge(bank_free, 2 + PROD[name] + j + 1)

            def inverse(name):
                for g in range(NORM_SHAPE[name][0]):
                    dve.wait_ge(root_ready, NGROUP[name] + g + 1)
                    r = plane(NORM[name][1] + g)
                    v.reciprocal(r, r).then_inc(rstd_ready, 1)

            def scaled(name, src, gain, dst):
                n, k = NORM_SHAPE[name]
                for j in range(n * k):
                    dve.wait_ge(rstd_ready, NGROUP[name] + j // k + 1)
                    v.scalar_tensor_tensor(out=dst(j), in0=src(j), scalar=gain(j), in1=plane(NORM[name][1] + j // k),
                                           op0=ALU.mult, op1=ALU.mult).then_inc(scaled_ready, 1)

            def low(name, src, shift=None):
                for j in range(dict(SPLITS)[name]):
                    dve.wait_ge(hi_ready, SPL[name] + j + 1)
                    h = hi(name, j).bitcast(F32)
                    if shift is None:
                        last = v.tensor_tensor(lo(name, j), src(j), h, ALU.subtract)
                    else:
                        last = v.scalar_tensor_tensor(out=lo(name, j), in0=src(j), scalar=shift(j), in1=h, op0=ALU.add,
                                                      op1=ALU.subtract)
                    last.then_inc(lo_ready, 1)

            own.do(v.memset(eps[:, 0:1], 1e-6))
            own.do(v.memset(eps[:, 1:2], 1e-5))
            own.do(v.memset(ones[:], 1.0))
            own.wait()
            dve.sem_inc(ones_ready, 1)
            dve.wait_ge(silu_ready, 1)
            own.do(v.tensor_copy(cparts[:, :, 0], cs[:]))
            own.wait()
            v.tensor_tensor(cparts[:, :, 1], cs[:], cparts[:, :, 0].bitcast(F32), ALU.subtract).then_inc(c_ready, 1)

            for n in range(DVE_TILES):
                dve.wait_ge(weights_loaded[n % RING], 16 * (n // RING + 1))
                if n >= SPLIT:
                    dve.wait_ge(tiles_started, n - SPLIT + 2)
                raw, h = ring[n % RING], whi[n % SPLIT]
                v.tensor_copy(h[:], raw[:]).then_inc(whi_ready, 1)
                dve.wait_ge(whi_ready, n + 1)
                v.tensor_tensor(wlo[n % SPLIT][:], raw[:], h[:].bitcast(F32), ALU.subtract).then_inc(split_ready, 1)
            dve.wait_ge(inputs_loaded, 16 * 2)

            lb0, lb1 = col("lb", 0, 8), col("lb", 8, 8)
            t0, t1, t2 = small[:, 32:40], small[:, 40:48], small[:, 48:56]
            own.do(v.tensor_tensor(t0, lb0, lb1, ALU.max))
            own.wait()
            own.do(v.tensor_tensor(t1, lb0, t0, ALU.subtract))
            v.tensor_tensor(t2, lb1, t0, ALU.subtract).then_inc(lb_in, 1)
            own.wait()
            dve.wait_ge(lb_exp, 1)
            own.do(v.tensor_tensor(t0, t1, t2, ALU.add))
            own.wait()
            own.do(v.reciprocal(t0, t0))
            own.wait()
            own.do(v.tensor_tensor(t1, t1, t0, ALU.mult))
            own.do(v.tensor_tensor(t2, t2, t0, ALU.mult))
            own.wait()
            own.do(v.tensor_tensor(t2, t1, t2, ALU.add))
            own.wait()
            own.do(v.tensor_tensor(small[:, LB:LB + 8], t2, t1, ALU.subtract))
            own.wait()
            own.do(v.tensor_scalar(small[:, OMLB:OMLB + 8], small[:, LB:LB + 8], -1.0, 1.0, ALU.mult, ALU.add))

            def ada_part(part, n, at):
                dve.wait_ge(ada_sums, part + n)
                pairs = ps[:, 7, 2 * part:2 * (part + n)].rearrange("p (n two) -> p n two", two=2)
                own.do(v.tensor_reduce(ada_col(part, 0, n), pairs, AX, ALU.add))
                own.wait()
                v.tensor_tensor(ada_col(part, 0, n), ada_col(part, 0, n), col("b_ada", part, n), ALU.add)\
                    .then_inc(ada_ready, 1)

            def modulation(part, at, gain):
                dve.wait_ge(ada_ready, at)
                own.do(v.scalar_tensor_tensor(out=small[:, GS1:GS1 + 8], in0=ada_col(part, 0, 8), scalar=1.0,
                                              in1=col(gain, 0, 8), op0=ALU.add, op1=ALU.mult))
                own.wait()

            ada_part(0, 16, 1)
            modulation(SCALE1, 1, "norm1_g")
            inverse("norm1")
            scaled("norm1", lambda j: X[:, j, :], lambda j: small[:, GS1 + j:GS1 + j + 1],
                   lambda j: plane(TMPH + j))
            dve.wait_ge(scaled_ready, SCALED["norm1"] + KC)
            low("norm1", lambda j: plane(TMPH + j), lambda j: ada_col(SHIFT1, j))

            taken("w_in", 18)
            pv3 = plane(PV).rearrange("p (b c) -> p b c", b=TB)
            v.tensor_tensor(pv3, pv3, col("b_v", 0, P).unsqueeze(1).broadcast_to([P, TB, P]), ALU.add)\
                .then_inc(bias_ready, 1)
            dve.wait_ge(consts_ready, 1)

            def win_shift(u):
                n, kv = divmod(u, 2)
                lo = P if n == 0 else 0
                dve.wait_ge(scores_ready, u + 1)
                s = ps[:, 2:4, :].rearrange("p b (h k) -> p (b h) k", h=2)[:, :, lo:2 * P]
                own.do(v.scalar_tensor_tensor(out=s, in0=s, scalar=HD ** -0.5,
                                              in1=win_mask[:, lo:2 * P].unsqueeze(1).broadcast_to([P, 4, 2 * P - lo]),
                                              op0=ALU.mult, op1=ALU.add))
                own.wait()
                own.do(v.tensor_reduce(sm(u, 0, 4), s, AX, ALU.max))
                own.wait()
                own.do(v.tensor_tensor(sm(u, 0, 4), sm(u, 0, 4), col("sinks", 4 * kv, 4), ALU.max))
                own.wait()
                own.do(v.tensor_tensor(sm(u, 4, 4), col("sinks", 4 * kv, 4), sm(u, 0, 4), ALU.subtract))
                v.tensor_scalar(sm(u, 0, 4), sm(u, 0, 4), -1.0, None, ALU.mult).then_inc(shift_ready, 1)

            def win_probs(u):
                n, kv = divmod(u, 2)
                lo = P if n == 0 else 0
                dve.wait_ge(exp_ready, u + 1)
                own.do(v.tensor_tensor(sm(u, 12, 4), sm(u, 12, 4), sm(u, 8, 4), ALU.add))
                own.wait()
                own.do(v.reciprocal(sm(u, 12, 4), sm(u, 12, 4)))
                own.wait()
                pv = A[:, PROBS[u % 2]:PROBS[u % 2] + 2, :].rearrange("p a (h k) -> p (a h) k", h=2)[:, :, lo:2 * P]
                v.tensor_tensor(pv, pv, sm(u, 12, 4).unsqueeze(2).broadcast_to([P, 4, 2 * P - lo]), ALU.mult)\
                    .then_inc(probs_ready, 1)

            win_shift(0)
            for u in range(UNITS):
                win_probs(u)
                if u + 1 < UNITS:
                    win_shift(u + 1)
                if u == 0:
                    own.do(v.memset(zv[:, :, 0:2], 0.0))
                    own.do(v.tensor_tensor(zv[:, :, 2:T + 2], A[:, PCG:PCG + 4, :], A[:, PU:PU + 4, :], ALU.mult))
                    z_step = own.n
                if 1 <= u <= 4:
                    j = u - 1
                    own.wait(z_step)
                    cp = plane(PU + j)
                    own.do(v.tensor_scalar(cp, zv[:, j, 2:T + 2], col("conv_w", 8 + j), None, ALU.mult))
                    own.wait()
                    own.do(v.scalar_tensor_tensor(out=cp, in0=zv[:, j, 1:T + 1], scalar=col("conv_w", 4 + j), in1=cp,
                                                  op0=ALU.mult, op1=ALU.add))
                    own.wait()
                    own.do(v.scalar_tensor_tensor(out=cp, in0=zv[:, j, 0:T], scalar=col("conv_w", j), in1=cp,
                                                  op0=ALU.mult, op1=ALU.add))
                    own.wait()
                    v.tensor_tensor(zv[:, j, 2:T + 2], cp, plane(PB_ + j), ALU.mult).then_inc(conv_ready, 1)
            inverse("attn")
            scaled("attn", lambda j: plane(ATT + j), lambda j: col("attn_out_g", j), lambda j: plane(MIX + j))
            inverse("conv")
            scaled("conv", lambda j: zv[:, j, 2:T + 2], lambda j: col("conv_out_g", j), lambda j: plane(MIX + 4 + j))
            dve.wait_ge(scaled_ready, SCALED["conv"] + 4)
            low("mix", lambda j: plane(MIX + j))
            ada_part(16, 24, 2)
            dve.wait_ge(ada_ready, 2)

            for j in range(KC):
                taken("w_out", j)
                v.scalar_tensor_tensor(out=X[:, j, :], in0=plane(PQ + j), scalar=ada_col(GATE1, j), in1=X[:, j, :],
                                       op0=ALU.mult, op1=ALU.add).then_inc(residual_ready, 1)
            ada_part(40, 8, 3)
            modulation(SCALE2, 3, "norm2_g")
            inverse("norm2")
            dve.wait_ge(residual_ready, RES["w_out"] + KC)
            scaled("norm2", lambda j: X[:, j, :], lambda j: small[:, GS1 + j:GS1 + j + 1],
                   lambda j: plane(TMPH + j))
            dve.wait_ge(scaled_ready, SCALED["norm2"] + KC)
            low("norm2", lambda j: plane(TMPH + j), lambda j: ada_col(SHIFT2, j))

            best = accf[:, 0:256].rearrange("p (h k) -> p h k", h=16)
            best_at = accf[:, 256:512].rearrange("p (h k) -> p h k", h=16)
            best_i = best_at.bitcast(U32)
            best_f = accf[:, 512:768].rearrange("p (h k) -> p h k", h=16)
            top = accf[:, 768:896].rearrange("p (h k) -> p h k", h=8)
            top_i = accf[:, 896:1024].bitcast(U32)
            hi_i = accf[:, 1024:1152].bitcast(U32)
            lo_i = accf[:, 1152:1280].bitcast(U32)
            place1 = accf[:, 1280:1408]
            place2 = accf[:, 1408:1536]
            total = accf[:, 1536:1544]

            def route(tb):
                four = A[:, SCORES + 4 * tb:SCORES + 4 * tb + 4, :].rearrange("p a t -> p (a t)")
                s = four.rearrange("p (h n) -> p h n", h=16)
                taken("keys", 8 + tb * 2 + 1)
                for h in range(16):
                    own.do(v.max(best[:, h, 0:8], s[:, h, :]))
                own.wait()
                for h in range(16):
                    own.do(v.max_index(best_i[:, h, 0:8], best[:, h, 0:8], s[:, h, :]))
                own.wait()
                for h in range(16):
                    own.do(v.match_replace(out=s[:, h, :], in_to_replace=best[:, h, 0:8], in_values=s[:, h, :],
                                           imm_value=LOWEST))
                own.wait()
                for h in range(16):
                    own.do(v.max(best[:, h, 8:16], s[:, h, :]))
                own.wait()
                for h in range(16):
                    own.do(v.max_index(best_i[:, h, 8:16], best[:, h, 8:16], s[:, h, :]))
                own.wait()
                own.do(v.tensor_copy(best_f, best_i))
                pair = best.rearrange("p (h f) k -> p h f k", f=2)
                cand4 = four.rearrange("p (h a b) -> p h a b", h=8, a=TOPK)
                cand = four.rearrange("p (h n) -> p h n", h=8)
                for h in range(8):
                    own.do(v.tensor_tensor(cand4[:, h], pair[:, h, 0, :].unsqueeze(2).broadcast_to([P, TOPK, TOPK]),
                                           pair[:, h, 1, :].unsqueeze(1).broadcast_to([P, TOPK, TOPK]), ALU.add))
                own.wait()
                top_iv = top_i.rearrange("p (h k) -> p h k", h=8)
                for h in range(8):
                    own.do(v.max(top[:, h, 0:8], cand[:, h, :]))
                own.wait()
                for h in range(8):
                    own.do(v.max_index(top_iv[:, h, 0:8], top[:, h, 0:8], cand[:, h, :]))
                own.wait()
                for h in range(8):
                    own.do(v.match_replace(out=cand[:, h, :], in_to_replace=top[:, h, 0:8], in_values=cand[:, h, :],
                                           imm_value=LOWEST))
                own.wait()
                for h in range(8):
                    own.do(v.max(top[:, h, 8:16], cand[:, h, :]))
                own.wait()
                for h in range(8):
                    own.do(v.max_index(top_iv[:, h, 8:16], top[:, h, 8:16], cand[:, h, :]))
                g_ap = routed[:, 2, :].rearrange("p (h k) -> p h k", h=8)
                if tb:
                    dve.wait_ge(route_turned, tb)
                v.tensor_tensor(g_ap, top, top[:, :, 0:1].broadcast_to([P, 8, TOPK]), ALU.subtract)\
                    .then_inc(gate_in, 1)
                own.wait()
                own.do(v.tensor_scalar(hi_i, top_i, 4, None, ALU.logical_shift_right))
                own.do(v.tensor_scalar(lo_i, top_i, 15, None, ALU.bitwise_and))
                own.wait()
                own.do(v.tensor_copy(place1, hi_i))
                own.do(v.tensor_copy(place2, lo_i))
                own.wait()
                pick = four.rearrange("p (h k a) -> p h k a", h=8, k=TOPK)
                pick3 = four.rearrange("p (q a) -> p q a", a=TOPK)
                bf = best_f.rearrange("p (h f) k -> p h f k", f=2)
                for f, place in enumerate((place1, place2)):
                    own.do(v.tensor_tensor(pick3, place.unsqueeze(2).broadcast_to([P, P, TOPK]),
                                           iota[:, 0:TOPK].unsqueeze(1).broadcast_to([P, P, TOPK]), ALU.is_equal))
                    own.wait()
                    own.do(v.tensor_tensor(pick, pick, bf[:, :, f, :].unsqueeze(2).broadcast_to([P, 8, TOPK, TOPK]),
                                           ALU.mult))
                    own.wait()
                    own.do(v.tensor_reduce(routed[:, f, :], pick3, AX, ALU.add))
                    own.wait()
                dve.wait_ge(gate_exp, tb + 1)
                own.do(v.tensor_reduce(total, g_ap, AX, ALU.add))
                own.wait()
                own.do(v.reciprocal(total, total))
                own.wait()
                v.tensor_tensor(g_ap, g_ap, total.unsqueeze(2).broadcast_to([P, 8, TOPK]), ALU.mult)\
                    .then_inc(route_ready, 1)

            for tb in range(TB):
                route(tb)
                dve.wait_ge(route_taken, tb + 1)
                with dve.Fori(0, P // 8) as i:
                    for s in range(8):
                        tok = tb * P + s
                        dve.wait_ge(onehot_free, i * 8 + tok + 1)
                        t = bass.ds(i * 8 + s, 1)
                        v.tensor_scalar(hot2[:, s % 4, :], iota[:], turned[:, 1, t], None, ALU.is_equal)
                        v.tensor_scalar(hot1[:, s % 4, :], iota[:], turned[:, 0, t], turned[:, 2, t], ALU.is_equal,
                                        ALU.mult).then_inc(onehot_ready, 1)

            ang, k, r = plane(ANG), plane(ANG + 1), plane(SIN)
            dve.wait_ge(pos_loaded, 16)
            own.do(v.tensor_copy(ang, plane(POS).bitcast(I32)))
            own.wait()
            own.do(v.tensor_scalar(ang, ang, col("inv_freq"), None, ALU.mult))
            own.wait()
            own.do(v.tensor_scalar(k, ang, 1.0 / (2.0 * np.pi), None, ALU.mult))
            own.wait()
            own.do(v.tensor_scalar(k, k, ROUND, None, ALU.add))
            own.wait()
            own.do(v.tensor_scalar(k, k, -ROUND, None, ALU.add))
            own.wait()
            for c in TWO_PI:
                own.do(v.scalar_tensor_tensor(out=ang, in0=k, scalar=-c, in1=ang, op0=ALU.mult, op1=ALU.add))
                own.wait()
            own.do(v.tensor_scalar(ang, ang, float(np.float32(3.1415925)), float(np.float32(-3.1415925)), ALU.min,
                                   ALU.max))
            own.wait()
            own.do(v.tensor_scalar(r, ang, 1.0, None, ALU.mult))
            own.do(v.scalar_tensor_tensor(out=k, in0=ang, scalar=-1.0, in1=ang, op0=ALU.mult, op1=ALU.max))
            own.wait()
            v.tensor_scalar(plane(COS), k, -1.0, float(np.pi / 2), ALU.mult, ALU.add).then_inc(rope_in, 1)
            dve.wait_ge(rope_out, 1)
            own.do(v.tensor_scalar(plane(SIN), plane(SIN), col("sin_sign"), None, ALU.mult))

            def mix(n, i=0):
                dve.wait_ge(ring_loaded[n % 8], i * 32 + 32 * (n // 8 + 1))
                a = plane(UR + n % 8)
                v.tensor_tensor(a, a, plane(GR + n % 8), ALU.mult).then_inc(mixed_ready, 1)

            def low_mixed(n, i=0):
                dve.wait_ge(mixed_hi, i * 8 + n + 1)
                v.tensor_tensor(lo("mixed", n % 4), plane(UR + n % 8), hi("mixed", n % 4).bitcast(F32), ALU.subtract)\
                    .then_inc(mixed_lo, 1)

            mix(0)
            with dve.Fori(0, NKEY // 8 - 1) as i:
                for n in range(8):
                    mix(n + 1, i)
                    low_mixed(n, i)
            for n in range(NKEY - 8, NKEY):
                if n + 1 < NKEY:
                    mix(n + 1)
                low_mixed(n)
            for j in range(KC):
                dve.wait_ge(sums_ready, j + 1)
                v.scalar_tensor_tensor(out=X[:, j, :], in0=ps[:, j, :], scalar=ada_col(GATE2, j), in1=X[:, j, :],
                                       op0=ALU.mult, op1=ALU.add).then_inc(residual_ready, 1)

            inverse("final")
            dve.wait_ge(residual_ready, RES["peer"] + KC)
            scaled("final", lambda j: X[:, j, :], lambda j: col("final_g", j), lambda j: X[:, j, :])
            dve.wait_ge(scaled_ready, SCALED["final"] + KC)
            low("x_mla", lambda j: X[:, j, :])

            inverse("cq")
            scaled("cq", lambda j: plane(DOWN + j), lambda j: col("q_norm", j), lambda j: plane(CQN + j))
            inverse("ckv")
            scaled("ckv", lambda j: plane(DOWN + 2 + j), lambda j: col("kv_norm", j),
                   lambda j: plane(CKN + j))
            dve.wait_ge(scaled_ready, SCALED["ckv"] + 2)
            low("cq", lambda j: plane(CQN + j))
            low("ckv", lambda j: plane(CKN + j))

            def rope(main, swapped, n):
                a, b = A[:, main:main + n, :], A[:, swapped:swapped + n, :]
                own.wait()
                own.do(v.tensor_tensor(a, a, plane(COS).unsqueeze(1).broadcast_to([P, n, T]), ALU.mult))
                own.do(v.tensor_tensor(b, b, plane(SIN).unsqueeze(1).broadcast_to([P, n, T]), ALU.mult))
                own.wait()
                v.tensor_tensor(a, a, b, ALU.add).then_inc(rope_ready, 1)

            taken("dqkv", 5)
            rope(DOWN + 4, DOWN + 5, 1)
            taken("uq", 15)
            rope(QR, QS, 4)

            scale = 192 ** -0.5

            def mla_shift(m):
                n, pair = divmod(m, 4)
                dve.wait_ge(scores_ready, UNITS + m + 1)
                d = ps[:, 2:4, n * P:(n + 1) * P]
                own.do(v.tensor_tensor(d, d, diag_mask[:].unsqueeze(1).broadcast_to([P, 2, P]), ALU.add))
                own.wait()
                own.do(v.tensor_reduce(sm(m, 0, 2), ps[:, 2:4, 0:(n + 1) * P], AX, ALU.max))
                own.wait()
                v.tensor_scalar(sm(m, 0, 2), sm(m, 0, 2), -scale, None, ALU.mult).then_inc(shift_ready, 1)

            def mla_probs(m):
                n, pair = divmod(m, 4)
                dve.wait_ge(exp_ready, UNITS + m + 1)
                own.do(v.reciprocal(sm(m, 12, 2), sm(m, 12, 2)))
                own.wait()
                for g in range(2):
                    a = A[:, MPROBS[m % 2] + g, 0:(n + 1) * P]
                    last = v.tensor_scalar(a, a, sm(m, 12 + g), None, ALU.mult)
                last.then_inc(probs_ready, 1)

            mla_shift(0)
            for m in range(16):
                mla_probs(m)
                if m + 1 < 16:
                    mla_shift(m + 1)

            low("o_mla", lambda j: plane(OM + j))

            def residual(stage, tmp):
                for j in range(KC):
                    taken(stage, j)
                    v.scalar_tensor_tensor(out=X[:, j, :], in0=X[:, j, :], scalar=ALPHA, in1=plane(tmp + j),
                                           op0=ALU.mult, op1=ALU.add).then_inc(residual_ready, 1)

            def layer_norm(name, gain):
                i = LN[name]
                dve.wait_ge(mean_ready, i + 1)
                dve.wait_ge(residual_ready, RES[AFTER[name]] + KC)
                for j in range(KC):
                    v.scalar_tensor_tensor(out=plane(CENTER + j), in0=ps[:, 4, :], scalar=-1.0 / D, in1=X[:, j, :],
                                           op0=ALU.mult, op1=ALU.add).then_inc(centered_ready, 1)
                inverse(name)
                dve.wait_ge(centered_ready, KC * (i + 1))
                scaled(name, lambda j: plane(CENTER + j), lambda j: col(gain, KC * int(name[-1]) + j), lambda j: X[:, j, :])
                low(name, lambda j: X[:, j, :])

            def ffn_and_ple(f):
                layer_norm(f"mix{f}", "ln_mix_g")
                ff_hi, ff_lo = parts[f"ff{f}"]
                with dve.Fori(0, FF // 2) as i:
                    for j in range(2):
                        dve.wait_ge(bank_free, i * 4 + 2 + PROD[f"ffn_in{f}"] + 2 * j + 2)
                        v.tensor_tensor(gated[:, j, :], plane(SG + j), plane(UU + j), ALU.mult).then_inc(ff_ready, 1)
                        dve.wait_ge(hi_ready, i * 2 + SPL[f"ff{f}"] + j + 1)
                        v.tensor_tensor(ff_lo[:, bass.ds(i * 2 + j, 1), :], gated[:, j:j + 1, :],
                                        ff_hi[:, bass.ds(i * 2 + j, 1), :].bitcast(F32), ALU.subtract)\
                            .then_inc(lo_ready, 1)
                residual(f"ffn_down{f}", TMPD)
                layer_norm(f"ffn{f}", "ln_ffn_g")
                low(f"p{f}", lambda j: plane(PRAW + j))
                for j in range(KC):
                    taken(f"ple_proj{f}", j)
                    own.do(v.tensor_tensor(plane(TMPP + j), plane(TMPP + j), plane(TMPG + j), ALU.mult))
                    own.wait()
                    v.tensor_tensor(X[:, j, :], X[:, j, :], plane(TMPP + j), ALU.add).then_inc(residual_ready, 1)

            residual("w_o", TMPO)
            ffn_and_ple(0)
            low("x_hgrn", lambda j: X[:, j, :])

            for h in range(HEADS):
                taken("hgrn_in", 8 + h)
                lf = plane(HLF + h)
                own.do(v.tensor_scalar(lf, lf, small[:, OMLB + h:OMLB + h + 1], small[:, LB + h:LB + h + 1], ALU.mult,
                                       ALU.add))
                own.do(v.tensor_scalar(plane(HK + h), plane(HK + h), small[:, OMLB + h:OMLB + h + 1], None, ALU.mult))
                own.wait()
                v.tensor_scalar(lf, lf, 2.0 ** -63, None, ALU.max).then_inc(forget_in, 1)
            for h in range(HEADS):
                dve.wait_ge(log_ready, h + 1)
                v.tensor_tensor_scan(plane(HG + h), scan_keep[:], plane(HLF + h), 0.0, ALU.mult, ALU.add)\
                    .then_inc(cum_ready, 1)
                dve.wait_ge(cum_ready, h + 1)
                g4 = plane(HG + h).rearrange("p (c t) -> p c t", c=NCH)
                if h == 0:
                    taken("hgrn_in", 31)
                v.tensor_tensor(plane(HKH + h).rearrange("p (c t) -> p c t", c=NCH),
                                g4[:, :, CH - 1:CH].broadcast_to([P, NCH, CH]), g4, ALU.subtract)\
                    .then_inc(decay_in, 1)
            for h in range(HEADS):
                dve.wait_ge(decay_ready, 2 * h + 2)
                own.do(v.tensor_tensor(plane(HLF + h), plane(HLF + h), plane(HQ + h), ALU.mult))
                v.tensor_tensor(plane(HKH + h), plane(HKH + h), plane(HK + h), ALU.mult).then_inc(khat_ready, 1)

            def by_level(ap, lv):
                return ap.rearrange("p (b two m) -> p b two m", two=2, m=2 ** lv)

            def make_level(e):
                h, lv = divmod(e, LEVELS)
                dve.wait_ge(gap_exp, e + 1)
                if e >= 2:
                    last_unit = ((e - 2) // LEVELS) * (LEVELS + 1) + (e - 2) % LEVELS
                    dve.wait_ge(pair_ready, last_unit + 1)
                m, x = by_level(plane(HM + e % 2), lv), by_level(plane(HE + e % 4), lv)
                v.tensor_tensor(m[:, :, 1, :], x[:, :, 1, :], by_level(plane(HQ + h), lv)[:, :, 1, :], ALU.mult)
                v.tensor_tensor(m[:, :, 0, :], x[:, :, 0, :], by_level(plane(HK + h), lv)[:, :, 0, :], ALU.mult)\
                    .then_inc(level_ready, 1)

            def mask_pairs(u):
                h, lv = divmod(u, LEVELS + 1)
                mask = level_mask[:, lv, :] if lv < LEVELS else ident[:]
                dve.wait_ge(pair_ready, u + 1)
                if u >= 2:
                    dve.wait_ge(intra_ready, u - 1)
                v.tensor_tensor(plane(HMASK + u % 2).rearrange("p (b t) -> p b t", b=TB),
                                ps[:, 6 + u % 2, :].rearrange("p (b t) -> p b t", b=TB),
                                mask.unsqueeze(1).broadcast_to([P, TB, P]), ALU.mult).then_inc(masked_ready, 1)

            make_level(0)
            for u in range(HEADS * (LEVELS + 1)):
                h, lv = divmod(u, LEVELS + 1)
                if lv != LEVELS - 1 and h * LEVELS + lv + (lv < LEVELS) < HEADS * LEVELS:
                    make_level(h * LEVELS + lv + (lv < LEVELS))
                mask_pairs(u)

            ov = A[:, HO:HO + 8, :]
            for c in range(NCH):
                if c:
                    dve.wait_ge(inter_ready, c)
                    dve.wait_ge(intra_taken, HEADS)
                    o_c = ov[:, :, c * CH:(c + 1) * CH]
                    v.tensor_tensor(o_c, o_c, ps[:, 6, :].rearrange("p (h t) -> p h t", h=HEADS), ALU.add)\
                        .then_inc(inter_added, 1)
                if c < NCH - 1:
                    dve.wait_ge(delta_ready, c + 1)
                    if c:
                        dve.wait_ge(state_ready, HEADS * c)
                    for h in range(HEADS):
                        d = ps[:, 2 + h // 4, (h % 4) * P:(h % 4) * P + P]
                        if c == 0:
                            v.tensor_copy(STATE[:, h, :], d).then_inc(state_ready, 1)
                        else:
                            v.scalar_tensor_tensor(out=STATE[:, h, :], in0=STATE[:, h, :],
                                                   scalar=dec[:, h, c:c + 1], in1=d, op0=ALU.mult,
                                                   op1=ALU.add).then_inc(state_ready, 1)
            inverse("hgrn")
            dve.wait_ge(inter_added, NCH - 1)
            scaled("hgrn", lambda j: plane(HO + j), lambda j: col("out_norm", j), lambda j: plane(HO + j))
            for h in range(HEADS):
                dve.wait_ge(scaled_ready, SCALED["hgrn"] + h + 1)
                v.tensor_tensor(plane(HO + h), plane(HO + h), plane(HGT + h), ALU.mult).then_inc(gated_ready, 1)
            low("o_hgrn", lambda j: plane(HO + j))
            residual("hgrn_o", TMPO)
            ffn_and_ple(1)

        @block.gpsimd
        def _(pool):
            g = nc.gpsimd
            own = Steps(pool, pool_step)

            def select(ap, op, fill, base, pattern, mult):
                own.wait()
                own.do(g.affine_select(out=ap, in_=ap, compare_op=op, fill=fill, base=base, pattern=pattern,
                                       channel_multiplier=mult))

            own.do(g.memset(halves[:], 1.0))
            own.do(g.memset(ident[:], 0.0))
            own.do(g.memset(win_mask[:], 0.0))
            own.do(g.memset(diag_mask[:], 0.0))
            own.do(g.memset(level_mask[:], 0.0))
            own.do(g.memset(scan_keep[:], 1.0))
            own.wait()
            own.do(g.memset(scan_keep[:].rearrange("p (c t) -> p c t", c=NCH)[:, :, 0:1], 0.0))
            own.do(g.iota(iota[:], [[1, P]], base=0, channel_multiplier=0, allow_small_or_imprecise_dtypes=True))
            hv = halves[:].rearrange("p (c t) -> p c t", c=2)
            select(hv, ALU.is_ge, 0.0, 0, [[-64, 2], [0, 64]], 1)
            select(hv, ALU.is_ge, 0.0, 63, [[64, 2], [0, 64]], -1)
            select(ident[:], ALU.not_equal, 1.0, 0, [[-1, P]], 1)
            select(win_mask[:], ALU.is_ge, NEG, P, [[-1, 2 * P]], 1)
            select(win_mask[:], ALU.is_gt, NEG, 0, [[1, 2 * P]], -1)
            select(diag_mask[:], ALU.is_ge, NEG, 0, [[-1, P]], 1)
            for lv in range(LEVELS):
                m = 2 ** lv
                nb = P // (2 * m)
                second = level_mask[:, lv, :].rearrange("p (b two m) -> p b two m", two=2, m=m)[:, :, 1, :]
                own.wait()
                own.do(g.memset(second, 1.0))
                select(second, ALU.is_ge, 0.0, 0, [[-2 * m, nb], [0, m]], 1)
                select(second, ALU.is_ge, 0.0, m - 1, [[2 * m, nb], [0, m]], -1)
            own.wait()
            pool.sem_inc(consts_ready, 1)

            def split(slot, n, i=0):
                raw, h, rest = ring[slot], whi[slot % SPLIT], wlo[slot % SPLIT]
                pool.wait_ge(weights_loaded[slot], i * 16 + 16 * (n // RING + 1))
                pool.wait_ge(tiles_started, i * RING + n - SPLIT + 2)
                pool.sem_inc(split_begun, 1)
                g.tensor_scalar(h[:], raw[:], 1.0, 0.0, ALU.mult, ALU.add).then_inc(whi_ready, 1)
                pool.wait_ge(whi_ready, i * RING + n + 1)
                g.tensor_tensor(rest[:], raw[:], h[:].bitcast(F32), ALU.subtract).then_inc(split_ready, 1)

            def split_tiles(n0, n1):
                loops = (n1 - n0) // RING
                with pool.Fori(0, loops) as i:
                    for n in range(n0, n0 + RING):
                        split(n % RING, n, i)
                for n in range(n0 + loops * RING, n1):
                    split(n % RING, n)

            split_tiles(DVE_TILES, FIRST["hgrn_o"])

            pool.wait_ge(decay_ready, 2 * HEADS)
            pool.wait_ge(kt_taken, HEADS)
            for h in range(HEADS):
                for lv in range(LEVELS):
                    e = h * LEVELS + lv
                    if e >= 4:
                        pool.wait_ge(level_ready, e - 3)
                    m = 2 ** lv
                    gv = plane(HG + h).rearrange("p (b two m) -> p b two m", two=2, m=m)
                    xv = plane(HE + e % 4).rearrange("p (b two m) -> p b two m", two=2, m=m)
                    mid = gv[:, :, 0, m - 1:m].broadcast_to([P, T // (2 * m), m])
                    g.tensor_tensor(xv[:, :, 1, :], gv[:, :, 1, :], mid, ALU.subtract)
                    g.tensor_tensor(xv[:, :, 0, :], mid, gv[:, :, 0, :], ALU.subtract).then_inc(gap_ready, 1)
            split_tiles(FIRST["hgrn_o"], NTILES)

        @block.sync
        def _(sp):
            sp.dma_start(par[:], params).then_inc(inputs_loaded, 16)
            sp.dma_start(X[:], x_in).then_inc(inputs_loaded, 16)
            for s in range(RING):
                sp.dma_start(ring[s][:], stream[s]).then_inc(weights_loaded[s], 16)

            def refill(i, s):
                sp.wait_ge(split_ready, i * RING + s - RING + 1)
                sp.dma_start(ring[s][:], stream[bass.ds(i * RING + s, 1)].rearrange("a p b n -> (a p) b n"))\
                    .then_inc(weights_loaded[s], 16)

            with sp.Fori(1, NTILES // RING) as i:
                for s in range(RING):
                    refill(i, s)
            for s in range(NTILES % RING):
                refill(NTILES // RING, s)
            for j in range(KC):
                sp.wait_ge(residual_ready, RES["ple1"] + j + 1)
                sp.dma_start(out[:, j, :], X[:, j, :]).then_inc(stored, 16)
            sp.wait_ge(stored, 16 * KC)


def blocks(w):
    w = np.asarray(w)
    k, n = w.shape
    return w.reshape(k // P, P, n // P, P).transpose(0, 2, 1, 3)


def by_output(w, pad=0):
    b = blocks(w).transpose(1, 0, 2, 3)
    if pad:
        b = np.concatenate([b, np.zeros((b.shape[0], pad, P, P), b.dtype)], axis=1)
    return b.reshape(-1, P, P)


def columns(v, n=None):
    return np.asarray(v).reshape(-1, P).T


def kernel(**inputs):
    import concourse.bacc as _bacc
    from concourse.bass_utils import run_bass_kernel_spmd as _run

    a = {k: np.asarray(v) for k, v in inputs.items()}
    parts = {}
    w_ada = by_output(a["w_ada"])
    for name, lo, n in (("shift1", 0, 8), ("scale1", 8, 8), ("ada_rest", 16, 24), ("gate2", 40, 8)):
        parts[name] = w_ada[lo * 8:(lo + n) * 8]
    w, b = a["w_in"], a["b_in"]
    pick = np.r_[0:512, 512:576, 512:576, 576:640, 576:640, 768:2304]
    parts["w_in"] = by_output(w[:, pick])
    parts["w_v"] = by_output(w[:, 640:768])
    parts["w_out"] = by_output(a["w_out"])
    parts["w_query"] = by_output(a["w_query"])
    keys = np.stack([a["peer_keys1"], a["peer_keys2"]], axis=1)
    parts["keys"] = keys.reshape(16, P, P).transpose(0, 2, 1)
    u = a["peer_u"].reshape(NKEY, P, KC, P).transpose(0, 2, 3, 1)
    parts["up"] = u.reshape(-1, P, P)
    parts["down"] = a["peer_v"].reshape(NKEY, P, KC, P).transpose(0, 2, 1, 3).reshape(-1, P, P)
    w = a["mla_w_dqkv_2"][0]
    turn = np.r_[544:576, 512:544]
    parts["dqkv"] = by_output(w[:, np.r_[0:576, 512:576, turn, turn]])
    w = a["mla_w_uq_2"][0].reshape(256, HEADS, 192)
    parts["uq"] = by_output(np.concatenate([w[:, :, 0:128].reshape(256, -1), w[:, :, 128:192].reshape(256, -1),
                                            w[:, :, np.r_[160:192, 128:160]].reshape(256, -1)], axis=1))
    w = a["mla_w_ukv_2"][0].reshape(256, HEADS, 256)
    parts["uk"] = by_output(w[:, :, 0:128].reshape(256, -1))
    parts["uv"] = by_output(w[:, :, 128:256].reshape(256, -1))
    parts["w_o"] = by_output(a["mla_w_o_2"][0])
    for i in range(2):
        w = a["ffn_w_in_2"][i].reshape(D, 2, FF, P).transpose(0, 2, 1, 3).reshape(D, -1)
        parts[f"ffn_in{i}"] = by_output(w)
        parts[f"ffn_down{i}"] = by_output(a["ffn_w_down_2"][i], pad=24 - FF)
        parts[f"ple_gate{i}"] = by_output(a["ple_w_gate_2"][i])
        parts[f"ple_proj{i}"] = by_output(a["ple_w_proj_2"][i])
    w = a["hgrn_w_in_2"][0]
    parts["hgrn_in"] = by_output(w[:, 0:2048])
    parts["hgrn_v"] = by_output(w[:, 2048:3072])
    parts["hgrn_gate"] = by_output(w[:, 3072:4096])
    parts["hgrn_o"] = by_output(a["hgrn_w_o_2"][0])
    flat = np.concatenate([parts[name] for name, n in PARTS if n])
    stream = np.ascontiguousarray(flat.reshape(NTILES, BLOCKS, P, P).transpose(0, 2, 1, 3))

    freq = (10000.0 ** (-np.arange(0, 64, 2, dtype=np.float32) / np.float32(64))).astype(np.float32)
    sign = np.repeat([-1.0, 1.0], 32)
    cols = dict(
        c=columns(a["c"]), b_ada=columns(a["b_ada"]), norm1_g=columns(a["norm1_g"]), b_in=columns(b[pick]),
        b_v=np.broadcast_to(b[640:768], (P, P)), sinks=np.broadcast_to(a["attn_sinks"][[0, 2, 1, 3, 4, 6, 5, 7]], (P, 8)),
        conv_w=columns(a["conv_w"]), attn_out_g=columns(a["attn_out_g"]), conv_out_g=columns(a["conv_out_g"]),
        b_out=columns(a["b_out"]), norm2_g=columns(a["norm2_g"]), final_g=columns(a["final_g"]),
        q_norm=columns(a["mla_q_norm_2"]), kv_norm=columns(a["mla_kv_norm_2"]), lb=columns(a["hgrn_lb_logits_2"]),
        out_norm=columns(a["hgrn_out_norm_2"]), ln_mix_g=columns(a["ln_mix_g_2"]), ln_mix_b=columns(a["ln_mix_b_2"]),
        ln_ffn_g=columns(a["ln_ffn_g_2"]), ln_ffn_b=columns(a["ln_ffn_b_2"]),
        inv_freq=np.tile(freq, 4)[:, None], sin_sign=np.tile(sign, 2)[:, None])
    arrays = {
        "stream": stream,
        "x_in": np.ascontiguousarray(a["x"][0].T.reshape(KC, P, T).transpose(1, 0, 2)),
        "params": np.ascontiguousarray(np.concatenate([cols[name] for name, _ in COLS], axis=1).astype(np.float32)),
        "positions": np.ascontiguousarray(np.broadcast_to(a["positions_2"].reshape(1, T), (P, T))),
        "ple_in": np.ascontiguousarray(a["p_2"][:, 0].transpose(0, 2, 1).reshape(2, 2, P, T).transpose(0, 2, 1, 3)),
    }
    nc = _bacc.Bacc("TRN2", target_bir_lowering=False, num_devices=1)
    args = [nc.dram_tensor(n, list(v.shape), mybir.dt.from_np(v.dtype), kind="ExternalInput").ap()
            for n, v in arrays.items()]
    out = nc.dram_tensor("out", [P, KC, T], F32, kind="ExternalOutput").ap()
    gate_map = nc.dram_tensor("gate_map", [NKEY, P, T], F32, kind="Internal").ap()
    gelu_map = nc.dram_tensor("gelu_map", [NKEY, P, T], F32, kind="Internal").ap()
    build(nc, *args, out, gate_map, gelu_map)
    r = _run(nc, [arrays], core_ids=[0])
    got = np.asarray(r.results[0]["out"])
    return got.transpose(2, 1, 0).reshape(1, T, D)
```

```python
import numpy as np
import concourse.bass as bass
from concourse import mybir
from contextlib import ExitStack

F32 = mybir.dt.float32
F32R = mybir.dt.float32r
U32 = mybir.dt.uint32
I32 = mybir.dt.int32
ALU = mybir.AluOpType
ACT = mybir.ActivationFunctionType
AX = mybir.AxisListType.X

PLANES = 74
P = 128
T = 512
D = 1024
KC = D // P
TB = T // P
RING = 4
SPLIT = 2
BLOCKS = 8

HEADS = 8
HD = 64
NKEY = 128
TOPK = 16
EARLY = 16
AMONG = (16, 16, 16, 8)
FF = 22
ALPHA = (2 * 2) ** 0.25
NEG = -1e30
LOWEST = -3e38
CH = 64
NCH = T // CH
LEVELS = 6

PARTS = [("w_in", 18), ("w_v", 1), ("w_out", 8), ("w_query", 16), ("keys", 2), ("up", NKEY), ("down", NKEY)]
PARTS += [("dqkv", 6), ("uq", 4), ("uk", 2), ("uv", 2), ("w_o", 8)]
for _i in range(2):
    if _i:
        PARTS += [("hgrn_in", 16), ("hgrn_v", 8), ("hgrn_gate", 8), ("hgrn_o", 8)]
    PARTS += [(f"ffn_in{_i}", 2 * FF), (f"ffn_down{_i}", 24), (f"ple_gate{_i}", 8), (f"ple_proj{_i}", 2)]
FIRST = {}
NTILES = 0
for _name, _n in PARTS:
    FIRST[_name] = NTILES
    NTILES += _n

PRODUCTS = [("w_in", 19), ("w_out", 8), ("w_query", 16), ("keys", 16), ("up", NKEY)]
PRODUCTS += [("dqkv", 6), ("uq", 16), ("uk", 8), ("uv", 8), ("w_o", 8), ("ffn_in0", 2 * FF), ("ffn_down0", 8),
             ("ple_gate0", 8), ("ple_proj0", 8), ("hgrn_in", 32), ("hgrn_o", 8), ("ffn_in1", 2 * FF),
             ("ffn_down1", 8), ("ple_gate1", 8), ("ple_proj1", 8)]
PROD = {}
_p = 0
for _name, _n in PRODUCTS:
    PROD[_name] = _p
    _p += _n

NORMS = [("norm1", 1, KC), ("heads", 1, KC), ("norm2", 1, KC), ("final", 1, KC), ("cq", 1, 2),
         ("ckv", 1, 2), ("mix0", 1, KC), ("ffn0", 1, KC), ("hgrn", 1, HEADS), ("mix1", 1, KC), ("ffn1", 1, KC)]
NGROUP, NSQ = {}, {}
_g0 = _s0 = 0
for _name, _n, _k in NORMS:
    NGROUP[_name], NSQ[_name] = _g0, _s0
    _g0 += _n
    _s0 += _n * _k
NORM_SHAPE = {name: (n, k) for name, n, k in NORMS}

SPLITS = [("norm1", 8), ("mix", 8), ("norm2", 8), ("x_mla", 8), ("cq", 2), ("ckv", 2), ("o_mla", 8), ("mix0", 8),
          ("ff0", FF), ("ffn0", 8), ("p0", 2), ("x_hgrn", 8), ("o_hgrn", 8), ("mix1", 8), ("ff1", FF), ("ffn1", 8),
          ("p1", 2)]
SPL = {}
_n0 = 0
for _name, _n in SPLITS:
    SPL[_name] = _n0
    _n0 += _n

PARTS_AT = dict(mixed=(32, 36), norm1=(0, 8), mix=(0, 8), norm2=(0, 8), x_mla=(0, 8),
                cq=(32, 36), ckv=(34, 38),
                o_mla=(24, 32), mix0=(0, 8), ff0=(22, 44), ffn0=(22, 30), p0=(58, 60), x_hgrn=(0, 8),
                o_hgrn=(24, 32), mix1=(0, 8), ff1=(22, 44), ffn1=(22, 30), p1=(58, 60))
HFF = 20

COLS = [("c", 8), ("b_ada", 48), ("norm1_g", 8), ("b_in", 18), ("b_v", 128), ("sinks", 8), ("conv_w", 12),
        ("attn_out_g", 4), ("conv_out_g", 4), ("b_out", 8), ("norm2_g", 8), ("final_g", 8), ("q_norm", 2),
        ("kv_norm", 2), ("lb", 16), ("out_norm", 8), ("ln_mix_g", 16), ("ln_mix_b", 16), ("ln_ffn_g", 16),
        ("ln_ffn_b", 16), ("inv_freq", 1), ("sin_sign", 1)]
COL = {}
_c = 0
for _name, _n in COLS:
    COL[_name] = _c
    _c += _n
NCOLS = _c
ROUND = 1.5 * 2.0 ** 23
TWO_PI = (6.28125, 0.0019350051879882812, 2.0 * np.pi - 6.28125 - 0.0019350051879882812)


def build(nc, stream, ada_w, x_in, params, positions, ple_in, out, gate_map, gelu_map):
    with ExitStack() as ctx:
        def sb(name, shape, dt=F32):
            return ctx.enter_context(nc.sbuf_tensor(name, shape, dt))

        def sem(name):
            return ctx.enter_context(nc.semaphore(name))

        ps = ctx.enter_context(nc.psum_tensor("ps", [P, 8, T], F32))

        ring = [sb(f"ring{i}", [P, BLOCKS, P]) for i in range(RING)]
        whi = [sb(f"whi{i}", [P, BLOCKS, P], F32R) for i in range(SPLIT)]
        wlo = [sb(f"wlo{i}", [P, BLOCKS, P], F32R) for i in range(SPLIT)]
        X = sb("X", [P, KC, T])

        def overlay(name, first, n, dt):
            with nc.sbuf_tensor(f"{name}_before", [P, first, T], dt) if first else ExitStack():
                with nc.sbuf_tensor(name, [P, n, T], dt) as t:
                    return t

        parts = {name: [overlay(f"{name}_{side}", first, n, F32R) for side, first in zip(("hi", "lo"), PARTS_AT[name])]
                 for name, n in SPLITS + [("mixed", 4)]}
        gated = overlay("gated", HFF, 2, F32)
        A = sb("A", [P, PLANES, T])
        par = sb("par", [P, NCOLS])
        ada = sb("ada", [P, 48])
        cs = sb("cs", [P, 8])
        ones = sb("ones", [P, P])
        pick_plane = sb("pick_plane", [P, 60])
        pick_halves = sb("pick_halves", [P, 60])
        ident = sb("ident", [P, P])
        iota = sb("iota", [P, P])
        win_mask = sb("win_mask", [P, 2 * P])
        diag_mask = sb("diag_mask", [P, P])
        level_mask = sb("level_mask", [P, LEVELS, P])
        scan_keep = sb("scan_keep", [P, T])
        small = sb("small", [P, 96])
        eps = sb("eps", [P, 2])
        early_root = sb("early_root", [P, len(NORMS)])
        dec = sb("dec", [P, HEADS, NCH])

        weights_loaded = [sem(f"weights_loaded{i}") for i in range(RING)]
        inputs_loaded = sem("inputs_loaded")
        pos_loaded = sem("pos_loaded")
        split_ready = sem("split_ready")
        whi_ready = sem("whi_ready")
        split_begun = sem("split_begun")
        hi_ready = sem("hi_ready")
        lo_ready = sem("lo_ready")
        tiles_started = sem("tiles_started")
        product_ready = sem("product_ready")
        bank_free = sem("bank_free")
        consts_ready = sem("consts_ready")
        pool_step = sem("pool_step")
        dve_step = sem("dve_step")
        silu_ready = sem("silu_ready")
        lb_in = sem("lb_in")
        lb_exp = sem("lb_exp")
        ada_loaded = [sem(f"ada_loaded{i}") for i in range(4)]
        ada_used = sem("ada_used")
        row_ready = sem("row_ready")
        ada_sums = sem("ada_sums")
        ada_ready = sem("ada_ready")
        sq_ready = sem("sq_ready")
        sq_used = sem("sq_used")
        root_ready = sem("root_ready")
        rstd_ready = sem("rstd_ready")
        spread_ready = sem("spread_ready")
        scaled_ready = sem("scaled_ready")
        h_ready = sem("h_ready")
        residual_ready = sem("residual_ready")
        mean_ready = sem("mean_ready")
        centered_ready = sem("centered_ready")
        bias_ready = sem("bias_ready")
        scores_ready = sem("scores_ready")
        shift_ready = sem("shift_ready")
        exp_ready = sem("exp_ready")
        sink_ready = sem("sink_ready")
        probs_ready = sem("probs_ready")
        pt_ready = sem("pt_ready")
        pt_taken = sem("pt_taken")
        o_ready = sem("o_ready")
        o_taken = sem("o_taken")
        conv_ready = sem("conv_ready")
        gate_in = sem("gate_in")
        gate_exp = sem("gate_exp")
        route_ready = sem("route_ready")
        route_turned = sem("route_turned")
        route_taken = sem("route_taken")
        onehot_ready = sem("onehot_ready")
        onehot_free = sem("onehot_free")
        gate_bank_free = sem("gate_bank_free")
        gate_stored = sem("gate_stored")
        gelu_stored = [sem(f"gelu_stored{i}") for i in range(2)]
        ring_loaded = [sem(f"ring_loaded{i}") for i in range(8)]
        mixed_ready = sem("mixed_ready")
        mixed_hi = sem("mixed_hi")
        mixed_lo = sem("mixed_lo")
        sums_ready = sem("sums_ready")
        ones_ready = sem("ones_ready")
        rope_in = sem("rope_in")
        rope_out = sem("rope_out")
        rope_ready = sem("rope_ready")
        ff_ready = sem("ff_ready")
        p_loaded = sem("p_loaded")
        forget_in = sem("forget_in")
        log_ready = sem("log_ready")
        cum_ready = sem("cum_ready")
        decay_in = sem("decay_in")
        decay_ready = sem("decay_ready")
        khat_ready = sem("khat_ready")
        kt_ready = sem("kt_ready")
        kt_taken = sem("kt_taken")
        gap_ready = sem("gap_ready")
        gap_exp = sem("gap_exp")
        level_ready = sem("level_ready")
        pair_ready = sem("pair_ready")
        masked_ready = sem("masked_ready")
        intra_ready = sem("intra_ready")
        intra_taken = sem("intra_taken")
        inter_ready = sem("inter_ready")
        delta_ready = sem("delta_ready")
        inter_added = sem("inter_added")
        state_ready = sem("state_ready")
        gated_ready = sem("gated_ready")
        stored = sem("stored")
        block = ctx.enter_context(nc.Block())

        def col(name, j=0, n=1):
            return par[:, COL[name] + j:COL[name] + j + n]

        def plane(i):
            return A[:, i, :]

        class Steps:
            def __init__(self, eng, s):
                self.eng, self.sem, self.n = eng, s, 0

            def do(self, ins):
                ins.then_inc(self.sem, 1)
                self.n += 1
                return self.n

            def wait(self, n=None):
                self.eng.wait_ge(self.sem, self.n if n is None else n)

        SHIFT1, SCALE1, GATE1, SHIFT2, SCALE2, GATE2 = range(0, 48, 8)

        def ada_col(part, j=0, n=1):
            return ada[:, part + j:part + j + n]

        ADA_FIRST, ADA_RING, ADA_ROWS = 24, 0, (56, 58)
        ADA_BANKS = ((7, 1), (6, 5))

        def ada_group(g):
            first = ADA_FIRST + 8 * g if g < 4 else ADA_RING + 8 * ((g - 4) % 3)
            view = A[:, first:first + 8, :].rearrange("p (k a) t -> p k (a t)", a=2)
            return (view, ada_loaded[g], 16) if g < 4 else (view, ada_loaded[(g - 4) % 3], 32 + 16 * ((g - 4) // 3))

        def ada_row(part):
            return A[0:1, ADA_ROWS[part % 2]:ADA_ROWS[part % 2] + 2, :]

        GS1, LB, OMLB = 0, 8, 16
        TMPH = 16
        PQ, PKD, PB_, PCG, PU, PV = 24, 28, 30, 34, 38, 42
        ATT, Z, MIX = 43, 47, 52
        PROBS, PT = (60, 62), (64, 66)
        zv = A[:, Z:Z + 5, :].rearrange("p a t -> p (a t)")[:, 0:4 * (T + 2)].rearrange("p (c t) -> p c t", c=4)
        STAGE = 16
        SCORES = 48
        GELU = 72
        UR, GR = 16, 24
        accf = A[:, 64:72, :].rearrange("p a t -> p (a t)")
        staging = A[:, STAGE:STAGE + 32, :].rearrange("p a t -> p (a t)").rearrange("p (i t) -> p i t", i=NKEY)
        turned = accf[:, 2048:2048 + 3 * P].rearrange("p (a t) -> p a t", a=3)
        hot1 = accf[:, 2560:3072].rearrange("p (s i) -> p s i", s=4)
        hot2 = accf[:, 3072:3584].rearrange("p (s i) -> p s i", s=4)
        routed = accf[:, 1664:2048].rearrange("p (a t) -> p a t", a=3)
        DOWN, COS, SIN, ANG, POS, CQN, CKN, QN, QR, QS, KN, VM, OM = 16, 64, 65, 66, 71, 27, 29, 40, 48, 52, 56, 0, 8
        MPROBS, MPT = (64, 66), (68, 70)
        TMPO, CENTER, SG, UU, TMPD, TMPG, TMPP, PRAW = 40, 56, 16, 18, 0, 40, 48, 66
        HQ, HLF, HK, HV, HGT, HG, HKH, HKT, HO, HM, HE, HMASK = 16, 24, 32, 40, 48, 56, 64, 8, 64, 72, 0, 4
        STATES = [A[:, first:first + 2, :].rearrange("p a t -> p (a t)").rearrange("p (h e) -> p h e", h=HEADS)
                  for first in (6, 4)]

        def hi(name, j):
            return parts[name][0][:, j, :]

        def lo(name, j):
            return parts[name][1][:, j, :]

        NORM = {}
        NORM.update(norm1=(68, 72), heads=(68, 16), norm2=(68, 72), final=(68, 72),
                    cq=(68, 72), ckv=(68, 73), mix0=(68, 72), ffn0=(68, 72), hgrn=(0, 16), mix1=(68, 72),
                    ffn1=(68, 72))
        AFTER = {"mix0": "mla", "ffn0": "ffn0", "mix1": "hgrn", "ffn1": "ffn1"}
        eps_col = {1e-6: eps[:, 0:1], 1e-5: eps[:, 1:2]}

        def sm(unit, c, n=1):
            return small[:, 64 + 16 * (unit % 2) + c:64 + 16 * (unit % 2) + c + n]

        LN = {"mix0": 0, "ffn0": 1, "mix1": 2, "ffn1": 3}
        spread_halves = A[0:32, PQ:PQ + 2, :].rearrange("p a (j m) -> p (a j) m", m=P)
        SCALED = NSQ
        PACKED = {"heads": pick_halves, "hgrn": pick_plane}
        RES = {"w_out": 0, "peer": 8, "mla": 16, "ffn0": 24, "ple0": 32, "hgrn": 40, "ffn1": 48, "ple1": 56}
        WIN_ORDER = (0, 2, 1, 3)
        UNITS = 8

        @block.tensor
        def _(pe):
            mm = nc.tensor.matmul

            def tile_in(tile, i=0):
                pe.wait_ge(split_ready, i + tile + 1)
                return whi[tile % SPLIT], wlo[tile % SPLIT]

            def three(out_, left, right, start, stop):
                (lh, ll), (rh, rl) = left, right
                first = mm(out_, lh, rh, start=start, stop=False)
                mm(out_, lh, rl, start=False, stop=False)
                return first, mm(out_, ll, rh, start=False, stop=stop)

            def linear(name, operand, kb=8, by_token=False, tiles=None, first=0, count=None,
                       mean_of=None):
                t0 = FIRST[tiles or name]
                p0 = p_first = PROD[name] + first
                pad = 8 * -(-kb // 8) if kb > 8 else kb
                n = dict(PRODUCTS)[name] if count is None else count
                body = max(SPLIT, 2 * pad // 8)
                per = body * 8 // pad

                def some(t0, p0, i, np_):
                    for q in range(np_):
                        p = p0 + q
                        pe.wait_ge(bank_free, i * per + p + 1)
                        for tb in range(TB if by_token else 1):
                            for b in range(kb):
                                s, w = divmod(q * pad + b, 8)
                                new = w == 0 and tb == 0
                                if new:
                                    tile_in(t0 + s, i * body)
                                wh, wl = (x[(t0 + s) % SPLIT][:, w, :] for x in (whi, wlo))
                                xh, xl = hi(operand, b), lo(operand, b)
                                if p == p_first and tb == 0:
                                    pe.wait_ge(lo_ready, SPL[operand] + b + 1)
                                out_ = ps[:, p % 2, :]
                                left, right = (wh, wl), (xh, xl)
                                if by_token:
                                    r = slice(tb * P, (tb + 1) * P)
                                    out_ = ps[:, p % 2, r]
                                    left, right = (xh[:, r], xl[:, r]), (wh, wl)
                                begun, last = three(out_, left, right, b == 0, b == kb - 1)
                                if new:
                                    begun.then_inc(tiles_started, 1)
                        last.then_inc(product_ready, 1)
                loops = n // per
                if mean_of:
                    def mean(j, i=0):
                        pe.wait_ge(residual_ready, i * per + RES[mean_of] + j + 1)
                        x = X[:, bass.ds(i * per + j, 1), :].rearrange("p a t -> p (a t)") if j < 0 else X[:, j, :]
                        return mm(ps[:, 4, :], ones[:], x, start=j == 0, stop=j == KC - 1)

                    some(t0, p0, 0, per)
                    some(t0 + body, p0 + per, 0, per)
                    mean(0)
                    mean(1)
                    with pe.Fori(2, loops) as i:
                        some(t0, p0, i, per)
                        mean(-2, i)
                        mean(-1, i)
                    mean(KC - 2)
                    mean(KC - 1).then_inc(mean_ready, 1)
                elif loops > 1:
                    with pe.Fori(0, loops) as i:
                        some(t0, p0, i, per)
                    if n > loops * per:
                        some(t0 + loops * body, p0 + loops * per, 0, n - loops * per)
                else:
                    some(t0, p0, 0, n)

            def sums(name):
                n, k = NORM_SHAPE[name]
                g = NGROUP[name]
                if g >= 2:
                    pe.wait_ge(root_ready, g - 1)
                for j in range(k):
                    c = NSQ[name] + j
                    pe.wait_ge(sq_ready, c + 1)
                    out_, left = ps[:, 2 + g % 2, :], ones[:]
                    if name in PACKED:
                        out_, left = ps[0:32, 2 + g % 2, :], PACKED[name][:, 28 - 4 * j:60 - 4 * j]
                    mm(out_, left, plane(NORM[name][0] + c % 4), start=j == 0, stop=j == k - 1).then_inc(sq_used, 1)

            def spread(name):
                pe.wait_ge(rstd_ready, NGROUP[name] + 1)
                for j in range(NORM_SHAPE[name][1]):
                    if j >= 2:
                        pe.wait_ge(scaled_ready, SCALED[name] + j - 1)
                    left = ident[0:32, 4 * j:4 * j + 1].broadcast_to([32, P]) if name == "hgrn" else spread_halves[:, j, :]
                    mm(ps[:, 4 + j % 2, :], left, A[0:32, NORM[name][1], :], start=True, stop=True)\
                        .then_inc(spread_ready, 1)

            def ada_sum(g):
                part = g // 2
                tiles, loaded, value = ada_group(g)
                pe.wait_ge(loaded, value)
                for k in range(4):
                    c = 4 * (g % 2) + k
                    for a, bank in enumerate(ADA_BANKS[part == 1]):
                        last = mm(ps[0:1, bank, :], cs[:, c:c + 1], tiles[:, k, a * T:(a + 1) * T], start=c == 0,
                                  stop=c == KC - 1)
                    if k == 3:
                        last.then_inc(ada_used, 1)

            def ada_columns(part):
                pe.wait_ge(row_ready, part + 1)
                if part:
                    pe.wait_ge(ada_ready, part)
                row = ada_row(part).rearrange("p a t -> p (a t)")
                for j in range(8):
                    last = mm(ps[:, 0, part * 8 + j:part * 8 + j + 1], row[:, j * P:(j + 1) * P], ones[0:1, 0:1],
                              start=True, stop=True)
                last.then_inc(ada_sums, 1)

            pe.sem_inc(onehot_free, 4)
            pe.wait_ge(ones_ready, 1)
            sums("norm1")
            pe.wait_ge(silu_ready, 1)
            for g in range(4):
                ada_sum(g)
            ada_columns(0)
            ada_columns(1)
            pe.wait_ge(ada_ready, 2)
            linear("w_in", "norm1", count=18)
            linear("w_in", "norm1", by_token=True, tiles="w_v", first=18, count=1)
            pe.wait_ge(consts_ready, 1)


            def win_scores(u):
                n, kv = divmod(u, 2)
                if u:
                    pe.wait_ge(exp_ready, u)
                lo = P if n == 0 else 0
                for g in range(4):
                    h = kv * 4 + WIN_ORDER[g]
                    r = slice(64 * (h % 2), 64 * (h % 2) + 64)
                    last = mm(ps[:, 2 + g // 2, (g % 2) * 256 + lo:(g % 2) * 256 + 256],
                              A[r, PQ + h // 2, n * P:(n + 1) * P], A[r, PKD + kv, (n - 1) * P + lo:(n + 1) * P],
                              start=True, stop=True)
                last.then_inc(scores_ready, 1)

            pe.wait_ge(bank_free, 2 + PROD["w_in"] + 6)
            win_scores(0)
            pe.wait_ge(bias_ready, 1)
            for u in range(UNITS):
                n, kv = divmod(u, 2)
                if u + 1 < UNITS:
                    win_scores(u + 1)
                if u == 0:
                    pe.wait_ge(bank_free, 2 + PROD["w_in"] + 19)
                elif u % 2 == 0:
                    ada_columns(u // 2 + 1)
                ada_sum(4 + u)
                pe.wait_ge(probs_ready, u + 1)
                kbs = [1] if n == 0 else [0, 1]
                pv = A[:, PROBS[u % 2]:PROBS[u % 2] + 2, :].rearrange("p a (h k) -> p (a h) k", h=2)
                if u:
                    pe.wait_ge(pt_taken, u)
                for g in range(4):
                    for kb in kbs:
                        i = g * 2 + kb
                        last = nc.tensor.transpose(ps[:, 4 + i // 4, (i % 4) * P:(i % 4) * P + P],
                                                   pv[:, g, kb * P:(kb + 1) * P], ident[:])
                last.then_inc(pt_ready, 1)
                pe.wait_ge(pt_taken, u + 1)
                if u:
                    pe.wait_ge(o_taken, u)
                ptv = A[:, PT[u % 2]:PT[u % 2] + 2, :].rearrange("p a (h k) -> p (a h) k", h=4)
                for g in range(4):
                    h = WIN_ORDER[g]
                    for kb in kbs:
                        t0 = (n - 1 + kb) * P
                        last = mm(ps[64 * (h % 2):64 * (h % 2) + 64, 6, (h // 2) * P:(h // 2) * P + P],
                                  A[:, PV, t0 + kv * 64:t0 + kv * 64 + 64], ptv[:, g * 2 + kb, :],
                                  start=kb == kbs[0], stop=kb == 1)
                last.then_inc(o_ready, 1)
            ada_columns(5)
            sums("heads")
            spread("heads")
            pe.wait_ge(ada_ready, 6)
            linear("w_out", "mix")
            sums("norm2")
            linear("w_query", "norm2")

            for t in range(2):
                wh, wl = (x[:].bitcast(F32) for x in tile_in(FIRST["keys"] + t))
                for tb in range(TB):
                    for f in range(2):
                        p = PROD["keys"] + t * 8 + tb * 2 + f
                        pe.wait_ge(bank_free, p + 1)
                        if t == 0 and tb == 0:
                            pe.wait_ge(bank_free, 2 + PROD["w_query"] + 16)
                        for j in range(4):
                            hh = t * 8 + f * 4 + j
                            q = A[:, STAGE + hh, tb * P:(tb + 1) * P]
                            begun = mm(ps[:, p % 2, j * P:(j + 1) * P], q, wh[:, f * 4 + j, :], start=True, stop=False)
                            last = mm(ps[:, p % 2, j * P:(j + 1) * P], q, wl[:, f * 4 + j, :], start=False, stop=True)
                            if tb == 0 and f == 0 and j == 0:
                                begun.then_inc(tiles_started, 1)
                        last.then_inc(product_ready, 1)

            ps_gates = ps[:, 6:8, :].rearrange("p b (t i) -> p b t i", t=4)

            def up_step(t, i, s, k):
                p = PROD["up"] + t + s
                if k == 0:
                    tile_in(FIRST["up"] + t + s, i * 2)
                    pe.wait_ge(bank_free, i * 2 + p + 1)
                wh, wl = (x[(FIRST["up"] + t + s) % SPLIT][:, k, :] for x in (whi, wlo))
                begun, last = three(ps[:, p % 2, :], (wh, wl), (hi("norm2", k), lo("norm2", k)), k == 0, k == KC - 1)
                if k == 0:
                    begun.then_inc(tiles_started, 1)
                if k == KC - 1:
                    last.then_inc(product_ready, 1)

            def expert_up(first, n):
                with pe.Fori(0, n // 2) as i:
                    for s in range(2):
                        for k in range(KC):
                            up_step(first, i, s, k)

            done = 0
            for tb in range(TB):
                expert_up(done, EARLY)
                done += EARLY
                pe.wait_ge(route_ready, tb + 1)
                for a in range(3):
                    last = nc.tensor.transpose(ps[:, 2, a * P:(a + 1) * P], routed[:, a, :], ident[:])
                last.then_inc(route_turned, 1)
                toks = P // AMONG[tb]
                with pe.Fori(0, AMONG[tb] // 2) as i:
                    for s in range(2):
                        for k in range(KC):
                            up_step(done, i, s, k)
                            for m in range(toks // KC):
                                at = s * toks + k * toks // KC + m
                                tok = tb * P + at
                                pe.wait_ge(onehot_ready, i * (2 * toks) + tok + 1)
                                if at % 4 == 0:
                                    pe.wait_ge(gate_bank_free, i * (toks // 2) + tok // 4 + 1)
                                mm(ps_gates[:, at // 4 % 2, at % 4, :], hot2[:, at % 4, :], hot1[:, at % 4, :],
                                   start=True, stop=True).then_inc(onehot_free, 1)
                done += AMONG[tb]
            expert_up(done, NKEY - done)

            pe.wait_ge(bank_free, 2 + PROD["up"] + NKEY)
            pe.wait_ge(gate_bank_free, 2 + P)
            pe.wait_ge(route_taken, TB)

            def expert_down(n0, i=0):
                for s in range(4):
                    n = n0 + s
                    t = FIRST["down"] + n
                    wh, wl = tile_in(t, i * 4)
                    pe.wait_ge(mixed_lo, i * 4 + n + 1)
                    for d in range(8):
                        begun, last = three(ps[:, d, :], (wh[:, d, :], wl[:, d, :]), (hi("mixed", s), lo("mixed", s)),
                                            n == 0, n == NKEY - 1)
                        if d == 0:
                            begun.then_inc(tiles_started, 1)
                        if n == NKEY - 1:
                            last.then_inc(sums_ready, 1)

            expert_down(0)
            with pe.Fori(0, NKEY // 4 - 2) as i:
                expert_down(4, i)
            expert_down(NKEY - 4)
            pe.wait_ge(residual_ready, RES["peer"] + 4)
            sums("final")

            linear("dqkv", "x_mla")
            sums("cq")
            sums("ckv")
            linear("uq", "cq", kb=2)
            linear("uk", "ckv", kb=2)
            linear("uv", "ckv", kb=2, by_token=True)

            def mla_scores(m):
                n, pair = divmod(m, 4)
                pe.wait_ge(exp_ready, UNITS + m)
                for g in range(2):
                    h = 2 * pair + g
                    out_ = ps[:, 2 + g, 0:(n + 1) * P]
                    mm(out_, A[:, QN + h, n * P:(n + 1) * P], A[:, KN + h, 0:(n + 1) * P], start=True, stop=False)
                    r = slice(64 * g, 64 * g + 64)
                    last = mm(out_, A[r, QR + pair, n * P:(n + 1) * P], A[r, DOWN + 4, 0:(n + 1) * P], start=False,
                              stop=True)
                last.then_inc(scores_ready, 1)

            pe.wait_ge(rope_ready, 2)
            mla_scores(0)
            for m in range(16):
                n, pair = divmod(m, 4)
                if m + 1 < 16:
                    mla_scores(m + 1)
                pe.wait_ge(probs_ready, UNITS + m + 1)
                pe.wait_ge(pt_taken, UNITS + m)
                pv = A[:, MPROBS[m % 2]:MPROBS[m % 2] + 2, :]
                for g in range(2):
                    for kb in range(n + 1):
                        last = nc.tensor.transpose(ps[:, 4 + g, kb * P:(kb + 1) * P], pv[:, g, kb * P:(kb + 1) * P],
                                                   ident[:])
                last.then_inc(pt_ready, 1)
                pe.wait_ge(pt_taken, UNITS + m + 1)
                pe.wait_ge(o_taken, UNITS + m)
                for g in range(2):
                    for kb in range(n + 1):
                        last = mm(ps[:, 6, g * P:(g + 1) * P], A[:, VM + 2 * pair + g, kb * P:(kb + 1) * P],
                                  A[:, MPT[m % 2] + g, kb * P:(kb + 1) * P], start=kb == 0, stop=kb == n)
                last.then_inc(o_ready, 1)
            linear("w_o", "o_mla", mean_of="mla")
            sums("mix0")

            def ffn_and_ple(i):
                linear(f"ffn_in{i}", f"mix{i}")
                linear(f"ffn_down{i}", f"ff{i}", kb=FF, mean_of=f"ffn{i}")
                sums(f"ffn{i}")
                linear(f"ple_gate{i}", f"ffn{i}")
                linear(f"ple_proj{i}", f"p{i}", kb=2)

            ffn_and_ple(0)

            linear("hgrn_in", "x_hgrn", count=16)
            linear("hgrn_in", "x_hgrn", by_token=True, tiles="hgrn_v", first=16, count=8)
            linear("hgrn_in", "x_hgrn", tiles="hgrn_gate", first=24, count=8)
            for h in range(HEADS):
                pe.wait_ge(khat_ready, h + 1)
                if h >= 2:
                    pe.wait_ge(kt_taken, h - 1)
                for tb in range(TB):
                    last = nc.tensor.transpose(ps[:, 2 + h % 2, tb * P:(tb + 1) * P], A[:, HKH + h, tb * P:(tb + 1) * P],
                                               ident[:])
                last.then_inc(kt_ready, 1)

            def pairs(u):
                h, lv = divmod(u, LEVELS + 1)
                if lv < LEVELS:
                    pe.wait_ge(level_ready, h * LEVELS + lv + 1)
                    k_ap = q_ap = plane(HM + (h * LEVELS + lv) % 2)
                else:
                    k_ap, q_ap = plane(HK + h), plane(HQ + h)
                if u >= 2:
                    pe.wait_ge(masked_ready, u - 1)
                for tb in range(TB):
                    r = slice(tb * P, (tb + 1) * P)
                    last = mm(ps[:, 6 + u % 2, r], k_ap[:, r], q_ap[:, r], start=True, stop=True)
                last.then_inc(pair_ready, 1)

            n_units = HEADS * (LEVELS + 1)
            pe.wait_ge(kt_taken, HEADS)
            pairs(0)
            for u in range(n_units):
                h, lv = divmod(u, LEVELS + 1)
                if u + 1 < n_units:
                    pairs(u + 1)
                pe.wait_ge(masked_ready, u + 1)
                if lv == 0 and h >= 2:
                    pe.wait_ge(intra_taken, h - 1)
                for tb in range(TB):
                    r = slice(tb * P, (tb + 1) * P)
                    last = mm(ps[:, 4 + h % 2, r], A[:, HV + h, r], A[:, HMASK + u % 2, r], start=lv == 0 and tb == 0,
                              stop=lv == LEVELS, skip_group_check=True)
                last.then_inc(intra_ready, 1)
            def chunk_delta(c):
                if c >= 2:
                    pe.wait_ge(state_ready, HEADS * (c - 1))
                r = slice(64 * (c % 2), 64 * (c % 2) + 64)
                w = slice((c // 2) * P, (c // 2) * P + P)
                for h in range(HEADS):
                    last = mm(ps[:, 2 + 2 * (c % 2) + h // 4, (h % 4) * P:(h % 4) * P + P], A[r, HKT + h, w],
                              A[r, HV + h, w], start=True, stop=True)
                last.then_inc(delta_ready, 1)

            pe.wait_ge(intra_taken, HEADS)
            chunk_delta(0)
            chunk_delta(1)
            for c in range(1, NCH):
                if c >= 3:
                    pe.wait_ge(inter_added, c - 2)
                pe.wait_ge(state_ready, HEADS * c)
                for h in range(HEADS):
                    last = mm(ps[:, 6 + c % 2, h * CH:(h + 1) * CH], STATES[(c - 1) % 2][:, h, :],
                              A[:, HLF + h, c * CH:(c + 1) * CH], start=True, stop=True)
                last.then_inc(inter_ready, 1)
                if c + 1 < NCH - 1:
                    chunk_delta(c + 1)
            sums("hgrn")
            spread("hgrn")
            linear("hgrn_o", "o_hgrn", mean_of="hgrn")
            sums("mix1")
            ffn_and_ple(1)

        @block.scalar
        def _(act):
            fn = nc.scalar.activation

            def take(name, j, out_, func=ACT.Copy, **kw):
                p = PROD[name] + j
                act.wait_ge(product_ready, p + 1)
                fn(out_, ps[:, p % 2, :], func, **kw).then_inc(bank_free, 1)

            def norm(name, src, ready, width, eps):
                n, k = NORM_SHAPE[name]
                g = NGROUP[name]
                fn(early_root[:, g:g + 1], ones[:, 0:1], ACT.Sqrt)
                for j in range(k):
                    c = NSQ[name] + j
                    if c >= 4:
                        act.wait_ge(sq_used, c - 3)
                    ready(j)
                    fn(plane(NORM[name][0] + c % 4), src(j), ACT.Square).then_inc(sq_ready, 1)
                rows = 32 if name in PACKED else P
                act.wait_ge(sq_used, NSQ[name] + k)
                fn(A[0:rows, NORM[name][1], :], ps[0:rows, 2 + g % 2, :], ACT.Sqrt, scale=1.0 / width,
                   bias=eps_col[eps][0:rows]).then_inc(root_ready, 1)

            def high(name, src, ready, func=ACT.Copy, **kw):
                for j in range(dict(SPLITS)[name]):
                    ready(j)
                    fn(hi(name, j), src(j), func, **{k: x(j) for k, x in kw.items()}).then_inc(hi_ready, 1)

            def row_out(part):
                act.wait_ge(ada_used, 2 * part + 2)
                row = ada_row(part)
                for a, bank in enumerate(ADA_BANKS[part == 1]):
                    last = fn(row[:, a, :], ps[0:1, bank, :], ACT.Copy)
                last.then_inc(row_ready, 1)

            act.sem_inc(bank_free, 2)
            act.sem_inc(gate_bank_free, 2)
            act.wait_ge(inputs_loaded, 16 * 2)
            fn(cs[:], col("c", 0, 8), ACT.Silu).then_inc(silu_ready, 1)
            act.wait_ge(lb_in, 1)
            fn(small[:, 40:56], small[:, 40:56], ACT.Exp).then_inc(lb_exp, 1)
            act.wait_ge(ones_ready, 1)
            norm("norm1", lambda j: X[:, j, :], lambda j: None, D, 1e-6)
            row_out(0)
            row_out(1)
            act.wait_ge(ada_ready, 2)
            high("norm1", lambda j: plane(TMPH + j), lambda j: act.wait_ge(scaled_ready, SCALED["norm1"] + j + 1),
                 ACT.Identity, bias=lambda j: ada_col(SHIFT1, j))
            for j in range(18):
                take("w_in", j, plane(PQ + j), ACT.Identity, bias=col("b_in", j))
            take("w_in", 18, plane(PV))

            def attention(base, n_units, exps, turned_out, o_out, extra=lambda u: None):
                for u in range(n_units):
                    if u == 0:
                        exps(0)
                    b = base + u
                    act.wait_ge(pt_ready, b + 1)
                    if b - base >= 2:
                        act.wait_ge(o_ready, b - 1)
                    turned_out(u)
                    if u + 1 < n_units:
                        exps(u + 1)
                    extra(u)
                    act.wait_ge(o_ready, b + 1)
                    o_out(u)

            def win_exps(u):
                n, kv = divmod(u, 2)
                lo = P if n == 0 else 0
                act.wait_ge(shift_ready, u + 1)
                if u >= 2:
                    act.wait_ge(pt_ready, u - 1)
                pv = A[:, PROBS[u % 2]:PROBS[u % 2] + 2, :].rearrange("p a (h k) -> p (a h) k", h=2)
                fn(sm(u, 8, 4), sm(u, 4, 4), ACT.Exp).then_inc(sink_ready, 1)
                for g in range(4):
                    last = fn(pv[:, g, lo:2 * P], ps[:, 2 + g // 2, (g % 2) * 256 + lo:(g % 2) * 256 + 256], ACT.Exp,
                              bias=sm(u, g), accum_out=sm(u, 12 + g))
                last.then_inc(exp_ready, 1)

            def win_turned(u):
                kbs = [1] if u < 2 else [0, 1]
                src = ps[:, 4:6, :].rearrange("p b (h k) -> p (b h) k", h=4)
                dst = A[:, PT[u % 2]:PT[u % 2] + 2, :].rearrange("p a (h k) -> p (a h) k", h=4)
                if u < 2:
                    src = src.rearrange("p (g k) t -> p g k t", k=2)[:, :, 1, :]
                    dst = dst.rearrange("p (g k) t -> p g k t", k=2)[:, :, 1, :]
                fn(dst, src, ACT.Copy).then_inc(pt_taken, 1)

            def win_out(u):
                n, kv = divmod(u, 2)
                fn(A[:, ATT + 2 * kv:ATT + 2 * kv + 2, n * P:(n + 1) * P],
                   ps[:, 6, 0:2 * P].rearrange("p (c t) -> p c t", c=2), ACT.Copy).then_inc(o_taken, 1)

            attention(0, UNITS, win_exps, win_turned, win_out, lambda u: row_out(u // 2 + 2) if u % 2 else None)
            act.wait_ge(o_taken, UNITS)
            norm("heads", lambda j: plane(ATT + j) if j < 4 else zv[:, j - 4, 2:T + 2],
                 lambda j: act.wait_ge(conv_ready, j - 3) if j >= 4 else None, HD, 1e-6)
            high("mix", lambda j: plane(MIX + j),
                 lambda j: act.wait_ge(scaled_ready, SCALED["heads"] + j + 1))
            for j in range(KC):
                take("w_out", j, plane(PQ + j), ACT.Identity, bias=col("b_out", j))
            norm("norm2", lambda j: X[:, j, :], lambda j: act.wait_ge(residual_ready, RES["w_out"] + j + 1), D, 1e-6)
            act.wait_ge(ada_ready, 5)
            high("norm2", lambda j: plane(TMPH + j), lambda j: act.wait_ge(scaled_ready, SCALED["norm2"] + j + 1),
                 ACT.Identity, bias=lambda j: ada_col(SHIFT2, j))
            act.dma_start(plane(POS).bitcast(I32), positions).then_inc(pos_loaded, 16)
            for j in range(16):
                take("w_query", j, plane(STAGE + j))

            for t in range(2):
                for tb in range(TB):
                    for f in range(2):
                        take("keys", t * 8 + tb * 2 + f, plane(SCORES + 4 * tb + 2 * t + f))
            def gelu_one(n0, s, i=0, waits=True):
                n, p = n0 + s, PROD["up"] + n0 + s
                if waits:
                    act.wait_ge(gelu_stored[s], i * 16 + 16 * (n // 2))
                act.wait_ge(product_ready, i * 2 + p + 1)
                fn(plane(GELU + s), ps[:, p % 2, :], ACT.Gelu).then_inc(bank_free, 1)
                act.wait_ge(bank_free, i * 2 + 2 + p + 1)
                act.dma_start(gelu_map[bass.ds(i * 2 + n, 1)].rearrange("i j t -> j i t"),
                              A[:, GELU + s:GELU + s + 1, :]).then_inc(gelu_stored[s], 16)

            def gelu_out(n0, i=0, waits=True):
                for s in range(2):
                    gelu_one(n0, s, i, waits)

            def store_gates(tb, q):
                act.wait_ge(gate_bank_free, 2 + 32 * (tb + 1))
                r = slice(q * NKEY // 4, (q + 1) * NKEY // 4)
                act.dma_start(gate_map[r].rearrange("i j t -> j i t")[:, :, tb * P:(tb + 1) * P], staging[:, r, :])\
                    .then_inc(gate_stored, 16)

            ps_gates = ps[:, 6:8, :].rearrange("p b (t i) -> p b i t", t=4)
            done = 0
            for tb in range(TB):
                if tb == 0:
                    gelu_out(0, waits=False)
                for q in range(4 if tb else 0):
                    gelu_one(done + q // 2 * 2, q % 2)
                    store_gates(tb - 1, q)
                with act.Fori(2 if tb else 1, EARLY // 2) as i:
                    gelu_out(done, i)
                done += EARLY
                act.wait_ge(gate_in, tb + 1)
                g_ap = routed[:, 2, :]
                fn(g_ap, g_ap, ACT.Exp).then_inc(gate_exp, 1)
                act.wait_ge(route_turned, tb + 1)
                fn(turned[:], ps[:, 2, 0:3 * P].rearrange("p (a t) -> p a t", a=3), ACT.Copy).then_inc(route_taken, 1)
                if tb == 0:
                    act.wait_ge(bank_free, 2 + PROD["keys"] + 16)
                else:
                    act.wait_ge(gate_stored, 64 * tb)
                toks = P // AMONG[tb]
                with act.Fori(0, AMONG[tb] // 2) as i:
                    for s in range(2):
                        for b in range(toks // 4):
                            at = s * toks + 4 * b
                            act.wait_ge(onehot_free, i * (2 * toks) + 4 + tb * P + at + 4)
                            fn(staging[:, :, bass.ds(i * (2 * toks) + at, 4)], ps_gates[:, b % 2, :, :], ACT.Copy)\
                                .then_inc(gate_bank_free, 1)
                        gelu_one(done, s, i)
                done += AMONG[tb]

            act.wait_ge(rope_in, 1)
            fn(plane(SIN), plane(SIN), ACT.Sin)
            fn(plane(COS), plane(COS), ACT.Sin).then_inc(rope_out, 1)

            def load_mixed(s, m, i=0):
                for planes, source in ((UR, gelu_map), (GR, gate_map)):
                    act.dma_start(A[:, planes + s:planes + s + 1, :], source[bass.ds(i * 8 + m, 1)]
                                  .rearrange("i j t -> j i t")).then_inc(ring_loaded[s], 16)

            def high_mixed(n, i=0, load=True):
                act.wait_ge(mixed_ready, i * 8 + n + 1)
                if n >= 4:
                    act.wait_ge(tiles_started, i * 8 + FIRST["down"] + n - 2)
                fn(hi("mixed", n % 4), plane(UR + n % 8), ACT.Copy).then_inc(mixed_hi, 1)
                if load and n >= 4:
                    act.wait_ge(mixed_lo, i * 8 + n - 3)
                    load_mixed((n + 4) % 8, n + 4, i)

            last = NKEY - 8
            assert done == last
            for q in range(4):
                gelu_one(last + q // 2 * 2, q % 2)
                store_gates(TB - 1, q)
            gelu_out(last + 4)
            act.wait_ge(gate_stored, 64 * TB)
            for s in range(8):
                load_mixed(s, s)
            gelu_out(last + 6)
            for n in range(4):
                high_mixed(n)
            for s in range(2):
                act.wait_ge(gelu_stored[s], 16 * NKEY // 2)
            for n in range(4, 8):
                high_mixed(n)
            with act.Fori(0, NKEY // 8 - 2) as i:
                for n in range(8, 16):
                    high_mixed(n, i)
            for n in range(last, NKEY):
                high_mixed(n, load=n + 4 < NKEY)
            norm("final", lambda j: X[:, j, :], lambda j: act.wait_ge(residual_ready, RES["peer"] + j + 1), D, 1e-6)

            high("x_mla", lambda j: X[:, j, :], lambda j: act.wait_ge(scaled_ready, SCALED["final"] + j + 1))
            for j in range(6):
                take("dqkv", j, plane(DOWN + j))
            norm("cq", lambda j: plane(DOWN + j), lambda j: act.wait_ge(bank_free, 2 + PROD["dqkv"] + j + 1), 256, 1e-6)
            norm("ckv", lambda j: plane(DOWN + 2 + j), lambda j: act.wait_ge(bank_free, 2 + PROD["dqkv"] + 2 + j + 1), 256,
                 1e-6)
            high("cq", lambda j: plane(CQN + j), lambda j: act.wait_ge(scaled_ready, SCALED["cq"] + j + 1))
            high("ckv", lambda j: plane(CKN + j), lambda j: act.wait_ge(scaled_ready, SCALED["ckv"] + j + 1))
            for j in range(16):
                take("uq", j, plane(QN + j))
            for j in range(8):
                take("uk", j, plane(KN + j))
            for j in range(8):
                take("uv", j, plane(VM + j))

            scale = 192 ** -0.5

            def mla_exps(m):
                n, pair = divmod(m, 4)
                act.wait_ge(shift_ready, UNITS + m + 1)
                if m >= 2:
                    act.wait_ge(pt_ready, UNITS + m - 1)
                for g in range(2):
                    last = fn(A[:, MPROBS[m % 2] + g, 0:(n + 1) * P], ps[:, 2 + g, 0:(n + 1) * P], ACT.Exp,
                              bias=sm(m, g), scale=scale, accum_out=sm(m, 12 + g))
                last.then_inc(exp_ready, 1)

            def mla_turned(m):
                w = (m // 4 + 1) * P
                fn(A[:, MPT[m % 2]:MPT[m % 2] + 2, 0:w], ps[:, 4:6, 0:w], ACT.Copy).then_inc(pt_taken, 1)

            def mla_out(m):
                n, pair = divmod(m, 4)
                fn(A[:, OM + 2 * pair:OM + 2 * pair + 2, n * P:(n + 1) * P],
                   ps[:, 6, 0:2 * P].rearrange("p (c t) -> p c t", c=2), ACT.Copy).then_inc(o_taken, 1)

            attention(UNITS, 16, mla_exps, mla_turned, mla_out)
            high("o_mla", lambda j: plane(OM + j), lambda j: act.wait_ge(o_taken, UNITS + 16))
            for j in range(KC):
                take("w_o", j, plane(TMPO + j))

            def layer_norm(name, g, b):
                i = LN[name]
                norm(name, lambda j: plane(CENTER + j), lambda j: act.wait_ge(centered_ready, KC * i + j + 1), D, 1e-5)
                bias = [col(b, KC * int(name[-1]) + j) for j in range(KC)]
                high(name, lambda j: X[:, j, :], lambda j: act.wait_ge(scaled_ready, SCALED[name] + j + 1), ACT.Identity,
                     bias=lambda j: bias[j])
                for j in range(KC):
                    act.wait_ge(lo_ready, SPL[name] + j + 1)
                    fn(X[:, j, :], X[:, j, :], ACT.Identity, bias=bias[j]).then_inc(h_ready, 1)

            def ffn_and_ple(f):
                act.wait_ge(residual_ready, RES[AFTER[f"mix{f}"]] + KC)
                act.dma_start(A[:, PRAW:PRAW + 2, :], ple_in[f]).then_inc(p_loaded, 16)
                layer_norm(f"mix{f}", "ln_mix_g", "ln_mix_b")
                with act.Fori(0, FF // 2) as i:
                    for j in range(2):
                        p = PROD[f"ffn_in{f}"] + 2 * j
                        act.wait_ge(product_ready, i * 4 + p + 1)
                        fn(plane(SG + j), ps[:, p % 2, :], ACT.Silu).then_inc(bank_free, 1)
                        act.wait_ge(product_ready, i * 4 + p + 2)
                        fn(plane(UU + j), ps[:, (p + 1) % 2, :], ACT.Copy).then_inc(bank_free, 1)
                        act.wait_ge(ff_ready, i * 2 + FF * f + j + 1)
                        fn(parts[f"ff{f}"][0][:, bass.ds(i * 2 + j, 1), :], gated[:, j:j + 1, :], ACT.Copy)\
                            .then_inc(hi_ready, 1)
                for j in range(KC):
                    take(f"ffn_down{f}", j, plane(TMPD + j))
                layer_norm(f"ffn{f}", "ln_ffn_g", "ln_ffn_b")
                high(f"p{f}", lambda j: plane(PRAW + j), lambda j: act.wait_ge(p_loaded, 16 * (f + 1)))
                for j in range(KC):
                    take(f"ple_gate{f}", j, plane(TMPG + j), ACT.Sigmoid)
                for j in range(KC):
                    take(f"ple_proj{f}", j, plane(TMPP + j))

            ffn_and_ple(0)

            high("x_hgrn", lambda j: X[:, j, :], lambda j: act.wait_ge(residual_ready, RES["ple0"] + j + 1))
            for j in range(8):
                take("hgrn_in", j, plane(HQ + j), ACT.Silu)
            for j in range(8):
                p = PROD["hgrn_in"] + 8 + j
                act.wait_ge(product_ready, p + 1)
                fn(plane(HLF + j), ps[:, p % 2, :], ACT.Sigmoid)
                fn(plane(HK + j), ps[:, p % 2, :], ACT.Sigmoid, scale=-1.0).then_inc(bank_free, 1)
            for h in range(HEADS):
                act.wait_ge(forget_in, h + 1)
                fn(plane(HLF + h), plane(HLF + h), ACT.Ln).then_inc(log_ready, 1)
            for h in range(HEADS):
                take("hgrn_in", 16 + h, plane(HV + h))
                act.wait_ge(cum_ready, h + 1)
                fn(plane(HLF + h), plane(HG + h), ACT.Exp).then_inc(decay_ready, 1)
                act.wait_ge(decay_in, h + 1)
                fn(plane(HKH + h), plane(HKH + h), ACT.Exp).then_inc(decay_ready, 1)
            ends = A[:, HG:HG + 8, :].rearrange("p h (c t) -> p h c t", c=NCH)[:, :, :, CH - 1]
            fn(dec[:], ends, ACT.Exp).then_inc(decay_ready, 1)
            for j in range(8):
                take("hgrn_in", 24 + j, plane(HGT + j), ACT.Silu)
            for h in range(HEADS):
                act.wait_ge(kt_ready, h + 1)
                fn(plane(HKT + h), ps[:, 2 + h % 2, :], ACT.Copy).then_inc(kt_taken, 1)
            for h in range(HEADS):
                for lv in range(LEVELS):
                    e = h * LEVELS + lv
                    act.wait_ge(gap_ready, e + 1)
                    fn(plane(HE + e % 4), plane(HE + e % 4), ACT.Exp).then_inc(gap_exp, 1)
                if h:
                    act.wait_ge(intra_ready, (LEVELS + 1) * h)
                    fn(plane(HO + h - 1), ps[:, 4 + (h - 1) % 2, :], ACT.Copy).then_inc(intra_taken, 1)
            act.wait_ge(intra_ready, (LEVELS + 1) * HEADS)
            fn(plane(HO + HEADS - 1), ps[:, 4 + (HEADS - 1) % 2, :], ACT.Copy).then_inc(intra_taken, 1)
            norm("hgrn", lambda j: plane(HO + j), lambda j: act.wait_ge(inter_added, NCH - 1), P, 1e-6)
            high("o_hgrn", lambda j: plane(HO + j), lambda j: act.wait_ge(gated_ready, j + 1))
            for j in range(KC):
                take("hgrn_o", j, plane(TMPO + j))
            ffn_and_ple(1)

        @block.vector
        def _(dve):
            v = nc.vector
            own = Steps(dve, dve_step)

            def taken(name, j):
                dve.wait_ge(bank_free, 2 + PROD[name] + j + 1)

            def inverse(name):
                dve.wait_ge(root_ready, NGROUP[name] + 1)
                r = A[0:32 if name in PACKED else P, NORM[name][1], :]
                v.reciprocal(r, r).then_inc(rstd_ready, 1)

            def scaled(name, j, src, gain, dst):
                if name in PACKED:
                    rstd = ps[:, 4 + j % 2, :]
                    dve.wait_ge(spread_ready, KC * list(PACKED).index(name) + j + 1)
                else:
                    rstd = plane(NORM[name][1])
                    dve.wait_ge(rstd_ready, NGROUP[name] + 1)
                v.scalar_tensor_tensor(out=dst, in0=src, scalar=gain, in1=rstd, op0=ALU.mult, op1=ALU.mult)\
                    .then_inc(scaled_ready, 1)

            def low(name, j, src, shift=None):
                dve.wait_ge(hi_ready, SPL[name] + j + 1)
                h = hi(name, j).bitcast(F32)
                if shift is None:
                    ins = v.tensor_tensor(lo(name, j), src, h, ALU.subtract)
                else:
                    ins = v.scalar_tensor_tensor(out=lo(name, j), in0=src, scalar=shift, in1=h, op0=ALU.add,
                                                 op1=ALU.subtract)
                ins.then_inc(lo_ready, 1)

            def behind(n, step, then):
                for j in range(n + 1):
                    if j < n:
                        step(j)
                    if j:
                        then(j - 1)

            own.do(v.memset(eps[:, 0:1], 1e-6))
            own.do(v.memset(eps[:, 1:2], 1e-5))
            own.do(v.memset(ones[:], 1.0))
            own.wait()
            dve.sem_inc(ones_ready, 1)
            dve.wait_ge(inputs_loaded, 16 * 2)

            lb0, lb1 = col("lb", 0, 8), col("lb", 8, 8)
            t0, t1, t2 = small[:, 32:40], small[:, 40:48], small[:, 48:56]
            own.do(v.tensor_tensor(t0, lb0, lb1, ALU.max))
            own.wait()
            own.do(v.tensor_tensor(t1, lb0, t0, ALU.subtract))
            v.tensor_tensor(t2, lb1, t0, ALU.subtract).then_inc(lb_in, 1)
            own.wait()
            dve.wait_ge(lb_exp, 1)
            own.do(v.tensor_tensor(t0, t1, t2, ALU.add))
            own.wait()
            own.do(v.reciprocal(t0, t0))
            own.wait()
            own.do(v.tensor_tensor(t1, t1, t0, ALU.mult))
            own.do(v.tensor_tensor(t2, t2, t0, ALU.mult))
            own.wait()
            own.do(v.tensor_tensor(t2, t1, t2, ALU.add))
            own.wait()
            own.do(v.tensor_tensor(small[:, LB:LB + 8], t2, t1, ALU.subtract))
            own.wait()
            own.do(v.tensor_scalar(small[:, OMLB:OMLB + 8], small[:, LB:LB + 8], -1.0, 1.0, ALU.mult, ALU.add))

            def ada_take(part):
                dve.wait_ge(ada_sums, part + 1)
                v.tensor_tensor(ada_col(8 * part, 0, 8), ps[:, 0, 8 * part:8 * part + 8], col("b_ada", 8 * part, 8),
                                ALU.add).then_inc(ada_ready, 1)

            def modulation(part, at, gain):
                dve.wait_ge(ada_ready, at)
                own.do(v.scalar_tensor_tensor(out=small[:, GS1:GS1 + 8], in0=ada_col(part, 0, 8), scalar=1.0,
                                              in1=col(gain, 0, 8), op0=ALU.add, op1=ALU.mult))
                own.wait()

            inverse("norm1")
            ada_take(0)
            ada_take(1)
            modulation(SCALE1, 2, "norm1_g")
            behind(KC, lambda j: scaled("norm1", j, X[:, j, :], small[:, GS1 + j:GS1 + j + 1], plane(TMPH + j)),
                   lambda j: low("norm1", j, plane(TMPH + j), ada_col(SHIFT1, j)))

            taken("w_in", 18)
            pv3 = plane(PV).rearrange("p (b c) -> p b c", b=TB)
            v.tensor_tensor(pv3, pv3, col("b_v", 0, P).unsqueeze(1).broadcast_to([P, TB, P]), ALU.add)\
                .then_inc(bias_ready, 1)
            dve.wait_ge(consts_ready, 1)

            def win_shift(u):
                n, kv = divmod(u, 2)
                lo = P if n == 0 else 0
                dve.wait_ge(scores_ready, u + 1)
                s = ps[:, 2:4, :].rearrange("p b (h k) -> p (b h) k", h=2)[:, :, lo:2 * P]
                own.do(v.scalar_tensor_tensor(out=s, in0=s, scalar=HD ** -0.5,
                                              in1=win_mask[:, lo:2 * P].unsqueeze(1).broadcast_to([P, 4, 2 * P - lo]),
                                              op0=ALU.mult, op1=ALU.add))
                own.wait()
                own.do(v.tensor_reduce(sm(u, 0, 4), s, AX, ALU.max))
                own.wait()
                own.do(v.tensor_tensor(sm(u, 0, 4), sm(u, 0, 4), col("sinks", 4 * kv, 4), ALU.max))
                own.wait()
                own.do(v.tensor_tensor(sm(u, 4, 4), col("sinks", 4 * kv, 4), sm(u, 0, 4), ALU.subtract))
                v.tensor_scalar(sm(u, 0, 4), sm(u, 0, 4), -1.0, None, ALU.mult).then_inc(shift_ready, 1)

            def win_probs(u):
                n, kv = divmod(u, 2)
                lo = P if n == 0 else 0
                dve.wait_ge(exp_ready, u + 1)
                own.do(v.tensor_tensor(sm(u, 12, 4), sm(u, 12, 4), sm(u, 8, 4), ALU.add))
                own.wait()
                own.do(v.reciprocal(sm(u, 12, 4), sm(u, 12, 4)))
                own.wait()
                pv = A[:, PROBS[u % 2]:PROBS[u % 2] + 2, :].rearrange("p a (h k) -> p (a h) k", h=2)[:, :, lo:2 * P]
                v.tensor_tensor(pv, pv, sm(u, 12, 4).unsqueeze(2).broadcast_to([P, 4, 2 * P - lo]), ALU.mult)\
                    .then_inc(probs_ready, 1)

            win_shift(0)
            for u in range(UNITS):
                win_probs(u)
                if u + 1 < UNITS:
                    win_shift(u + 1)
                if u == 0:
                    own.do(v.memset(zv[:, :, 0:2], 0.0))
                    own.do(v.tensor_tensor(zv[:, :, 2:T + 2], A[:, PCG:PCG + 4, :], A[:, PU:PU + 4, :], ALU.mult))
                    z_step = own.n
                if u and u % 2 == 0:
                    ada_take(u // 2 + 1)
                if 1 <= u <= 4:
                    j = u - 1
                    own.wait(z_step)
                    cp = plane(PU + j)
                    own.do(v.tensor_scalar(cp, zv[:, j, 2:T + 2], col("conv_w", 8 + j), None, ALU.mult))
                    own.wait()
                    own.do(v.scalar_tensor_tensor(out=cp, in0=zv[:, j, 1:T + 1], scalar=col("conv_w", 4 + j), in1=cp,
                                                  op0=ALU.mult, op1=ALU.add))
                    own.wait()
                    own.do(v.scalar_tensor_tensor(out=cp, in0=zv[:, j, 0:T], scalar=col("conv_w", j), in1=cp,
                                                  op0=ALU.mult, op1=ALU.add))
                    own.wait()
                    v.tensor_tensor(zv[:, j, 2:T + 2], cp, plane(PB_ + j), ALU.mult).then_inc(conv_ready, 1)
            ada_take(5)
            own.do(v.tensor_copy(spread_halves.rearrange("p j (a m) -> p (j a) m", a=2),
                                 ident[0:32, 0:32].rearrange("p (q b) -> p q b", b=2)[:, :, 0:1]
                                 .broadcast_to([32, 16, 64])))
            own.wait()
            inverse("heads")
            dve.wait_ge(conv_ready, 4)
            behind(KC, lambda j: scaled("heads", j, plane(ATT + j) if j < 4 else zv[:, j - 4, 2:T + 2],
                                        par[:, COL["attn_out_g"] + j:COL["attn_out_g"] + j + 1], plane(MIX + j)),
                   lambda j: low("mix", j, plane(MIX + j)))
            dve.wait_ge(ada_ready, 3)

            for j in range(KC):
                taken("w_out", j)
                v.scalar_tensor_tensor(out=X[:, j, :], in0=plane(PQ + j), scalar=ada_col(GATE1, j), in1=X[:, j, :],
                                       op0=ALU.mult, op1=ALU.add).then_inc(residual_ready, 1)
            modulation(SCALE2, 5, "norm2_g")
            inverse("norm2")
            dve.wait_ge(residual_ready, RES["w_out"] + KC)
            behind(KC, lambda j: scaled("norm2", j, X[:, j, :], small[:, GS1 + j:GS1 + j + 1], plane(TMPH + j)),
                   lambda j: low("norm2", j, plane(TMPH + j), ada_col(SHIFT2, j)))

            best = accf[:, 0:256].rearrange("p (h k) -> p h k", h=16)
            best_at = accf[:, 256:512].rearrange("p (h k) -> p h k", h=16)
            best_i = best_at.bitcast(U32)
            best_f = accf[:, 512:768].rearrange("p (h k) -> p h k", h=16)
            top = accf[:, 768:896].rearrange("p (h k) -> p h k", h=8)
            top_i = accf[:, 896:1024].bitcast(U32)
            hi_i = accf[:, 1024:1152].bitcast(U32)
            lo_i = accf[:, 1152:1280].bitcast(U32)
            place1 = accf[:, 1280:1408]
            place2 = accf[:, 1408:1536]
            total = accf[:, 1536:1544]

            def route(tb):
                four = A[:, SCORES + 4 * tb:SCORES + 4 * tb + 4, :].rearrange("p a t -> p (a t)")
                s = four.rearrange("p (h n) -> p h n", h=16)
                taken("keys", 8 + tb * 2 + 1)
                for h in range(16):
                    own.do(v.max(best[:, h, 0:8], s[:, h, :]))
                own.wait()
                for h in range(16):
                    own.do(v.max_index(best_i[:, h, 0:8], best[:, h, 0:8], s[:, h, :]))
                own.wait()
                for h in range(16):
                    own.do(v.match_replace(out=s[:, h, :], in_to_replace=best[:, h, 0:8], in_values=s[:, h, :],
                                           imm_value=LOWEST))
                own.wait()
                for h in range(16):
                    own.do(v.max(best[:, h, 8:16], s[:, h, :]))
                own.wait()
                for h in range(16):
                    own.do(v.max_index(best_i[:, h, 8:16], best[:, h, 8:16], s[:, h, :]))
                own.wait()
                own.do(v.tensor_copy(best_f, best_i))
                pair = best.rearrange("p (h f) k -> p h f k", f=2)
                cand4 = four.rearrange("p (h a b) -> p h a b", h=8, a=TOPK)
                cand = four.rearrange("p (h n) -> p h n", h=8)
                for h in range(8):
                    own.do(v.tensor_tensor(cand4[:, h], pair[:, h, 0, :].unsqueeze(2).broadcast_to([P, TOPK, TOPK]),
                                           pair[:, h, 1, :].unsqueeze(1).broadcast_to([P, TOPK, TOPK]), ALU.add))
                own.wait()
                top_iv = top_i.rearrange("p (h k) -> p h k", h=8)
                for h in range(8):
                    own.do(v.max(top[:, h, 0:8], cand[:, h, :]))
                own.wait()
                for h in range(8):
                    own.do(v.max_index(top_iv[:, h, 0:8], top[:, h, 0:8], cand[:, h, :]))
                own.wait()
                for h in range(8):
                    own.do(v.match_replace(out=cand[:, h, :], in_to_replace=top[:, h, 0:8], in_values=cand[:, h, :],
                                           imm_value=LOWEST))
                own.wait()
                for h in range(8):
                    own.do(v.max(top[:, h, 8:16], cand[:, h, :]))
                own.wait()
                for h in range(8):
                    own.do(v.max_index(top_iv[:, h, 8:16], top[:, h, 8:16], cand[:, h, :]))
                g_ap = routed[:, 2, :].rearrange("p (h k) -> p h k", h=8)
                if tb:
                    dve.wait_ge(route_turned, tb)
                v.tensor_tensor(g_ap, top, top[:, :, 0:1].broadcast_to([P, 8, TOPK]), ALU.subtract)\
                    .then_inc(gate_in, 1)
                own.wait()
                own.do(v.tensor_scalar(hi_i, top_i, 4, None, ALU.logical_shift_right))
                own.do(v.tensor_scalar(lo_i, top_i, 15, None, ALU.bitwise_and))
                own.wait()
                own.do(v.tensor_copy(place1, hi_i))
                own.do(v.tensor_copy(place2, lo_i))
                own.wait()
                pick = four.rearrange("p (h k a) -> p h k a", h=8, k=TOPK)
                pick3 = four.rearrange("p (q a) -> p q a", a=TOPK)
                bf = best_f.rearrange("p (h f) k -> p h f k", f=2)
                for f, place in enumerate((place1, place2)):
                    own.do(v.tensor_tensor(pick3, place.unsqueeze(2).broadcast_to([P, P, TOPK]),
                                           iota[:, 0:TOPK].unsqueeze(1).broadcast_to([P, P, TOPK]), ALU.is_equal))
                    own.wait()
                    own.do(v.tensor_tensor(pick, pick, bf[:, :, f, :].unsqueeze(2).broadcast_to([P, 8, TOPK, TOPK]),
                                           ALU.mult))
                    own.wait()
                    own.do(v.tensor_reduce(routed[:, f, :], pick3, AX, ALU.add))
                    own.wait()
                dve.wait_ge(gate_exp, tb + 1)
                own.do(v.tensor_reduce(total, g_ap, AX, ALU.add))
                own.wait()
                own.do(v.reciprocal(total, total))
                own.wait()
                v.tensor_tensor(g_ap, g_ap, total.unsqueeze(2).broadcast_to([P, 8, TOPK]), ALU.mult)\
                    .then_inc(route_ready, 1)

            for tb in range(TB):
                route(tb)
                dve.wait_ge(route_taken, tb + 1)
                with dve.Fori(0, P // 8) as i:
                    for s in range(8):
                        tok = tb * P + s
                        dve.wait_ge(onehot_free, i * 8 + tok + 1)
                        t = bass.ds(i * 8 + s, 1)
                        v.tensor_scalar(hot2[:, s % 4, :], iota[:], turned[:, 1, t], None, ALU.is_equal)
                        v.tensor_scalar(hot1[:, s % 4, :], iota[:], turned[:, 0, t], turned[:, 2, t], ALU.is_equal,
                                        ALU.mult).then_inc(onehot_ready, 1)

            ang, k, r = plane(ANG), plane(ANG + 1), plane(SIN)
            dve.wait_ge(pos_loaded, 16)
            own.do(v.tensor_copy(ang, plane(POS).bitcast(I32)))
            own.wait()
            own.do(v.tensor_scalar(ang, ang, col("inv_freq"), None, ALU.mult))
            own.wait()
            own.do(v.tensor_scalar(k, ang, 1.0 / (2.0 * np.pi), None, ALU.mult))
            own.wait()
            own.do(v.tensor_scalar(k, k, ROUND, None, ALU.add))
            own.wait()
            own.do(v.tensor_scalar(k, k, -ROUND, None, ALU.add))
            own.wait()
            for c in TWO_PI:
                own.do(v.scalar_tensor_tensor(out=ang, in0=k, scalar=-c, in1=ang, op0=ALU.mult, op1=ALU.add))
                own.wait()
            own.do(v.tensor_scalar(ang, ang, float(np.float32(3.1415925)), float(np.float32(-3.1415925)), ALU.min,
                                   ALU.max))
            own.wait()
            own.do(v.tensor_scalar(r, ang, 1.0, None, ALU.mult))
            own.do(v.scalar_tensor_tensor(out=k, in0=ang, scalar=-1.0, in1=ang, op0=ALU.mult, op1=ALU.max))
            own.wait()
            v.tensor_scalar(plane(COS), k, -1.0, float(np.pi / 2), ALU.mult, ALU.add).then_inc(rope_in, 1)
            dve.wait_ge(rope_out, 1)
            own.do(v.tensor_scalar(plane(SIN), plane(SIN), col("sin_sign"), None, ALU.mult))

            def mix(n, i=0):
                dve.wait_ge(ring_loaded[n % 8], i * 32 + 32 * (n // 8 + 1))
                a = plane(UR + n % 8)
                v.tensor_tensor(a, a, plane(GR + n % 8), ALU.mult).then_inc(mixed_ready, 1)

            def low_mixed(n, i=0):
                dve.wait_ge(mixed_hi, i * 8 + n + 1)
                v.tensor_tensor(lo("mixed", n % 4), plane(UR + n % 8), hi("mixed", n % 4).bitcast(F32), ALU.subtract)\
                    .then_inc(mixed_lo, 1)

            mix(0)
            with dve.Fori(0, NKEY // 8 - 1) as i:
                for n in range(8):
                    mix(n + 1, i)
                    low_mixed(n, i)
            for n in range(NKEY - 8, NKEY):
                if n + 1 < NKEY:
                    mix(n + 1)
                low_mixed(n)
            for j in range(KC):
                dve.wait_ge(sums_ready, j + 1)
                v.scalar_tensor_tensor(out=X[:, j, :], in0=ps[:, j, :], scalar=ada_col(GATE2, j), in1=X[:, j, :],
                                       op0=ALU.mult, op1=ALU.add).then_inc(residual_ready, 1)

            inverse("final")
            dve.wait_ge(residual_ready, RES["peer"] + KC)
            behind(KC, lambda j: scaled("final", j, X[:, j, :], col("final_g", j), X[:, j, :]),
                   lambda j: low("x_mla", j, X[:, j, :]))

            inverse("cq")
            for j in range(2):
                scaled("cq", j, plane(DOWN + j), col("q_norm", j), plane(CQN + j))
            inverse("ckv")
            for j in range(2):
                scaled("ckv", j, plane(DOWN + 2 + j), col("kv_norm", j), plane(CKN + j))
            for name, first in (("cq", CQN), ("ckv", CKN)):
                for j in range(2):
                    low(name, j, plane(first + j))

            def rope(main, swapped, n):
                a, b = A[:, main:main + n, :], A[:, swapped:swapped + n, :]
                own.wait()
                own.do(v.tensor_tensor(a, a, plane(COS).unsqueeze(1).broadcast_to([P, n, T]), ALU.mult))
                own.do(v.tensor_tensor(b, b, plane(SIN).unsqueeze(1).broadcast_to([P, n, T]), ALU.mult))
                own.wait()
                v.tensor_tensor(a, a, b, ALU.add).then_inc(rope_ready, 1)

            taken("dqkv", 5)
            rope(DOWN + 4, DOWN + 5, 1)
            taken("uq", 15)
            rope(QR, QS, 4)

            scale = 192 ** -0.5

            def mla_shift(m):
                n, pair = divmod(m, 4)
                dve.wait_ge(scores_ready, UNITS + m + 1)
                d = ps[:, 2:4, n * P:(n + 1) * P]
                own.do(v.tensor_tensor(d, d, diag_mask[:].unsqueeze(1).broadcast_to([P, 2, P]), ALU.add))
                own.wait()
                own.do(v.tensor_reduce(sm(m, 0, 2), ps[:, 2:4, 0:(n + 1) * P], AX, ALU.max))
                own.wait()
                v.tensor_scalar(sm(m, 0, 2), sm(m, 0, 2), -scale, None, ALU.mult).then_inc(shift_ready, 1)

            def mla_probs(m):
                n, pair = divmod(m, 4)
                dve.wait_ge(exp_ready, UNITS + m + 1)
                own.do(v.reciprocal(sm(m, 12, 2), sm(m, 12, 2)))
                own.wait()
                for g in range(2):
                    a = A[:, MPROBS[m % 2] + g, 0:(n + 1) * P]
                    last = v.tensor_scalar(a, a, sm(m, 12 + g), None, ALU.mult)
                last.then_inc(probs_ready, 1)

            mla_shift(0)
            for m in range(16):
                mla_probs(m)
                if m + 1 < 16:
                    mla_shift(m + 1)

            for j in range(KC):
                low("o_mla", j, plane(OM + j))

            def residual(stage, tmp):
                for j in range(KC):
                    taken(stage, j)
                    v.scalar_tensor_tensor(out=X[:, j, :], in0=X[:, j, :], scalar=ALPHA, in1=plane(tmp + j),
                                           op0=ALU.mult, op1=ALU.add).then_inc(residual_ready, 1)

            def layer_norm(name, gain, bias):
                i = LN[name]
                dve.wait_ge(mean_ready, i + 1)
                dve.wait_ge(residual_ready, RES[AFTER[name]] + KC)
                for j in range(KC):
                    v.scalar_tensor_tensor(out=plane(CENTER + j), in0=ps[:, 4, :], scalar=-1.0 / D, in1=X[:, j, :],
                                           op0=ALU.mult, op1=ALU.add).then_inc(centered_ready, 1)
                inverse(name)
                dve.wait_ge(centered_ready, KC * (i + 1))
                behind(KC, lambda j: scaled(name, j, plane(CENTER + j), col(gain, KC * int(name[-1]) + j), X[:, j, :]),
                       lambda j: low(name, j, X[:, j, :], col(bias, KC * int(name[-1]) + j)))

            def ffn_and_ple(f):
                layer_norm(f"mix{f}", "ln_mix_g", "ln_mix_b")
                ff_hi, ff_lo = parts[f"ff{f}"]
                with dve.Fori(0, FF // 2) as i:
                    for j in range(2):
                        dve.wait_ge(bank_free, i * 4 + 2 + PROD[f"ffn_in{f}"] + 2 * j + 2)
                        v.tensor_tensor(gated[:, j, :], plane(SG + j), plane(UU + j), ALU.mult).then_inc(ff_ready, 1)
                        dve.wait_ge(hi_ready, i * 2 + SPL[f"ff{f}"] + j + 1)
                        v.tensor_tensor(ff_lo[:, bass.ds(i * 2 + j, 1), :], gated[:, j:j + 1, :],
                                        ff_hi[:, bass.ds(i * 2 + j, 1), :].bitcast(F32), ALU.subtract)\
                            .then_inc(lo_ready, 1)
                dve.wait_ge(h_ready, KC * LN[f"mix{f}"] + KC)
                residual(f"ffn_down{f}", TMPD)
                layer_norm(f"ffn{f}", "ln_ffn_g", "ln_ffn_b")
                for j in range(2):
                    low(f"p{f}", j, plane(PRAW + j))

                dve.wait_ge(h_ready, KC * LN[f"ffn{f}"] + KC)

                def add_ple(j):
                    taken(f"ple_proj{f}", j)
                    own.do(v.tensor_tensor(plane(TMPP + j), plane(TMPP + j), plane(TMPG + j), ALU.mult))
                    own.wait()
                    v.tensor_tensor(X[:, j, :], X[:, j, :], plane(TMPP + j), ALU.add).then_inc(residual_ready, 1)

                behind(KC, add_ple, lambda j: low("x_hgrn", j, X[:, j, :]) if f == 0 else None)

            residual("w_o", TMPO)
            ffn_and_ple(0)

            for h in range(HEADS):
                taken("hgrn_in", 8 + h)
                lf = plane(HLF + h)
                own.do(v.tensor_scalar(lf, lf, small[:, OMLB + h:OMLB + h + 1], small[:, LB + h:LB + h + 1], ALU.mult,
                                       ALU.add))
                own.do(v.tensor_scalar(plane(HK + h), plane(HK + h), small[:, OMLB + h:OMLB + h + 1], None, ALU.mult))
                own.wait()
                v.tensor_scalar(lf, lf, 2.0 ** -63, None, ALU.max).then_inc(forget_in, 1)
            for h in range(HEADS):
                dve.wait_ge(log_ready, h + 1)
                v.tensor_tensor_scan(plane(HG + h), scan_keep[:], plane(HLF + h), 0.0, ALU.mult, ALU.add)\
                    .then_inc(cum_ready, 1)
                dve.wait_ge(cum_ready, h + 1)
                g4 = plane(HG + h).rearrange("p (c t) -> p c t", c=NCH)
                v.tensor_tensor(plane(HKH + h).rearrange("p (c t) -> p c t", c=NCH),
                                g4[:, :, CH - 1:CH].broadcast_to([P, NCH, CH]), g4, ALU.subtract)\
                    .then_inc(decay_in, 1)
            for h in range(HEADS):
                dve.wait_ge(decay_ready, 2 * h + 2)
                own.do(v.tensor_tensor(plane(HLF + h), plane(HLF + h), plane(HQ + h), ALU.mult))
                v.tensor_tensor(plane(HKH + h), plane(HKH + h), plane(HK + h), ALU.mult).then_inc(khat_ready, 1)

            def by_level(ap, lv):
                return ap.rearrange("p (b two m) -> p b two m", two=2, m=2 ** lv)

            def make_level(e):
                h, lv = divmod(e, LEVELS)
                dve.wait_ge(gap_exp, e + 1)
                if e >= 2:
                    last_unit = ((e - 2) // LEVELS) * (LEVELS + 1) + (e - 2) % LEVELS
                    dve.wait_ge(pair_ready, last_unit + 1)
                m, x = by_level(plane(HM + e % 2), lv), by_level(plane(HE + e % 4), lv)
                v.tensor_tensor(m[:, :, 1, :], x[:, :, 1, :], by_level(plane(HQ + h), lv)[:, :, 1, :], ALU.mult)
                v.tensor_tensor(m[:, :, 0, :], x[:, :, 0, :], by_level(plane(HK + h), lv)[:, :, 0, :], ALU.mult)\
                    .then_inc(level_ready, 1)

            def mask_pairs(u):
                h, lv = divmod(u, LEVELS + 1)
                mask = level_mask[:, lv, :] if lv < LEVELS else ident[:]
                dve.wait_ge(pair_ready, u + 1)
                if u >= 2:
                    dve.wait_ge(intra_ready, u - 1)
                v.tensor_tensor(plane(HMASK + u % 2).rearrange("p (b t) -> p b t", b=TB),
                                ps[:, 6 + u % 2, :].rearrange("p (b t) -> p b t", b=TB),
                                mask.unsqueeze(1).broadcast_to([P, TB, P]), ALU.mult).then_inc(masked_ready, 1)

            make_level(0)
            for u in range(HEADS * (LEVELS + 1)):
                h, lv = divmod(u, LEVELS + 1)
                if lv != LEVELS - 1 and h * LEVELS + lv + (lv < LEVELS) < HEADS * LEVELS:
                    make_level(h * LEVELS + lv + (lv < LEVELS))
                mask_pairs(u)

            ov = A[:, HO:HO + 8, :]
            def update_state(c):
                dve.wait_ge(delta_ready, c + 1)
                if c:
                    dve.wait_ge(state_ready, HEADS * c)
                if c >= 2:
                    dve.wait_ge(inter_ready, c - 1)
                for h in range(HEADS):
                    d = ps[:, 2 + 2 * (c % 2) + h // 4, (h % 4) * P:(h % 4) * P + P]
                    new = STATES[c % 2][:, h, :]
                    if c == 0:
                        v.tensor_copy(new, d).then_inc(state_ready, 1)
                    else:
                        v.scalar_tensor_tensor(out=new, in0=STATES[(c - 1) % 2][:, h, :], scalar=dec[:, h, c:c + 1],
                                               in1=d, op0=ALU.mult, op1=ALU.add).then_inc(state_ready, 1)

            update_state(0)
            for c in range(1, NCH):
                if c < NCH - 1:
                    update_state(c)
                dve.wait_ge(inter_ready, c)
                o_c = ov[:, :, c * CH:(c + 1) * CH]
                v.tensor_tensor(o_c, o_c, ps[:, 6 + c % 2, :].rearrange("p (h t) -> p h t", h=HEADS), ALU.add)\
                    .then_inc(inter_added, 1)
            inverse("hgrn")
            dve.wait_ge(inter_added, NCH - 1)

            def gate_output(h):
                scaled("hgrn", h, plane(HO + h), col("out_norm", h), plane(HO + h))
                dve.wait_ge(scaled_ready, SCALED["hgrn"] + h + 1)
                v.tensor_tensor(plane(HO + h), plane(HO + h), plane(HGT + h), ALU.mult).then_inc(gated_ready, 1)

            behind(HEADS, gate_output, lambda h: low("o_hgrn", h, plane(HO + h)))
            residual("hgrn_o", TMPO)
            ffn_and_ple(1)

        @block.gpsimd
        def _(pool):
            g = nc.gpsimd
            own = Steps(pool, pool_step)

            def select(ap, op, fill, base, pattern, mult):
                own.wait()
                own.do(g.affine_select(out=ap, in_=ap, compare_op=op, fill=fill, base=base, pattern=pattern,
                                       channel_multiplier=mult))

            own.do(g.memset(pick_plane[:], 0.0))
            own.do(g.memset(pick_halves[:], 0.0))
            own.do(g.memset(ident[:], 0.0))
            own.do(g.memset(win_mask[:], 0.0))
            own.do(g.memset(diag_mask[:], 0.0))
            own.do(g.memset(level_mask[:], 0.0))
            own.do(g.memset(scan_keep[:], 1.0))
            own.wait()
            own.do(g.memset(scan_keep[:].rearrange("p (c t) -> p c t", c=NCH)[:, :, 0:1], 0.0))
            own.do(g.iota(iota[:], [[1, P]], base=0, channel_multiplier=0, allow_small_or_imprecise_dtypes=True))
            own.do(g.memset(pick_plane[:, 28:32], 1.0))
            own.wait()
            own.do(g.memset(pick_halves[0:64, 28:30], 1.0))
            own.wait()
            own.do(g.memset(pick_halves[64:P, 30:32], 1.0))
            own.wait()
            select(ident[:], ALU.not_equal, 1.0, 0, [[-1, P]], 1)
            select(win_mask[:], ALU.is_ge, NEG, P, [[-1, 2 * P]], 1)
            select(win_mask[:], ALU.is_gt, NEG, 0, [[1, 2 * P]], -1)
            select(diag_mask[:], ALU.is_ge, NEG, 0, [[-1, P]], 1)
            for lv in range(LEVELS):
                m = 2 ** lv
                nb = P // (2 * m)
                second = level_mask[:, lv, :].rearrange("p (b two m) -> p b two m", two=2, m=m)[:, :, 1, :]
                own.wait()
                own.do(g.memset(second, 1.0))
                select(second, ALU.is_ge, 0.0, 0, [[-2 * m, nb], [0, m]], 1)
                select(second, ALU.is_ge, 0.0, m - 1, [[2 * m, nb], [0, m]], -1)
            own.wait()
            pool.sem_inc(consts_ready, 1)

            def split(slot, n, i=0):
                raw, h, rest = ring[slot], whi[slot % SPLIT], wlo[slot % SPLIT]
                pool.wait_ge(weights_loaded[slot], i * 16 + 16 * (n // RING + 1))
                if n >= SPLIT:
                    pool.wait_ge(tiles_started, i * RING + n - SPLIT + 2)
                pool.sem_inc(split_begun, 1)
                g.tensor_scalar(h[:], raw[:], 1.0, 0.0, ALU.mult, ALU.add).then_inc(whi_ready, 1)
                pool.wait_ge(whi_ready, i * RING + n + 1)
                g.tensor_tensor(rest[:], raw[:], h[:].bitcast(F32), ALU.subtract).then_inc(split_ready, 1)

            def split_tiles(n0, n1):
                loops = (n1 - n0) // RING
                with pool.Fori(0, loops) as i:
                    for n in range(n0, n0 + RING):
                        split(n % RING, n, i)
                for n in range(n0 + loops * RING, n1):
                    split(n % RING, n)

            for n in range(RING):
                split(n, n)
            split_tiles(RING, FIRST["hgrn_o"])

            pool.wait_ge(decay_ready, 2 * HEADS)
            pool.wait_ge(kt_taken, HEADS)
            for h in range(HEADS):
                for lv in range(LEVELS):
                    e = h * LEVELS + lv
                    if e >= 4:
                        pool.wait_ge(level_ready, e - 3)
                    m = 2 ** lv
                    gv = plane(HG + h).rearrange("p (b two m) -> p b two m", two=2, m=m)
                    xv = plane(HE + e % 4).rearrange("p (b two m) -> p b two m", two=2, m=m)
                    mid = gv[:, :, 0, m - 1:m].broadcast_to([P, T // (2 * m), m])
                    g.tensor_tensor(xv[:, :, 1, :], gv[:, :, 1, :], mid, ALU.subtract)
                    g.tensor_tensor(xv[:, :, 0, :], mid, gv[:, :, 0, :], ALU.subtract).then_inc(gap_ready, 1)
            split_tiles(FIRST["hgrn_o"], NTILES)

        @block.sync
        def _(sp):
            sp.dma_start(par[:], params).then_inc(inputs_loaded, 16)
            sp.dma_start(X[:], x_in).then_inc(inputs_loaded, 16)

            def load_ada(g):
                tiles, loaded, _ = ada_group(g)
                sp.dma_start(tiles, ada_w[4 * g:4 * g + 4].rearrange("k p n -> p k n")).then_inc(loaded, 16)

            for g in range(4):
                load_ada(g)
            for s in range(RING):
                sp.dma_start(ring[s][:], stream[s]).then_inc(weights_loaded[s], 16)

            def refill(n, i=0):
                sp.wait_ge(split_ready, i * RING + n - RING + 1)
                sp.dma_start(ring[n % RING][:], stream[bass.ds(i * RING + n, 1)].rearrange("a p b n -> (a p) b n"))\
                    .then_inc(weights_loaded[n % RING], 16)

            def refills(n0, n1):
                loops = (n1 - n0) // RING
                with sp.Fori(0, loops) as i:
                    for n in range(n0, n0 + RING):
                        refill(n, i)
                for n in range(n0 + loops * RING, n1):
                    refill(n)

            refills(RING, FIRST["w_out"] + RING)
            sp.wait_ge(product_ready, PROD["w_in"] + 19)
            for g in range(4, 12):
                if g >= 7:
                    sp.wait_ge(ada_used, g - 2)
                load_ada(g)
            refills(FIRST["w_out"] + RING, NTILES)
            for j in range(KC):
                sp.wait_ge(residual_ready, RES["ple1"] + j + 1)
                sp.dma_start(out[:, j, :], X[:, j, :]).then_inc(stored, 16)
            sp.wait_ge(stored, 16 * KC)


def blocks(w):
    w = np.asarray(w)
    k, n = w.shape
    return w.reshape(k // P, P, n // P, P).transpose(0, 2, 1, 3)


def by_output(w, pad=0):
    b = blocks(w).transpose(1, 0, 2, 3)
    if pad:
        b = np.concatenate([b, np.zeros((b.shape[0], pad, P, P), b.dtype)], axis=1)
    return b.reshape(-1, P, P)


def columns(v, n=None):
    return np.asarray(v).reshape(-1, P).T


def kernel(**inputs):
    import concourse.bacc as _bacc
    from concourse.bass_utils import run_bass_kernel_spmd as _run

    a = {k: np.asarray(v) for k, v in inputs.items()}
    parts = {}
    w, b = a["w_in"], a["b_in"]
    pick = np.r_[0:512, 512:576, 512:576, 576:640, 576:640, 768:2304]
    parts["w_in"] = by_output(w[:, pick])
    parts["w_v"] = by_output(w[:, 640:768])
    parts["w_out"] = by_output(a["w_out"])
    parts["w_query"] = by_output(a["w_query"])
    keys = np.stack([a["peer_keys1"], a["peer_keys2"]], axis=1)
    parts["keys"] = keys.reshape(16, P, P).transpose(0, 2, 1)
    u = a["peer_u"].reshape(NKEY, P, KC, P).transpose(0, 2, 3, 1)
    parts["up"] = u.reshape(-1, P, P)
    parts["down"] = a["peer_v"].reshape(NKEY, P, KC, P).transpose(0, 2, 1, 3).reshape(-1, P, P)
    w = a["mla_w_dqkv_2"][0]
    turn = np.r_[544:576, 512:544]
    parts["dqkv"] = by_output(w[:, np.r_[0:576, 512:576, turn, turn]])
    w = a["mla_w_uq_2"][0].reshape(256, HEADS, 192)
    parts["uq"] = by_output(np.concatenate([w[:, :, 0:128].reshape(256, -1), w[:, :, 128:192].reshape(256, -1),
                                            w[:, :, np.r_[160:192, 128:160]].reshape(256, -1)], axis=1))
    w = a["mla_w_ukv_2"][0].reshape(256, HEADS, 256)
    parts["uk"] = by_output(w[:, :, 0:128].reshape(256, -1))
    parts["uv"] = by_output(w[:, :, 128:256].reshape(256, -1))
    parts["w_o"] = by_output(a["mla_w_o_2"][0])
    for i in range(2):
        w = a["ffn_w_in_2"][i].reshape(D, 2, FF, P).transpose(0, 2, 1, 3).reshape(D, -1)
        parts[f"ffn_in{i}"] = by_output(w)
        parts[f"ffn_down{i}"] = by_output(a["ffn_w_down_2"][i], pad=24 - FF)
        parts[f"ple_gate{i}"] = by_output(a["ple_w_gate_2"][i])
        parts[f"ple_proj{i}"] = by_output(a["ple_w_proj_2"][i])
    w = a["hgrn_w_in_2"][0]
    parts["hgrn_in"] = by_output(w[:, 0:2048])
    parts["hgrn_v"] = by_output(w[:, 2048:3072])
    parts["hgrn_gate"] = by_output(w[:, 3072:4096])
    parts["hgrn_o"] = by_output(a["hgrn_w_o_2"][0])
    flat = np.concatenate([parts[name] for name, n in PARTS if n])
    stream = np.ascontiguousarray(flat.reshape(NTILES, BLOCKS, P, P).transpose(0, 2, 1, 3))

    freq = (10000.0 ** (-np.arange(0, 64, 2, dtype=np.float32) / np.float32(64))).astype(np.float32)
    sign = np.repeat([-1.0, 1.0], 32)
    cols = dict(
        c=columns(a["c"]), b_ada=columns(a["b_ada"]), norm1_g=columns(a["norm1_g"]), b_in=columns(b[pick]),
        b_v=np.broadcast_to(b[640:768], (P, P)), sinks=np.broadcast_to(a["attn_sinks"][[0, 2, 1, 3, 4, 6, 5, 7]], (P, 8)),
        conv_w=columns(a["conv_w"]), attn_out_g=columns(a["attn_out_g"]), conv_out_g=columns(a["conv_out_g"]),
        b_out=columns(a["b_out"]), norm2_g=columns(a["norm2_g"]), final_g=columns(a["final_g"]),
        q_norm=columns(a["mla_q_norm_2"]), kv_norm=columns(a["mla_kv_norm_2"]), lb=columns(a["hgrn_lb_logits_2"]),
        out_norm=columns(a["hgrn_out_norm_2"]), ln_mix_g=columns(a["ln_mix_g_2"]), ln_mix_b=columns(a["ln_mix_b_2"]),
        ln_ffn_g=columns(a["ln_ffn_g_2"]), ln_ffn_b=columns(a["ln_ffn_b_2"]),
        inv_freq=np.tile(freq, 4)[:, None], sin_sign=np.tile(sign, 2)[:, None])
    arrays = {
        "stream": stream,
        "ada_w": np.ascontiguousarray(a["w_ada"].reshape(KC, P, 6, D).transpose(2, 0, 1, 3)).reshape(48, P, D),
        "x_in": np.ascontiguousarray(a["x"][0].T.reshape(KC, P, T).transpose(1, 0, 2)),
        "params": np.ascontiguousarray(np.concatenate([cols[name] for name, _ in COLS], axis=1).astype(np.float32)),
        "positions": np.ascontiguousarray(np.broadcast_to(a["positions_2"].reshape(1, T), (P, T))),
        "ple_in": np.ascontiguousarray(a["p_2"][:, 0].transpose(0, 2, 1).reshape(2, 2, P, T).transpose(0, 2, 1, 3)),
    }
    nc = _bacc.Bacc("TRN2", target_bir_lowering=False, num_devices=1)
    args = [nc.dram_tensor(n, list(v.shape), mybir.dt.from_np(v.dtype), kind="ExternalInput").ap()
            for n, v in arrays.items()]
    out = nc.dram_tensor("out", [P, KC, T], F32, kind="ExternalOutput").ap()
    gate_map = nc.dram_tensor("gate_map", [NKEY, P, T], F32, kind="Internal").ap()
    gelu_map = nc.dram_tensor("gelu_map", [NKEY, P, T], F32, kind="Internal").ap()
    build(nc, *args, out, gate_map, gelu_map)
    r = _run(nc, [arrays], core_ids=[0])
    got = np.asarray(r.results[0]["out"])
    return got.transpose(2, 1, 0).reshape(1, T, D)
```
